# Optimizing a Trainium2 kernel written in Bass

```python
import math
import jax, jax.numpy as jnp
from jax import lax
import numpy as np

D_MODEL = 1024
BATCH = 1
SEQ = 256
DEPTH = 4

N_MIXERS = 3
HEAD_DIM = 64
PLE_DIM = 256
D_FF = 4 * D_MODEL
NORM_EPS = 1e-6
NEG_INF = -1e30
Q_BLOCK = 128

REL_BUCKETS = 32
REL_MAX_DIST = 128
REL_HEADS = D_MODEL // HEAD_DIM

DA_HEADS = D_MODEL // (2 * HEAD_DIM)
DA_IN = 3 * D_MODEL

NSA_HEADS = D_MODEL // HEAD_DIM
NSA_KV_GROUPS = 4
NSA_GROUP_SIZE = NSA_HEADS // NSA_KV_GROUPS
NSA_CMP_LEN = 32
NSA_CMP_STRIDE = 16
NSA_CMP_HIDDEN = 256
NSA_SEL_LEN = 64
NSA_TOP_N = 16
NSA_WINDOW = 512
NSA_Q_CHUNK = 64
NSA_FORCE_SCORE = 1e4
NSA_KV_DIM = NSA_KV_GROUPS * HEAD_DIM
NSA_IN = NSA_HEADS * HEAD_DIM + 6 * NSA_KV_DIM + 3 * NSA_HEADS

FOX_HEADS = D_MODEL // HEAD_DIM
FOX_IN = 3 * D_MODEL + FOX_HEADS

N_DA = (DEPTH + 2) // 3
N_NSA = (DEPTH + 1) // 3
N_FOX = DEPTH // 3


def rmsnorm(x, g):
    xf = x.astype(jnp.float32)
    y = xf * lax.rsqrt(jnp.mean(xf * xf, axis=-1, keepdims=True) + NORM_EPS)
    return (y * g.astype(jnp.float32)).astype(x.dtype)

def t5_bucket(dist):
    n = jnp.maximum(dist, 0)
    max_exact = REL_BUCKETS // 2
    nf = jnp.maximum(n, 1).astype(jnp.float32)
    large = max_exact + (jnp.log(nf / max_exact) / math.log(REL_MAX_DIST / max_exact)
                         * (REL_BUCKETS - max_exact)).astype(jnp.int32)
    large = jnp.minimum(large, REL_BUCKETS - 1)
    return jnp.where(n < max_exact, n, large)

def masked_softmax(s, mask):
    s = jnp.where(mask, s.astype(jnp.float32), NEG_INF)
    return jnp.where(mask, jax.nn.softmax(s, axis=-1), 0.0)

def query_blocks(a, blk):
    B, S = a.shape[:2]
    return jnp.moveaxis(a.reshape(B, S // blk, blk, *a.shape[2:]), 1, 0)

def merge_blocks(o):
    o = jnp.moveaxis(o, 0, 1)
    return o.reshape(o.shape[0], -1, *o.shape[3:])

def diff_attention(h, w_in, lam, subln_g, w_out, rel_bias, lam_init):
    B, S, _ = h.shape
    q, k, v = jnp.split(h @ w_in, 3, axis=-1)
    q = q.reshape(B, S, DA_HEADS, 2, HEAD_DIM)
    k = k.reshape(B, S, DA_HEADS, 2, HEAD_DIM)
    v = v.reshape(B, S, DA_HEADS, 2 * HEAD_DIM)
    lf = lam.astype(jnp.float32)
    lam_full = jnp.exp(jnp.sum(lf[0] * lf[1])) - jnp.exp(jnp.sum(lf[2] * lf[3])) + lam_init
    scale = HEAD_DIM ** -0.5
    key_pos = jnp.arange(S)

    def block(args):
        qb, q0 = args
        t = q0 + jnp.arange(Q_BLOCK)
        dist = t[:, None] - key_pos[None, :]
        mask = dist >= 0
        bias = rel_bias[t5_bucket(dist)].astype(jnp.float32)
        bias = jnp.moveaxis(bias, -1, 0).reshape(DA_HEADS, 2, Q_BLOCK, S)
        s = jnp.einsum('bqhcd,bkhcd->bhcqk', qb, k).astype(jnp.float32) * scale + bias[None]
        pr = masked_softmax(s, mask)
        a = pr[:, :, 0] - lam_full * pr[:, :, 1]
        return jnp.einsum('bhqk,bkhe->bqhe', a.astype(v.dtype), v)

    starts = jnp.arange(S // Q_BLOCK) * Q_BLOCK
    o = merge_blocks(lax.map(block, (query_blocks(q, Q_BLOCK), starts)))
    o = rmsnorm(o, subln_g) * (1.0 - lam_init)
    return o.reshape(B, S, D_MODEL) @ w_out

def nsa_attention(h, w_in, cmp_pe, cmp_w1, cmp_w2, w_out, rel_bias):
    B, S, _ = h.shape
    G, R, hd, Qc = NSA_KV_GROUPS, NSA_GROUP_SIZE, HEAD_DIM, NSA_Q_CHUNK
    proj = h @ w_in
    nq = NSA_HEADS * hd
    q = proj[..., :nq].reshape(B, S, G, R, hd)
    kv = proj[..., nq:nq + 6 * NSA_KV_DIM].reshape(B, S, 6, G, hd)
    k_cmp, v_cmp, k_sel, v_sel, k_win, v_win = [kv[:, :, i] for i in range(6)]
    gates = jax.nn.sigmoid(proj[..., nq + 6 * NSA_KV_DIM:].reshape(B, S, G, R, 3))
    scale = hd ** -0.5

    n_cmp = (S - NSA_CMP_LEN) // NSA_CMP_STRIDE + 1
    tok = jnp.arange(n_cmp)[:, None] * NSA_CMP_STRIDE + jnp.arange(NSA_CMP_LEN)[None, :]

    def compress(a, pe, w1, w2):
        blk = a[:, tok] + pe[None, None, :, None, :]
        blk = jnp.moveaxis(blk, 3, 2).reshape(B, n_cmp, G, NSA_CMP_LEN * hd)
        return jax.nn.gelu(blk @ w1) @ w2

    kc = compress(k_cmp, cmp_pe[0], cmp_w1[0], cmp_w2[0])
    vc = compress(v_cmp, cmp_pe[1], cmp_w1[1], cmp_w2[1])
    cmp_start = jnp.arange(n_cmp) * NSA_CMP_STRIDE
    cmp_end = cmp_start + NSA_CMP_LEN - 1

    n_sel_blk = S // NSA_SEL_LEN
    n_top = min(NSA_TOP_N, n_sel_blk)
    sel_start = jnp.arange(n_sel_blk) * NSA_SEL_LEN
    overlap = ((cmp_start[:, None] < sel_start[None, :] + NSA_SEL_LEN)
               & (cmp_end[:, None] >= sel_start[None, :])).astype(jnp.float32)
    ks_blk = jnp.moveaxis(k_sel.reshape(B, n_sel_blk, NSA_SEL_LEN, G, hd), 3, 1)
    vs_blk = jnp.moveaxis(v_sel.reshape(B, n_sel_blk, NSA_SEL_LEN, G, hd), 3, 1)

    pad = ((0, 0), (NSA_WINDOW, 0), (0, 0), (0, 0))
    kw_pad = jnp.pad(k_win, pad)
    vw_pad = jnp.pad(v_win, pad)

    rel = rel_bias.reshape(REL_BUCKETS, G, R)
    b_idx = jnp.arange(B)[:, None, None, None]
    g_idx = jnp.arange(G)[None, :, None, None]
    j_blk = jnp.arange(n_sel_blk)
    K_sel = n_top * NSA_SEL_LEN

    def chunk(args):
        qc, gc, q0 = args
        t = q0 + jnp.arange(Qc)
        d_c = t[:, None] - cmp_end[None, :]
        m_c = d_c >= 0
        b_c = jnp.moveaxis(rel[t5_bucket(d_c)], (2, 3), (0, 1)).astype(jnp.float32)
        s_c = jnp.einsum('bqgrd,bngd->bgrqn', qc, kc).astype(jnp.float32) * scale + b_c
        p_c = masked_softmax(s_c, m_c)
        o_c = jnp.einsum('bgrqn,bngd->bqgrd', p_c.astype(vc.dtype), vc)
        imp = jnp.einsum('bgrqn,nj->bgqj', p_c, overlap)
        cur = t // NSA_SEL_LEN
        forced = (j_blk[None, :] == 0) | (j_blk[None, :] == cur[:, None]) | (j_blk[None, :] == cur[:, None] - 1)
        valid = sel_start[None, :] <= t[:, None]
        imp = jnp.where(valid, jnp.where(forced, NSA_FORCE_SCORE, imp), -1.0)
        _, sel = lax.top_k(imp, n_top)
        k_g = ks_blk[b_idx, g_idx, sel].reshape(B, G, Qc, K_sel, hd)
        v_g = vs_blk[b_idx, g_idx, sel].reshape(B, G, Qc, K_sel, hd)
        pos = (sel[..., None] * NSA_SEL_LEN + jnp.arange(NSA_SEL_LEN)).reshape(B, G, Qc, K_sel)
        d_s = t[None, None, :, None] - pos
        m_s = (d_s >= 0)[:, :, None]
        b_s = jnp.moveaxis(rel[t5_bucket(d_s), g_idx], -1, 2).astype(jnp.float32)
        s_s = jnp.einsum('bqgrd,bgqkd->bgrqk', qc, k_g).astype(jnp.float32) * scale + b_s
        p_s = masked_softmax(s_s, m_s)
        o_s = jnp.einsum('bgrqk,bgqkd->bqgrd', p_s.astype(v_g.dtype), v_g)
        kw = lax.dynamic_slice_in_dim(kw_pad, q0, NSA_WINDOW + Qc, axis=1)
        vw = lax.dynamic_slice_in_dim(vw_pad, q0, NSA_WINDOW + Qc, axis=1)
        w_pos = q0 - NSA_WINDOW + jnp.arange(NSA_WINDOW + Qc)
        d_w = t[:, None] - w_pos[None, :]
        m_w = (d_w >= 0) & (d_w < NSA_WINDOW) & (w_pos[None, :] >= 0)
        b_w = jnp.moveaxis(rel[t5_bucket(d_w)], (2, 3), (0, 1)).astype(jnp.float32)
        s_w = jnp.einsum('bqgrd,bkgd->bgrqk', qc, kw).astype(jnp.float32) * scale + b_w
        p_w = masked_softmax(s_w, m_w)
        o_w = jnp.einsum('bgrqk,bkgd->bqgrd', p_w.astype(vw.dtype), vw)
        return gc[..., 0:1] * o_c + gc[..., 1:2] * o_s + gc[..., 2:3] * o_w

    starts = jnp.arange(S // Qc) * Qc
    o = merge_blocks(lax.map(chunk, (query_blocks(q, Qc), query_blocks(gates, Qc), starts)))
    return o.reshape(B, S, D_MODEL) @ w_out

def forgetting_attention(h, w_in, b_f, w_out):
    B, S, _ = h.shape
    proj = h @ w_in
    q = proj[..., :D_MODEL].reshape(B, S, FOX_HEADS, HEAD_DIM)
    k = proj[..., D_MODEL:2 * D_MODEL].reshape(B, S, FOX_HEADS, HEAD_DIM)
    v = proj[..., 2 * D_MODEL:3 * D_MODEL].reshape(B, S, FOX_HEADS, HEAD_DIM)
    log_f = jax.nn.log_sigmoid((proj[..., 3 * D_MODEL:] + b_f).astype(jnp.float32))
    c = jnp.cumsum(log_f, axis=1)
    c_k = jnp.moveaxis(c, 1, 2)
    scale = HEAD_DIM ** -0.5
    key_pos = jnp.arange(S)

    def block(args):
        qb, cq, q0 = args
        t = q0 + jnp.arange(Q_BLOCK)
        mask = t[:, None] >= key_pos[None, :]
        decay = jnp.moveaxis(cq, 1, 2)[..., None] - c_k[:, :, None, :]
        s = jnp.einsum('bqhd,bkhd->bhqk', qb, k).astype(jnp.float32) * scale + decay
        pr = masked_softmax(s, mask)
        return jnp.einsum('bhqk,bkhd->bqhd', pr.astype(v.dtype), v)

    starts = jnp.arange(S // Q_BLOCK) * Q_BLOCK
    o = merge_blocks(lax.map(block, (query_blocks(q, Q_BLOCK), query_blocks(c, Q_BLOCK), starts)))
    return o.reshape(B, S, D_MODEL) @ w_out

def sqrelu_mlp(h, w1, w2):
    return jnp.square(jax.nn.relu(h @ w1)) @ w2

def first_inputs(seed: int = 0) -> dict:
    key = jax.random.key(seed)
    ks = list(jax.random.split(key, 24))

    def nrm(i, shape, scale):
        return jax.random.normal(ks[i], shape, jnp.float32) * scale

    D = D_MODEL
    return {
        'x': nrm(0, (BATCH, SEQ, D), 1.0),
        'p': nrm(1, (DEPTH, BATCH, SEQ, PLE_DIM), 1.0),
        'rel_bias': nrm(2, (REL_BUCKETS, REL_HEADS), 0.5),
        'norm_g': 1.0 + nrm(3, (DEPTH, 4, D), 0.02),
        'mlp_w1': nrm(4, (DEPTH, D, D_FF), D ** -0.5),
        'mlp_w2': nrm(5, (DEPTH, D_FF, D), D_FF ** -0.5),
        'ple_w': nrm(6, (DEPTH, PLE_DIM, D), PLE_DIM ** -0.5),
        'ple_gate_w': nrm(7, (DEPTH, D, D), D ** -0.5),
        'da_w_in': nrm(8, (N_DA, D, DA_IN), D ** -0.5),
        'da_lambda': nrm(9, (N_DA, 4, HEAD_DIM), 0.1),
        'da_subln': 1.0 + nrm(10, (N_DA, 2 * HEAD_DIM), 0.02),
        'da_w_out': nrm(11, (N_DA, D, D), D ** -0.5),
        'nsa_w_in': nrm(12, (N_NSA, D, NSA_IN), D ** -0.5),
        'nsa_cmp_pe': nrm(13, (N_NSA, 2, NSA_CMP_LEN, HEAD_DIM), 0.1),
        'nsa_cmp_w1': nrm(14, (N_NSA, 2, NSA_CMP_LEN * HEAD_DIM, NSA_CMP_HIDDEN), (NSA_CMP_LEN * HEAD_DIM) ** -0.5),
        'nsa_cmp_w2': nrm(15, (N_NSA, 2, NSA_CMP_HIDDEN, HEAD_DIM), NSA_CMP_HIDDEN ** -0.5),
        'nsa_w_out': nrm(16, (N_NSA, D, D), D ** -0.5),
        'fox_w_in': nrm(17, (N_FOX, D, FOX_IN), D ** -0.5),
        'fox_b_f': 3.0 + nrm(18, (N_FOX, FOX_HEADS), 1.0),
        'fox_w_out': nrm(19, (N_FOX, D, D), D ** -0.5),
    }

def first_block(x, p, rel_bias, norm_g, mlp_w1, mlp_w2, ple_w, ple_gate_w,
              da_w_in, da_lambda, da_subln, da_w_out,
              nsa_w_in, nsa_cmp_pe, nsa_cmp_w1, nsa_cmp_w2, nsa_w_out,
              fox_w_in, fox_b_f, fox_w_out):
    ia, ib, ic = 0, 0, 0
    for i in range(DEPTH):
        g = norm_g[i]
        h = rmsnorm(x, g[0])
        kind = i % N_MIXERS
        if kind == 0:
            lam_init = 0.8 - 0.6 * math.exp(-0.3 * i)
            y = diff_attention(h, da_w_in[ia], da_lambda[ia], da_subln[ia], da_w_out[ia], rel_bias, lam_init)
            ia += 1
        elif kind == 1:
            y = nsa_attention(h, nsa_w_in[ib], nsa_cmp_pe[ib], nsa_cmp_w1[ib], nsa_cmp_w2[ib], nsa_w_out[ib], rel_bias)
            ib += 1
        else:
            y = forgetting_attention(h, fox_w_in[ic], fox_b_f[ic], fox_w_out[ic])
            ic += 1
        x = x + rmsnorm(y, g[1])
        y = sqrelu_mlp(rmsnorm(x, g[2]), mlp_w1[i], mlp_w2[i])
        x = x + rmsnorm(y, g[3])
        x = x + jax.nn.sigmoid(x @ ple_gate_w[i]) * (p[i] @ ple_w[i])
    return x


DEPTH_2 = 2

D_FF_2 = 2816
SSD_EXPAND = 2
SSD_D_INNER = SSD_EXPAND * D_MODEL
SSD_HEAD_DIM = 64
SSD_HEADS = SSD_D_INNER // SSD_HEAD_DIM
SSD_GROUPS = 4
SSD_HPG = SSD_HEADS // SSD_GROUPS
SSD_STATE = 128
SSD_CONV = 4
SSD_CHUNK = 128
SSD_CONV_DIM = SSD_D_INNER + 2 * SSD_GROUPS * SSD_STATE
MLA_HEADS = 8
MLA_Q_LORA = 512
MLA_KV_LORA = 256
MLA_NOPE = 128
MLA_ROPE = 64
MLA_V = 128
MLA_QK = MLA_NOPE + MLA_ROPE
ATTN_BLOCK = 128
ROPE_THETA = 10000.0
EPS = 1e-6
IN_SPLIT_SIZES = (SSD_D_INNER, SSD_CONV_DIM, SSD_HEADS, MLA_Q_LORA, MLA_KV_LORA, MLA_ROPE, 2 * D_MODEL)
D_IN_PROJ = SSD_D_INNER + SSD_CONV_DIM + SSD_HEADS + MLA_Q_LORA + MLA_KV_LORA + MLA_ROPE + 2 * D_MODEL


def rms_norm(x, g):
    xf = x.astype(jnp.float32)
    y = xf * lax.rsqrt(jnp.mean(xf * xf, axis=-1, keepdims=True) + EPS)
    return (y * g.astype(jnp.float32)).astype(x.dtype)

def swiglu(x, w13, w2):
    gu = x @ w13
    gate, up = gu[..., :D_FF_2], gu[..., D_FF_2:]
    return (jax.nn.silu(gate) * up) @ w2

def split_cols(t, sizes):
    out, start = [], 0
    for n in sizes:
        out.append(t[..., start:start + n])
        start += n
    return out

def rope_tables(positions):
    inv = 1.0 / (ROPE_THETA ** (jnp.arange(0, MLA_ROPE, 2, dtype=jnp.float32) / MLA_ROPE))
    ang = positions.astype(jnp.float32)[..., None] * inv
    return jnp.cos(ang), jnp.sin(ang)

def apply_rope(t, cos, sin):
    half = MLA_ROPE // 2
    tf = t.astype(jnp.float32)
    t1, t2 = tf[..., :half], tf[..., half:]
    c, s = cos[:, :, None, :], sin[:, :, None, :]
    return jnp.concatenate([t1 * c - t2 * s, t2 * c + t1 * s], axis=-1).astype(t.dtype)

def causal_depthwise_conv(t, w, b):
    y = lax.conv_general_dilated(
        t, w[:, None, :].astype(t.dtype), window_strides=(1,), padding=[(SSD_CONV - 1, 0)],
        dimension_numbers=('NWC', 'WIO', 'NWC'), feature_group_count=t.shape[-1])
    return y + b.astype(t.dtype)

def ssd_chunked_scan(xh, dt, a, bmat, cmat):
    bsz, s = xh.shape[0], xh.shape[1]
    nc = s // SSD_CHUNK

    def chunks(t):
        t = t.reshape((bsz, nc, SSD_CHUNK) + t.shape[2:])
        return jnp.moveaxis(t, 1, 0)

    x_c = chunks(xh.astype(jnp.float32).reshape(bsz, s, SSD_GROUPS, SSD_HPG, SSD_HEAD_DIM))
    dt_c = chunks(dt.reshape(bsz, s, SSD_GROUPS, SSD_HPG))
    b_c = chunks(bmat.astype(jnp.float32))
    c_c = chunks(cmat.astype(jnp.float32))
    a_g = a.reshape(SSD_GROUPS, SSD_HPG)
    causal = jnp.tril(jnp.ones((SSD_CHUNK, SSD_CHUNK), dtype=bool))[None, :, :, None, None]

    def step(state, inp):
        xc, dtc, bc, cc = inp
        acum = jnp.cumsum(dtc * a_g, axis=1)
        seg = acum[:, :, None] - acum[:, None, :]
        decay = jnp.exp(jnp.where(causal, seg, -jnp.inf))
        cb = jnp.einsum('btgn,bsgn->btsg', cc, bc)
        xdt = xc * dtc[..., None]
        y_diag = jnp.einsum('btsg,btsgh,bsghp->btghp', cb, decay, xdt)
        y_off = jnp.einsum('btgn,bghpn->btghp', cc, state) * jnp.exp(acum)[..., None]
        last = acum[:, -1]
        w_state = jnp.exp(last[:, None] - acum)
        new_state = (state * jnp.exp(last)[..., None, None]
                     + jnp.einsum('bsgn,bsgh,bsghp->bghpn', bc, w_state, xdt))
        return new_state, y_diag + y_off

    state0 = jnp.zeros((bsz, SSD_GROUPS, SSD_HPG, SSD_HEAD_DIM, SSD_STATE), jnp.float32)
    _, y = lax.scan(step, state0, (x_c, dt_c, b_c, c_c))
    return jnp.moveaxis(y, 0, 1).reshape(bsz, s, SSD_HEADS, SSD_HEAD_DIM)

def ssd_branch(z, xbc, dt_raw, conv_w, conv_b, dt_bias, a_log, d_skip, norm_g, w_out):
    bsz, s, _ = z.shape
    xbc = jax.nn.silu(causal_depthwise_conv(xbc, conv_w, conv_b))
    xs, bm, cm = split_cols(xbc, (SSD_D_INNER, SSD_GROUPS * SSD_STATE, SSD_GROUPS * SSD_STATE))
    xh = xs.reshape(bsz, s, SSD_HEADS, SSD_HEAD_DIM)
    bm = bm.reshape(bsz, s, SSD_GROUPS, SSD_STATE)
    cm = cm.reshape(bsz, s, SSD_GROUPS, SSD_STATE)
    dt = jax.nn.softplus(dt_raw.astype(jnp.float32) + dt_bias.astype(jnp.float32))
    a = -jnp.exp(a_log.astype(jnp.float32))
    y = ssd_chunked_scan(xh, dt, a, bm, cm) + xh.astype(jnp.float32) * d_skip.astype(jnp.float32)[:, None]
    y = y.reshape(bsz, s, SSD_D_INNER).astype(z.dtype)
    y = rms_norm(y * jax.nn.silu(z), norm_g)
    return y @ w_out

def causal_block_attention(q, k, v):
    bsz, s, h, dq = q.shape
    nb = s // ATTN_BLOCK
    scale = dq ** -0.5
    qb = jnp.moveaxis(q.reshape(bsz, nb, ATTN_BLOCK, h, dq), 1, 0)
    kpos = jnp.arange(s)

    def one_block(args):
        i, qi = args
        sc = jnp.einsum('bqhd,bkhd->bhqk', qi, k, preferred_element_type=jnp.float32) * scale
        qpos = i * ATTN_BLOCK + jnp.arange(ATTN_BLOCK)
        sc = jnp.where(kpos[None, :] <= qpos[:, None], sc, -jnp.inf)
        p = jax.nn.softmax(sc, axis=-1)
        return jnp.einsum('bhqk,bkhd->bqhd', p.astype(v.dtype), v)

    o = lax.map(one_block, (jnp.arange(nb), qb))
    return jnp.moveaxis(o, 0, 1).reshape(bsz, s, h, v.shape[-1])

def mla_branch(cq, ckv, kr, cos, sin, q_lora_g, w_uq, kv_lora_g, w_ukv, q_norm_g, k_norm_g, w_out):
    bsz, s, _ = cq.shape
    q = (rms_norm(cq, q_lora_g) @ w_uq).reshape(bsz, s, MLA_HEADS, MLA_QK)
    kv = (rms_norm(ckv, kv_lora_g) @ w_ukv).reshape(bsz, s, MLA_HEADS, MLA_NOPE + MLA_V)
    k_nope, v = kv[..., :MLA_NOPE], kv[..., MLA_NOPE:]
    k_pe = jnp.broadcast_to(kr[:, :, None, :], (bsz, s, MLA_HEADS, MLA_ROPE))
    k = jnp.concatenate([k_nope, k_pe], axis=-1)
    q = rms_norm(q, q_norm_g)
    k = rms_norm(k, k_norm_g)
    q = jnp.concatenate([q[..., :MLA_NOPE], apply_rope(q[..., MLA_NOPE:], cos, sin)], axis=-1)
    k = jnp.concatenate([k[..., :MLA_NOPE], apply_rope(k[..., MLA_NOPE:], cos, sin)], axis=-1)
    o = causal_block_attention(q, k, v)
    return o.reshape(bsz, s, MLA_HEADS * MLA_V) @ w_out

def second_inputs(seed: int = 0) -> dict:
    key = jax.random.key(seed)
    ks = jax.random.split(key, 32)
    f32 = jnp.float32

    def nrm(k, shape, fan_in):
        return jax.random.normal(k, shape, f32) * (fan_in ** -0.5)

    def gain(k, n):
        return 1.0 + 0.02 * jax.random.normal(k, (DEPTH_2, n), f32)

    dt0 = jnp.exp(jax.random.uniform(ks[10], (DEPTH_2, SSD_HEADS), f32) * (np.log(0.1) - np.log(0.001)) + np.log(0.001))
    dt_bias = dt0 + jnp.log(-jnp.expm1(-dt0))
    a_log = jnp.log(jax.random.uniform(ks[11], (DEPTH_2, SSD_HEADS), f32, 1.0, 16.0))
    return {
        "x": jax.random.normal(ks[0], (BATCH, SEQ, D_MODEL), f32),
        "positions": jnp.broadcast_to(jnp.arange(SEQ, dtype=jnp.int32)[None, :], (BATCH, SEQ)),
        "ln_ffn1": gain(ks[1], D_MODEL),
        "ffn1_w13": nrm(ks[2], (DEPTH_2, D_MODEL, 2 * D_FF_2), D_MODEL),
        "ffn1_w2": nrm(ks[3], (DEPTH_2, D_FF_2, D_MODEL), D_FF_2),
        "ln_mix": gain(ks[4], D_MODEL),
        "w_in": nrm(ks[5], (DEPTH_2, D_MODEL, D_IN_PROJ), D_MODEL),
        "conv_w": nrm(ks[6], (DEPTH_2, SSD_CONV, SSD_CONV_DIM), SSD_CONV),
        "conv_b": 0.02 * jax.random.normal(ks[7], (DEPTH_2, SSD_CONV_DIM), f32),
        "dt_bias": dt_bias,
        "a_log": a_log,
        "d_skip": 1.0 + 0.1 * jax.random.normal(ks[12], (DEPTH_2, SSD_HEADS), f32),
        "ssd_norm": gain(ks[13], SSD_D_INNER),
        "w_ssd_out": nrm(ks[14], (DEPTH_2, SSD_D_INNER, D_MODEL), SSD_D_INNER),
        "q_lora_norm": gain(ks[15], MLA_Q_LORA),
        "w_uq": nrm(ks[16], (DEPTH_2, MLA_Q_LORA, MLA_HEADS * MLA_QK), MLA_Q_LORA),
        "kv_lora_norm": gain(ks[17], MLA_KV_LORA),
        "w_ukv": nrm(ks[18], (DEPTH_2, MLA_KV_LORA, MLA_HEADS * (MLA_NOPE + MLA_V)), MLA_KV_LORA),
        "q_norm": gain(ks[19], MLA_QK),
        "k_norm": gain(ks[20], MLA_QK),
        "w_mla_out": nrm(ks[21], (DEPTH_2, MLA_HEADS * MLA_V, D_MODEL), MLA_HEADS * MLA_V),
        "w_o": nrm(ks[22], (DEPTH_2, D_MODEL, D_MODEL), D_MODEL),
        "ln_ffn2": gain(ks[23], D_MODEL),
        "ffn2_w13": nrm(ks[24], (DEPTH_2, D_MODEL, 2 * D_FF_2), D_MODEL),
        "ffn2_w2": nrm(ks[25], (DEPTH_2, D_FF_2, D_MODEL), D_FF_2),
    }

def second_block(x, positions, ln_ffn1, ffn1_w13, ffn1_w2, ln_mix, w_in, conv_w, conv_b, dt_bias,
              a_log, d_skip, ssd_norm, w_ssd_out, q_lora_norm, w_uq, kv_lora_norm, w_ukv,
              q_norm, k_norm, w_mla_out, w_o, ln_ffn2, ffn2_w13, ffn2_w2):
    cos, sin = rope_tables(positions)
    h = x
    for l in range(DEPTH_2):
        h = h + 0.5 * swiglu(rms_norm(h, ln_ffn1[l]), ffn1_w13[l], ffn1_w2[l])
        u = rms_norm(h, ln_mix[l])
        z, xbc, dt_raw, cq, ckv, kr, gates = split_cols(u @ w_in[l], IN_SPLIT_SIZES)
        y_ssd = ssd_branch(z, xbc, dt_raw, conv_w[l], conv_b[l], dt_bias[l], a_log[l], d_skip[l],
                           ssd_norm[l], w_ssd_out[l])
        y_mla = mla_branch(cq, ckv, kr, cos, sin, q_lora_norm[l], w_uq[l], kv_lora_norm[l], w_ukv[l],
                           q_norm[l], k_norm[l], w_mla_out[l])
        g = jax.nn.sigmoid(gates.astype(jnp.float32)).astype(h.dtype)
        merged = g[..., :D_MODEL] * y_ssd + g[..., D_MODEL:] * y_mla
        h = h + merged @ w_o[l]
        h = h + 0.5 * swiglu(rms_norm(h, ln_ffn2[l]), ffn2_w13[l], ffn2_w2[l])
    return h


def setup_inputs(seed=0):
    out = dict(first_inputs(seed))
    for name, value in second_inputs(seed + 1).items():
        if name != "x":
            out[name + "_2"] = value
    return out


def reference(
    x, p, rel_bias, norm_g, mlp_w1, mlp_w2, ple_w, ple_gate_w, da_w_in, da_lambda, da_subln,
    da_w_out, nsa_w_in, nsa_cmp_pe, nsa_cmp_w1, nsa_cmp_w2, nsa_w_out, fox_w_in, fox_b_f,
    fox_w_out, positions_2, ln_ffn1_2, ffn1_w13_2, ffn1_w2_2, ln_mix_2, w_in_2, conv_w_2,
    conv_b_2, dt_bias_2, a_log_2, d_skip_2, ssd_norm_2, w_ssd_out_2, q_lora_norm_2, w_uq_2,
    kv_lora_norm_2, w_ukv_2, q_norm_2, k_norm_2, w_mla_out_2, w_o_2, ln_ffn2_2, ffn2_w13_2,
    ffn2_w2_2,
):
    x = first_block(
        x, p, rel_bias, norm_g, mlp_w1, mlp_w2, ple_w, ple_gate_w, da_w_in, da_lambda, da_subln,
        da_w_out, nsa_w_in, nsa_cmp_pe, nsa_cmp_w1, nsa_cmp_w2, nsa_w_out, fox_w_in, fox_b_f,
        fox_w_out,
    )
    return second_block(
        x, positions_2, ln_ffn1_2, ffn1_w13_2, ffn1_w2_2, ln_mix_2, w_in_2, conv_w_2, conv_b_2,
        dt_bias_2, a_log_2, d_skip_2, ssd_norm_2, w_ssd_out_2, q_lora_norm_2, w_uq_2,
        kv_lora_norm_2, w_ukv_2, q_norm_2, k_norm_2, w_mla_out_2, w_o_2, ln_ffn2_2, ffn2_w13_2,
        ffn2_w2_2,
    )


_drawn_inputs = setup_inputs


def setup_inputs(seed=0):
    import zlib

    import numpy as np

    out = dict(_drawn_inputs(seed))
    spreads = {}
    factors = {'da_subln': 2.905,
     'ln_ffn1_2': 8.0,
     'ln_mix_2': 7.162,
     'conv_b_2': 30.361,
     'd_skip_2': 28.112,
     'ssd_norm_2': 39.371,
     'q_lora_norm_2': 8.0,
     'kv_lora_norm_2': 8.0,
     'q_norm_2': 8.0,
     'k_norm_2': 8.0,
     'ln_ffn2_2': 8.0}
    for name, (base, spread) in spreads.items():
        noise = np.random.default_rng([zlib.crc32(name.encode()), seed]).standard_normal(out[name].shape)
        drawn = base * np.exp(spread * noise) if base else spread * noise
        out[name] = __import__('jax').numpy.asarray(drawn.astype(out[name].dtype))
    for name, factor in factors.items():
        out[name] = (out[name] * factor).astype(out[name].dtype)
    return out
```

```python
import math
from contextlib import ExitStack, contextmanager

import numpy as np

import concourse.bass as bass
from concourse import mybir
from concourse.alu_op_type import AluOpType as ALU

F32 = mybir.dt.float32
F32R = mybir.dt.float32r
I32 = mybir.dt.int32
ACT = mybir.ActivationFunctionType
AX = mybir.AxisListType

P = 128
D = 1024
S = 256
NT = S // P
DC = D // P
DEPTH = 4
NEG = -1.0e30
EPS = 1e-6
BLK = 4096
H64 = 16
NB = 32
NCMP = (S - 32) // 16 + 1
F_MLP = 4096
F_GLU = 2816
DEPTH2 = 2
W_IN2 = 8032
O_Z, O_XBC, O_DT, O_CQ, O_CKV, O_KR, O_G = 0, 2048, 5120, 5152, 5664, 5920, 5984
LAM_INIT = [0.8 - 0.6 * math.exp(-0.3 * i) for i in range(DEPTH)]


class Track:

    def __init__(self, eng):
        self.eng, self.n, self.per, self.i, self.last = eng, {}, {}, None, None
        self.m = 0

    def adds(self, s, k=1):
        self.n[s] = self.n.get(s, 0) + k
        self.last = s
        return k

    def skip(self, s, k=1):
        self.n[s] = self.n.get(s, 0) + k

    def sofar(self, s, back=0):
        v = self.n.get(s, 0) - back
        if self.i is not None and self.per.get(s, 0):
            return self.i * self.per[s] + v
        return v

    def next(self, s, k=1):
        self.skip(s, k)
        return self.sofar(s)

    def seen(self, s, back=0):
        if self.n.get(s, 0) - back <= 0 and self.i is not None:
            raise ValueError(f"{s.name}: the first turn would wait for nothing")
        return self.n.get(s, 0) - back > 0

    def slot(self):
        self.m += 1
        return (self.m - 1) % 2

    @contextmanager
    def loop(self, turns, per):
        start, m = dict(self.n), self.m
        with self.eng.Fori(0, turns) as i:
            self.i, self.per = i, per
            yield i
        got = {s: v - start.get(s, 0) for s, v in self.n.items() if v != start.get(s, 0)}
        if got != {s: v for s, v in per.items() if v}:
            raise ValueError(f"a turn adds { {s.name: v for s, v in got.items()} }, stated { {s.name: v for s, v in per.items()} }")
        for s, v in per.items():
            self.n[s] = start.get(s, 0) + turns * v
        self.i, self.per = None, {}
        if (self.m - m) % 2:
            raise ValueError("a turn takes an odd number of blocks")
        self.m += (turns - 1) * (self.m - m)


def shape_constants():
    dist = np.arange(512) - 255
    n = np.maximum(dist, 0)
    nf = np.maximum(n, 1).astype(np.float32)
    large = 16 + (np.log(nf / np.float32(16)) / np.float32(math.log(8)) * np.float32(16)).astype(np.int32)
    bucket = np.where(n < 16, n, np.minimum(large, NB - 1))
    fwd = np.zeros((NB + 1, 512), np.float32)
    for j in range(511):
        if dist[j] < 0:
            fwd[NB, j] = NEG
        else:
            fwd[bucket[j], j] = 1.0
    rev = np.zeros((NB + 1, 512), np.float32)
    rev[:, :511] = fwd[:, :511][:, ::-1]
    q = np.arange(P)[:, None]
    k = np.arange(P)[None, :]
    tri = np.where(k <= q, 0.0, NEG).astype(np.float32)
    mask = np.concatenate([np.zeros((P, P), np.float32), tri], axis=1)
    t = np.arange(S).reshape(NT, P).T[:, :, None]
    cend = np.arange(NCMP)[None, None, :] * 16 + 31
    cmask = np.zeros((P, NT, 16), np.float32)
    cmask[:, :, :NCMP] = (t >= cend)
    inv = (1.0 / (np.float32(10000.0) ** (np.arange(0, 64, 2, dtype=np.float32) / np.float32(64)))).astype(np.float32)
    return {
        "c_ident": np.eye(P, dtype=np.float32),
        "c_fwd": fwd,
        "c_flip": np.ascontiguousarray(np.eye(P, dtype=np.float32)[::-1]),
        "c_rev": rev,
        "c_mask": mask,
        "c_cmask": cmask.reshape(P, NT * 16),
        "c_inv": np.tile(inv[None, :], (P, 1)),
        "c_upper": np.ascontiguousarray((k >= q).astype(np.float32)),
    }


def build(nc, d, out, stop=None):
    ctx = ExitStack()
    with ctx:
        sb = lambda n, s, dt=F32: ctx.enter_context(nc.sbuf_tensor(n, s, dt))
        sem = lambda n: ctx.enter_context(nc.semaphore(n))

        raw = sb("raw", [P, 2, BLK])
        wh = sb("wh", [P, 2, BLK], F32R)
        wl = sb("wl", [P, 2, BLK], F32R)
        xT = sb("xT", [P, DC, S])
        yT = sb("yT", [P, DC, S])
        ah = sb("ah", [P, DC, S], F32R)
        al = sb("al", [P, DC, S], F32R)
        ar = sb("ar", [P, 14336])
        ar_r = sb("ar_r", [P, 4096], F32R)
        ident = sb("ident", [P, P])
        ones = sb("ones", [P, P])
        cinv = sb("cinv", [P, 32])
        mask = sb("mask", [P, S])
        gT = sb("gT", [P, P])
        g2 = sb("g2", [P, P])
        st = sb("st", [P, 2, S])
        sm = sb("sm", [P, 608])
        ps = ctx.enter_context(nc.psum_tensor("ps", [P, 8, 512], F32))

        s_const = sem("s_const")
        s_rows = sem("s_rows")
        s_raw = [sem("s_raw0"), sem("s_raw1")]
        s_hi = sem("s_hi")
        s_lo = sem("s_lo")
        s_mm = sem("s_mm")
        s_ev = sem("s_ev")
        s_evd = sem("s_evd")
        s_a = sem("s_a")
        s_d = sem("s_d")
        s_u = sem("s_u")
        s_uh = sem("s_uh")
        s_op = sem("s_op")
        s_sq = sem("s_sq")
        s_ss = sem("s_ss")
        s_var = sem("s_var")
        s_rt = sem("s_rt")
        s_x = sem("s_x")
        s_tp = sem("s_tp")
        s_tpe = sem("s_tpe")
        s_stg = sem("s_stg")
        s_sc = sem("s_sc")
        s_scd = sem("s_scd")
        s_mx = sem("s_mx")
        s_e = sem("s_e")
        s_pt = sem("s_pt")
        s_pc = sem("s_pc")
        s_o = sem("s_o")
        s_od = sem("s_od")
        s_g = sem("s_g")
        s_p = sem("s_p")
        s_out = sem("s_out")
        s_fwd = sem("s_fwd")
        s_cin = sem("s_cin")
        s_wo = sem("s_wo")
        s_small = sem("s_small")
        s_scr = sem("s_scr")
        s_dec = sem("s_dec")
        s_mix = sem("s_mix")
        s_mixp = sem("s_mixp")
        s_mixa = sem("s_mixa")

        scratch = nc.dram_tensor("bias_rows", [H64, 512], F32, kind="Internal").ap()
        bias_kept = nc.dram_tensor("bias_kept", [P, H64 * S], F32, kind="Internal").ap()

        def view(t, at, shape):
            n = math.prod(shape[1:])
            v = t[:, at:at + n]
            if len(shape) == 2:
                return v
            names = "abcd"[:len(shape) - 1]
            return v.rearrange(f"p ({' '.join(names)}) -> p {' '.join(names)}", **{c: s for c, s in zip(names[1:], shape[2:])})

        qk = view(ar, 0, [P, DC, 2, S])
        vv = view(ar, 4096, [P, NT, D])
        bias = view(ar, 6144, [P, H64, S])
        scb = view(ar, 10240, [P, 2, 384])
        eb = view(ar, 11008, [P, 2, 384])
        ptb = view(ar, 11776, [P, 2, 384])
        stg = view(ar, 12544, [P, 2, S])
        fcm = view(ar, 6144, [P, H64, S])
        orow = yT[:, :, :].rearrange("p c t -> p (c t)").rearrange("p (q n) -> p q n", q=NT)
        rr = view(ar, 13312, [P, 2, 2, S])
        hh = view(ar_r, 0, [P, 2, 4, S])
        hl = view(ar_r, 2048, [P, 2, 4, S])
        sq = view(ar, 0, [P, DC, S])
        tn = view(ar, 2048, [P, DC, S])
        sg = view(ar, 0, [P, DC, S])
        pT = view(ar_r, 0, [P, 2, S])
        pTl = view(ar_r, 512, [P, 2, S])
        prow = view(ar, 4096, [P, NT, S])
        bank = lambda b: ps[:, b, :].rearrange("p (g t) -> p g t", g=2)

        def wv(t, slot, cols, kc):
            return t[:, slot, 0:kc * cols].rearrange("p (k n) -> p k n", n=cols)

        total = [0]
        def load(E, slot, parts):
            E.eng.wait_ge(s_lo, E.next(s_lo))
            total[0] = E.m
            for dst, src in parts:
                E.eng.dma_start(dst, src).then_inc(s_raw[slot], 16)

        def sp_cols(E, w, cols, kc):
            slot = E.slot()
            v, half = wv(raw, slot, cols, kc), kc // 2
            src = w.rearrange("(k p) n -> p k n", p=P)
            load(E, slot, [(v[:, 0:half, :], src[:, 0:half, :]), (v[:, half:, :], src[:, half:, :])])

        def sp_mlp(E, w1, w2):
            w1v = w1.rearrange("k (f n) -> f k n", n=512)
            w2v = w2.rearrange("(f r) n -> f r n", r=512)
            n = w1v.shape[0]
            sp_cols(E, w1v[0], 512, 8)
            with E.loop((n - 2) // 2, {s_lo: 4}) as i:
                for u in range(2):
                    sp_cols(E, w1v[2 * i + 1 + u], 512, 8)
                    sp_cols(E, w2v[2 * i + u], 1024, 4)
            sp_cols(E, w1v[n - 1], 512, 8)
            sp_cols(E, w2v[n - 2], 1024, 4)
            sp_cols(E, w2v[n - 1], 1024, 4)

        def sp_glu(E, w13, w2):
            wv13 = w13.rearrange("(k p) (h f n) -> f h p k n", p=P, h=2, n=256)
            w2v = w2.rearrange("(f r) n -> f r n", r=256)
            n = wv13.shape[0]

            def up(f):
                slot = E.slot()
                v = wv(raw, slot, 512, 8)
                load(E, slot, [(v[:, :, 0:256], wv13[f, 0]), (v[:, :, 256:512], wv13[f, 1])])
            up(0)
            with E.loop((n - 3) // 2, {s_lo: 4}) as i:
                for u in range(2):
                    up(2 * i + 1 + u)
                    sp_cols(E, w2v[2 * i + u], 1024, 2)
            for f in (n - 2, n - 1):
                up(f)
                sp_cols(E, w2v[f - 1], 1024, 2)
            sp_cols(E, w2v[n - 1], 1024, 2)

        def act_hi(E):
            if E.m >= total[0]:
                return
            slot = E.slot()
            E.eng.wait_ge(s_raw[slot], E.next(s_raw[slot], 32))
            nc.scalar.activation(wh[:, slot, :], raw[:, slot, :], ACT.Copy).then_inc(s_hi, E.adds(s_hi))

        def dve_lo(E, mm=0):
            E.skip(s_mm, mm)
            if E.m >= total[0]:
                return
            slot = E.slot()
            E.eng.wait_ge(s_hi, E.next(s_hi))
            nc.vector.tensor_tensor(wl[:, slot, :], raw[:, slot, :], wh[:, slot, :].bitcast(F32), ALU.subtract).then_inc(s_lo, E.adds(s_lo))

        def mm3(o, wa, wb, xa, xb, start, stop):
            nc.tensor.matmul(o, wa, xa, start=start, stop=False)
            nc.tensor.matmul(o, wa, xb, start=False, stop=False)
            return nc.tensor.matmul(o, wb, xa, start=False, stop=stop)

        def pe_T(E, cols, kc, xa, xb, b0, width=S):
            slot = E.slot()
            E.eng.wait_ge(s_lo, E.next(s_lo))
            a, b = wv(wh, slot, cols, kc), wv(wl, slot, cols, kc)
            nm = cols // P
            for m in range(nm):
                o = ps[:, b0 + m // 2, (m % 2) * S:(m % 2) * S + width]
                for k in range(kc):
                    c = slice(m * P, (m + 1) * P)
                    last = mm3(o, a[:, k, c], b[:, k, c], xa[:, k], xb[:, k], k == 0, k == kc - 1)
                if m % 2 or m == nm - 1:
                    last.then_inc(s_mm, E.adds(s_mm))

        def pe_rows(E, cols, kc, xa, xb, b0):
            slot = E.slot()
            E.eng.wait_ge(s_lo, E.next(s_lo))
            a, b = wv(wh, slot, cols, kc), wv(wl, slot, cols, kc)
            for q in range(NT):
                for k in range(kc):
                    t = slice(q * P, (q + 1) * P)
                    last = mm3(ps[:, b0 + q, 0:cols], xa[:, k, t], xb[:, k, t], a[:, k, :], b[:, k, :], k == 0, k == kc - 1)
                last.then_inc(s_mm, E.adds(s_mm))

        def act_copy(E, dsts, b0):
            for n, dst in enumerate(dsts):
                E.eng.wait_ge(s_mm, E.next(s_mm))
                nc.scalar.activation(dst, bank(b0 + n) if len(dst.shape) == 3 else ps[:, b0 + n, :], ACT.Copy).then_inc(s_ev, E.adds(s_ev))
            act_hi(E)

        def act_stats(E, src, nch, wait=True):
            if wait:
                E.eng.wait_ge(s_x, E.next(s_x))
            for h in range(0, nch, 4):
                n = min(4, nch - h)
                nc.scalar.activation(sq[:, h:h + n, :], src[:, h:h + n, :], ACT.Square).then_inc(s_sq, E.adds(s_sq))
            E.eng.wait_ge(s_var, E.next(s_var))
            nc.scalar.activation(st[:, 1, :], st[:, 0, :], ACT.Sqrt).then_inc(s_rt, E.adds(s_rt))

        def pe_stats(E, nch, b=7):
            pe_free(E)
            for h in range(0, nch, 4):
                n = min(4, nch - h)
                E.eng.wait_ge(s_sq, E.next(s_sq))
                for c in range(h, h + n):
                    last = nc.tensor.matmul(ps[:, b, 0:S], ones[:, :], sq[:, c, :], start=c == 0, stop=c == nch - 1)
            last.then_inc(s_ss, E.adds(s_ss))
            E.skip(s_var)

        def dve_stats(E, nch, b=7):
            E.eng.wait_ge(s_ss, E.next(s_ss))
            nc.vector.tensor_scalar(st[:, 0, :], ps[:, b, 0:S], 1.0 / (nch * P), EPS, ALU.mult, ALU.add).then_inc(s_var, E.adds(s_var))
            E.eng.wait_ge(s_rt, E.next(s_rt))
            nc.vector.reciprocal(st[:, 1, :], st[:, 1, :]).then_inc(s_d, E.adds(s_d))
            E.eng.wait_ge(E.last, E.sofar(E.last))

        def dve_operand(E, src, gcol, nch, oh, ol, normed=True, tmp=None):
            tmp = tn if tmp is None else tmp
            if normed:
                for c in range(nch):
                    nc.vector.scalar_tensor_tensor(out=tmp[:, c, :], in0=src[:, c, :], scalar=gcol(c), in1=st[:, 1, :],
                                                          op0=ALU.mult, op1=ALU.mult).then_inc(s_u, E.adds(s_u))
                E.eng.wait_ge(s_u, E.sofar(s_u))
            else:
                tmp = src
            for c in range(nch):
                E.eng.wait_ge(s_uh, E.next(s_uh))
                nc.vector.tensor_tensor(ol[:, c, :], tmp[:, c, :], oh[:, c, :].bitcast(F32), ALU.subtract).then_inc(s_op, E.adds(s_op))

        def act_operand(E, src, nch, oh, normed=True, tmp=None):
            tmp = (tn if tmp is None else tmp) if normed else src
            if not normed:
                E.eng.wait_ge(s_x, E.next(s_x))
            for c in range(nch):
                if normed:
                    E.eng.wait_ge(s_u, E.next(s_u))
                nc.scalar.activation(oh[:, c, :], tmp[:, c, :], ACT.Copy).then_inc(s_uh, E.adds(s_uh))
            E.skip(s_op, nch)

        def dve_residual(E, gcol, scale=None):
            for c in range(DC):
                nc.vector.scalar_tensor_tensor(out=tn[:, c, :], in0=yT[:, c, :], scalar=gcol(c), in1=st[:, 1, :],
                                                      op0=ALU.mult, op1=ALU.mult).then_inc(s_d, E.adds(s_d))
            E.eng.wait_ge(s_d, E.sofar(s_d))
            nc.vector.tensor_tensor(xT[:, :, :], xT[:, :, :], tn[:, :, :], ALU.add).then_inc(s_x, E.adds(s_x))
            E.eng.wait_ge(s_x, E.sofar(s_x))

        def pe_h(E):
            if E.seen(s_ev):
                E.eng.wait_ge(s_ev, E.sofar(s_ev))
            pe_T(E, 512, 8, ah, al, 0)
            E.skip(s_ev, 2)

        def pe_y(E, buf, kc, n_op):
            E.eng.wait_ge(s_op, E.next(s_op, n_op))
            if E.seen(s_evd):
                E.eng.wait_ge(s_evd, E.sofar(s_evd))
            pe_T(E, 1024, kc, hh[:, buf], hl[:, buf], 4)
            E.skip(s_evd, 4)

        def act_h(E, buf):
            if E.seen(s_op):
                E.eng.wait_ge(s_op, E.sofar(s_op))
            for n in range(2):
                E.eng.wait_ge(s_mm, E.next(s_mm))
                nc.scalar.activation(rr[:, n], bank(n), ACT.Relu).then_inc(s_ev, E.adds(s_ev))
                E.eng.wait_ge(s_ev, E.sofar(s_ev))
                nc.scalar.activation(hh[:, buf, 2 * n:2 * n + 2, :], rr[:, n], ACT.Square).then_inc(s_uh, E.adds(s_uh))
            E.skip(s_op, 2)
            act_hi(E)

        def act_y(E):
            E.eng.wait_ge(s_mm, E.next(s_mm, 4))
            act_hi(E)

        def dve_h(E, buf):
            for n in range(2):
                E.eng.wait_ge(s_uh, E.next(s_uh))
                nc.vector.tensor_tensor(rr[:, n], rr[:, n], rr[:, n], ALU.mult).then_inc(s_d, E.adds(s_d))
                E.eng.wait_ge(s_d, E.sofar(s_d))
                nc.vector.tensor_tensor(hl[:, buf, 2 * n:2 * n + 2, :], rr[:, n], hh[:, buf, 2 * n:2 * n + 2, :].bitcast(F32), ALU.subtract).then_inc(s_op, E.adds(s_op))
            dve_lo(E, 2)

        def dve_y(E):
            E.eng.wait_ge(s_evd, E.sofar(s_evd))
            for n in range(4):
                E.eng.wait_ge(s_mm, E.next(s_mm))
                nc.vector.tensor_tensor(yT[:, 2 * n:2 * n + 2, :], yT[:, 2 * n:2 * n + 2, :], bank(4 + n), ALU.add).then_inc(s_evd, E.adds(s_evd))
            dve_lo(E)

        def ahead(E, n, h, y, per):
            h(0)
            turns = (n - 2) // 2
            with E.loop(turns, per):
                h(1)
                y(0)
                h(0)
                y(1)
            for f in range(2 * turns, n - 1):
                h((f + 1) % 2)
                y(f % 2)
            y((n - 1) % 2)

        v4 = vv.rearrange("p q (j n) -> p q j n", n=P)
        o4 = orow.rearrange("p q (j n) -> p q j n", n=P)
        nm, sums, rs = view(sm, 0, [P, 2, 2]), view(sm, 4, [P, 2, 2]), view(sm, 8, [P, 2, 2])
        lamn = view(sm, 12, [P, 2])
        lamL = [0]
        gates = view(sm, 16, [P, NT, 48])
        g6 = gates.rearrange("p q (j c b) -> p q j c b", c=2, b=3)
        COLS = ((0, P), (P, 384))

        def pe_scores(E, fox=None):
            E.eng.wait_ge(s_stg, E.next(s_stg))
            if E.seen(s_scd):
                E.eng.wait_ge(s_scd, E.sofar(s_scd))
            for c in range(2):
                lo = slice(64 * c, 64 * c + 64)
                for q, (a, b) in enumerate(COLS):
                    o, keys = ps[:, c, a:b], slice(0, b - a)
                    if fox is not None:
                        nc.tensor.matmul(o, ones[:, :], fcm[:, 2 * fox + c, keys], start=True, stop=False)
                    last = nc.tensor.matmul(o, stg[lo, 0, q * P:(q + 1) * P], stg[lo, 1, keys], start=fox is None, stop=True)
                last.then_inc(s_sc, E.adds(s_sc))
            E.skip(s_scd, 2)

        def pe_values(E, j, shared, wide=64, v=None):
            E.eng.wait_ge(s_e, E.next(s_e))
            for c in range(2):
                for n in range(3):
                    last = nc.tensor.transpose(ps[:, 2 + c, n * P:(n + 1) * P], eb[:, c, n * P:(n + 1) * P], ident[:, :])
                last.then_inc(s_pt, E.adds(s_pt))
            if E.seen(s_od):
                E.eng.wait_ge(s_od, E.sofar(s_od))
            for c in range(2):
                E.eng.wait_ge(s_pc, E.next(s_pc))
                if v is not None:
                    val = lambda t: v(t, j, c)
                elif wide == P:
                    val = lambda t: vv[:, t, :].rearrange("p (h n) -> p h n", n=P)[:, 2 * j + c, :]
                else:
                    val = lambda t: v4[:, t, j, :] if shared else v4[:, t, j, 64 * c:64 * c + 64]
                w = P if shared else wide
                nc.tensor.matmul(ps[:, 4 + c, 0:w], ptb[:, c, 0:P], val(0), start=True, stop=True)
                nc.tensor.matmul(ps[:, 4 + c, P:P + w], ptb[:, c, P:2 * P], val(0), start=True, stop=False)
                last = nc.tensor.matmul(ps[:, 4 + c, P:P + w], ptb[:, c, 2 * P:], val(1), start=False, stop=True)
                last.then_inc(s_o, E.adds(s_o))
            E.skip(s_od, 2)

        def act_exp(E):
            E.eng.wait_ge(s_mx, E.next(s_mx))
            for c in range(2):
                for q, (a, b) in enumerate(COLS):
                    last = nc.scalar.activation(eb[:, c, a:b], scb[:, c, a:b], ACT.Exp, bias=nm[:, c, q:q + 1], accum_out=sums[:, c, q:q + 1])
            last.then_inc(s_e, E.adds(s_e))

        def act_pt(E):
            if E.seen(s_o):
                E.eng.wait_ge(s_o, E.sofar(s_o))
            for c in range(2):
                E.eng.wait_ge(s_pt, E.next(s_pt))
                nc.scalar.activation(ptb[:, c, :], ps[:, 2 + c, 0:384], ACT.Copy).then_inc(s_pc, E.adds(s_pc))
            E.skip(s_o, 2)

        def dve_stage(E, j, src=None):
            nc.vector.tensor_copy(stg[:, :, :], (qk if src is None else src)[:, j, :, :]).then_inc(s_stg, E.adds(s_stg))

        def dve_scale(E, j, table, scale):
            for c in range(2):
                E.eng.wait_ge(s_sc, E.next(s_sc))
                for a, b in COLS:
                    tab = bias[:, 2 * j + c, :] if table else mask[:, :]
                    tab = tab[:, S - (b - a):]
                    last = nc.vector.scalar_tensor_tensor(out=scb[:, c, a:b], in0=ps[:, c, a:b], scalar=scale, in1=tab, op0=ALU.mult, op1=ALU.add)
                last.then_inc(s_scd, E.adds(s_scd))
            E.eng.wait_ge(s_scd, E.sofar(s_scd))
            for q, (a, b) in enumerate(COLS):
                last = nc.vector.tensor_reduce(nm[:, :, q], scb[:, :, a:b], AX.X, ALU.max, negate=True)
            last.then_inc(s_mx, E.adds(s_mx))

        def dve_sums(E, j, kind, branch=0):
            E.eng.wait_ge(s_e, E.next(s_e))
            E.eng.wait_ge(E.last, E.sofar(E.last))
            nc.vector.reciprocal(rs[:, :, :], sums[:, :, :]).then_inc(s_d, E.adds(s_d))
            E.eng.wait_ge(s_d, E.sofar(s_d))
            if kind == "da":
                nc.vector.tensor_scalar(rs[:, 1, :], rs[:, 1, :], lamn[:, lamL[0]:lamL[0] + 1], None, ALU.mult).then_inc(s_d, E.adds(s_d))
                E.eng.wait_ge(s_d, E.sofar(s_d))
            if kind == "nsa":
                nc.vector.tensor_tensor(rs[:, :, :], rs[:, :, :], g6[:, :, j, :, branch].rearrange("p q c -> p c q"), ALU.mult).then_inc(s_d, E.adds(s_d))
                E.eng.wait_ge(s_d, E.sofar(s_d))

        def dve_out(E, j, kind, add=False, wide=64):
            for c in range(2):
                E.eng.wait_ge(s_o, E.next(s_o))
                for q in range(NT):
                    w = P if kind == "da" else wide
                    if kind == "da":
                        o = o4[:, q, j, :]
                    elif wide == P:
                        o = orow[:, q, :].rearrange("p (h n) -> p h n", n=P)[:, 2 * j + c, :]
                    else:
                        o = o4[:, q, j, 64 * c:64 * c + 64]
                    src = ps[:, 4 + c, q * P:q * P + w]
                    if add or (kind == "da" and c):
                        last = nc.vector.scalar_tensor_tensor(out=o, in0=src, scalar=rs[:, c, q:q + 1], in1=o, op0=ALU.mult, op1=ALU.add)
                    else:
                        last = nc.vector.tensor_scalar(o, src, rs[:, c, q:q + 1], None, ALU.mult)
                last.then_inc(s_od, E.adds(s_od))
                if kind == "da" and c == 0:
                    E.eng.wait_ge(s_od, E.sofar(s_od))

        def pe_attention(E, n, shared=False, fox=False, wide=64, scores=pe_scores, v=None):
            f = (lambda j: j) if fox else (lambda j: None)
            scores(E, f(0))
            scores(E, f(1))
            pe_values(E, 0, shared, wide, v)
            with E.loop(n - 2, {s_stg: 1, s_scd: 2, s_sc: 2, s_e: 1, s_pt: 2, s_pc: 2, s_o: 2, s_od: 2}) as i:
                scores(E, f(i + 2))
                pe_values(E, i + 1, shared, wide, v)
            pe_values(E, n - 1, shared, wide, v)

        def act_attention(E, n):
            act_exp(E)
            act_pt(E)
            with E.loop(n - 1, {s_mx: 1, s_e: 1, s_pt: 2, s_pc: 2, s_o: 2}):
                act_exp(E)
                act_pt(E)

        def dve_attention(E, n, kind, scale, branch=0, src=None, table=True, wide=64, stage=dve_stage):
            add = branch > 0
            stage(E, 0, src)
            dve_scale(E, 0, table, scale)
            stage(E, 1, src)
            dve_sums(E, 0, kind, branch)
            per = {s_sc: 2, s_scd: 2, s_mx: 1, s_stg: 1, s_o: 2, s_od: 2, s_e: 1, s_d: 1 + (kind in ("da", "nsa"))}
            with E.loop(n - 2, per) as i:
                dve_scale(E, i + 1, table, scale)
                stage(E, i + 2, src)
                dve_out(E, i, kind, add, wide)
                dve_sums(E, i + 1, kind, branch)
            dve_scale(E, n - 1, table, scale)
            dve_out(E, n - 2, kind, add, wide)
            dve_sums(E, n - 1, kind, branch)
            dve_out(E, n - 1, kind, add, wide)

        def pe_turn(E, src=None, ready=None):
            src = orow if src is None else src
            if ready is None:
                E.eng.wait_ge(s_mix, E.next(s_mix))
            else:
                if E.seen(ready):
                    E.eng.wait_ge(ready, E.sofar(ready))
            for b in range(4):
                for c in (2 * b, 2 * b + 1):
                    for q in range(NT):
                        o = ps[:, b, (c % 2) * S + q * P:(c % 2) * S + (q + 1) * P]
                        last = nc.tensor.transpose(o, src[:, q, c * P:(c + 1) * P], ident[:, :])
                last.then_inc(s_tp, E.adds(s_tp))

        def act_turn(E, scale=1.0, oh=None):
            oh = ah if oh is None else oh
            for b in range(4):
                E.eng.wait_ge(s_tp, E.next(s_tp))
                for c in (2 * b, 2 * b + 1):
                    sc = scale(c) if callable(scale) else scale
                    last = nc.scalar.activation(oh[:, c, :], bank(b)[:, c % 2, :], ACT.Copy, scale=sc)
                last.then_inc(s_uh, E.adds(s_uh))
            E.skip(s_op, 4)

        def dve_turn(E, scale=1.0, oh=None, ol=None):
            oh, ol = (ah, al) if oh is None else (oh, ol)
            for b in range(4):
                E.eng.wait_ge(s_uh, E.next(s_uh))
                for c in (2 * b, 2 * b + 1):
                    sc = scale(c) if callable(scale) else scale
                    last = nc.vector.scalar_tensor_tensor(out=ol[:, c, :], in0=bank(b)[:, c % 2, :], scalar=sc, in1=oh[:, c, :].bitcast(F32),
                                                          op0=ALU.mult, op1=ALU.subtract)
                last.then_inc(s_op, E.adds(s_op))

        def pe_out(E, n_op):
            E.eng.wait_ge(s_op, E.next(s_op, n_op))
            pe_free(E)
            pe_T(E, 512, 8, ah, al, 0)
            pe_T(E, 512, 8, ah, al, 2)
            E.skip(s_ev, 4)

        def act_out(E):
            act_copy(E, [yT[:, 0:2, :], yT[:, 2:4, :]], 0)
            act_copy(E, [yT[:, 4:6, :], yT[:, 6:8, :]], 2)
            E.eng.wait_ge(s_ev, E.sofar(s_ev))

        def dve_out_splits(E):
            dve_lo(E, 2)
            dve_lo(E, 2)

        def pe_free(E):
            for s in (s_ev, s_evd, s_var, s_scd, s_pc, s_od):
                if E.seen(s):
                    E.eng.wait_ge(s, E.sofar(s))

        xrow = view(ar, 0, [P, NT, D])
        grow = view(ar, 2048, [P, P])
        g2row = view(ar, 2176, [P, P])
        lrow = view(ar, 2304, [P, 512])
        lprod = view(ar, 2816, [P, 2, 2, 64])
        rel = view(sm, 144, [P, H64])
        crev = view(ar, 3088, [P, 512])
        brow = view(ar, 13312, [P, 512])
        lsum = view(sm, 120, [P, 2, 2])
        subl = view(sm, 124, [P, 2])
        G2 = {}
        packs, at = [], 0
        for name, n in (("da_subln", 2), ("ln_ffn1_2", 16), ("ln_mix_2", 16), ("ln_ffn2_2", 16), ("ssd_norm_2", 32),
                        ("q_lora_norm_2", 8), ("kv_lora_norm_2", 4), ("nsa_cmp_pe", 32)):
            G2[name] = at
            packs.append((name, at, n))
            at += n
        n2 = at
        flat = lambda ap: ap.rearrange({1: "a -> a", 2: "a b -> (a b)", 3: "a b c -> (a b c)", 4: "a b c d -> (a b c d)"}[len(ap.shape)])
        DA_L = [0, 3]

        def sp_start(E):
            e = E.eng
            e.dma_start(xrow[:, :, :], d["x"][0].rearrange("(q p) n -> p q n", p=P)).then_inc(s_const, 16)
            e.dma_start(ident[:, :], d["c_ident"]).then_inc(s_const, 16)
            e.dma_start(grow[:, :], flat(d["norm_g"]).rearrange("(r n) -> r n", n=P)).then_inc(s_const, 16)
            for name, at, n in packs:
                e.dma_start(g2row[at:at + n, :], flat(d[name]).rearrange("(r n) -> r n", n=P)).then_inc(s_const, 16)
            e.dma_start(rel[0:NB, :], d["rel_bias"]).then_inc(s_const, 16)
            e.dma_start(cinv[:, :], d["c_inv"]).then_inc(s_const, 16)
            e.dma_start(crev[0:NB + 1, :], d["c_rev"]).then_inc(s_const, 16)
            e.dma_start(mask[:, :], d["c_mask"]).then_inc(s_const, 16)
            e.dma_start(lrow[:, :], flat(d["da_lambda"]).partition_broadcast(P)).then_inc(s_const, 16)
            e.dma_start(bfc[0:H64, :], flat(d["fox_b_f"]).rearrange("(h a) -> h a", a=1)).then_inc(s_const, 16)
            e.dma_start(cmaskv[:, :, :], d["c_cmask"].rearrange("p (q n) -> p q n", q=NT)).then_inc(s_const, 16)
            for n, w2 in enumerate((cw2k, cw2v)):
                e.dma_start(w2[:, :, :], d["nsa_cmp_w2"][0, n].rearrange("(k p) n -> p k n", p=P)).then_inc(s_const, 16)
            e.dma_start(flip[:, :], d["c_flip"]).then_inc(s_const, 16)
        n_const = 16 * (13 + len(packs))
        flip = view(ar, 10240, [P, P])
        bfc = view(sm, 126, [P, 1])
        cmaskv = view(sm, 220, [P, NT, 16])
        cw2k, cw2v = view(sm, 256, [P, 2, 64]), view(sm, 384, [P, 2, 64])

        def pool_start(E):
            e = E.eng
            e.wait_ge(s_mixa, 1)
            e.dma_start(scratch, brow[0:H64, :]).then_inc(s_scr, 16)
            e.wait_ge(s_scr, 16)
            e.dma_start(bias[:, :, :], bass.AP(scratch.tensor, 0, [[1, P], [512, H64], [1, S]])).then_inc(s_rows, 16)
            e.wait_ge(s_mixa, 3)
            e.dma_start(bias_kept, bias.rearrange("p h k -> p (h k)")).then_inc(s_scr, 16)
            e.wait_ge(s_scr, 32)

        def pe_flip(E):
            E.eng.wait_ge(s_rows, E.next(s_rows, 16))
            pe_free(E)
            for b in range(8):
                nc.tensor.matmul(ps[:, b, :], flip[:, :], bias[:, 2 * b:2 * b + 2, :].rearrange("p h k -> p (h k)"), start=True, stop=True).then_inc(s_tp, E.adds(s_tp))
            E.eng.wait_ge(s_mixa, E.next(s_mixa))

        def act_flip(E):
            for b in range(8):
                E.eng.wait_ge(s_tp, E.next(s_tp))
                last = nc.scalar.activation(bias[:, 2 * b:2 * b + 2, :], bank(b), ACT.Copy)
            last.then_inc(s_mixa, E.adds(s_mixa))

        def pe_start(E):
            E.eng.wait_ge(s_const, E.next(s_const, n_const))
            E.eng.wait_ge(s_g, E.next(s_g))
            for b in range(4):
                for c in (2 * b, 2 * b + 1):
                    for q in range(NT):
                        o = ps[:, b, (c % 2) * S + q * P:(c % 2) * S + (q + 1) * P]
                        last = nc.tensor.transpose(o, xrow[:, q, c * P:(c + 1) * P], ident[:, :])
                last.then_inc(s_tp, E.adds(s_tp))
            nc.tensor.transpose(ps[:, 4, 0:P], grow[:, :], ident[:, :])
            nc.tensor.transpose(ps[:, 4, P:P + n2], g2row[0:n2, :], ident[0:n2, 0:n2]).then_inc(s_tp, E.adds(s_tp))
            nc.tensor.matmul(ps[0:H64, 5, :], rel[0:NB + 1, :], crev[0:NB + 1, :], start=True, stop=True).then_inc(s_tp, E.adds(s_tp))
            E.skip(s_ev, 4)
            E.skip(s_evd)
            E.skip(s_lo, 2)
            E.skip(s_mix)
            E.skip(s_mixa, 2)

        def act_start(E):
            for b in range(4):
                E.eng.wait_ge(s_tp, E.next(s_tp))
                nc.scalar.activation(xT[:, 2 * b:2 * b + 2, :], bank(b), ACT.Copy).then_inc(s_ev, E.adds(s_ev))
            E.eng.wait_ge(s_tp, E.next(s_tp))
            nc.scalar.activation(gT[:, :], ps[:, 4, 0:P], ACT.Copy)
            nc.scalar.activation(g2[:, 0:n2], ps[:, 4, P:P + n2], ACT.Copy).then_inc(s_a, E.adds(s_a))
            E.eng.wait_ge(s_tp, E.next(s_tp))
            nc.scalar.activation(brow[0:H64, :], ps[0:H64, 5, :], ACT.Copy).then_inc(s_mixa, E.adds(s_mixa))
            E.eng.wait_ge(s_mix, E.next(s_mix))
            nc.scalar.activation(lsum[:, :, :], lsum[:, :, :], ACT.Exp).then_inc(s_mixa, E.adds(s_mixa))
            act_hi(E)
            act_hi(E)
            E.eng.wait_ge(s_ev, E.sofar(s_ev))

        def dve_start(E):
            nc.vector.memset(ones[:, :], 1.0)
            nc.vector.memset(rel[NB:NB + 1, :], 1.0).then_inc(s_g, E.adds(s_g))
            for slot in range(2):
                nc.vector.memset(raw[:, slot, :], 0.0).then_inc(s_lo, E.adds(s_lo))
            nc.vector.memset(st[:, :, :], 0.0).then_inc(s_evd, E.adds(s_evd))
            E.eng.wait_ge(s_const, E.next(s_const, n_const))
            lv = lrow.rearrange("p (l a b n) -> p l a b n", l=2, a=2, b=2)
            nc.vector.tensor_tensor(lprod[:, :, :, :], lv[:, :, :, 0, :], lv[:, :, :, 1, :], ALU.mult).then_inc(s_d, E.adds(s_d))
            E.eng.wait_ge(E.last, E.sofar(E.last))
            nc.vector.tensor_reduce(lsum[:, :, :], lprod[:, :, :, :], AX.X, ALU.add).then_inc(s_mix, E.adds(s_mix))
            E.eng.wait_ge(s_mixa, E.next(s_mixa, 2))
            for n, layer in enumerate(DA_L):
                nc.vector.tensor_scalar(lamn[:, n:n + 1], lsum[:, n, 1:2], lsum[:, n, 0:1], -LAM_INIT[layer], ALU.subtract, ALU.add).then_inc(s_d, E.adds(s_d))
                nc.vector.tensor_scalar(subl[:, n:n + 1], g2[:, n:n + 1], 1.0 - LAM_INIT[layer], None, ALU.mult).then_inc(s_d, E.adds(s_d))
            dve_lo(E)
            dve_lo(E)

        g1 = lambda layer, which: (lambda c: gT[:, (layer * 4 + which) * DC + c:(layer * 4 + which) * DC + c + 1])
        gg = lambda name, layer, n: (lambda c: g2[:, G2[name] + layer * n + c:G2[name] + layer * n + c + 1])

        def sp_da(E, k):
            w = d["da_w_in"][k].rearrange("k (a n) -> a k n", n=512)
            with E.loop(2, {s_lo: 2}) as i:
                for b in range(2):
                    sp_cols(E, w[2 * i + b], 512, 8)
            for b in range(2):
                sp_cols(E, w[4 + b], 512, 8)
            sp_out(E, d["da_w_out"][k])

        def sp_out(E, w):
            for b in range(2):
                sp_cols(E, w[:, 512 * b:512 * b + 512], 512, 8)

        def pe_qkv(E):
            E.eng.wait_ge(s_op, E.next(s_op, 8))
            pe_free(E)
            with E.loop(2, {s_lo: 2, s_mm: 4, s_ev: 4}):
                for b in range(2):
                    if E.seen(s_ev, 2):
                        E.eng.wait_ge(s_ev, E.sofar(s_ev, 2))
                    pe_T(E, 512, 8, ah, al, 2 * b)
                    E.skip(s_ev, 2)
            for b in range(2):
                if E.seen(s_ev, 2):
                    E.eng.wait_ge(s_ev, E.sofar(s_ev, 2))
                pe_rows(E, 512, 8, ah, al, 2 * b)
                E.skip(s_ev, 2)

        def act_qkv(E):
            with E.loop(2, {s_mm: 4, s_ev: 4, s_raw[0]: 32, s_raw[1]: 32, s_hi: 2}) as i:
                for b in range(2):
                    act_copy(E, [qk[:, 4 * b:4 * b + 2, i, :], qk[:, 4 * b + 2:4 * b + 4, i, :]], 2 * b)
            for b in range(2):
                act_copy(E, [vv[:, q, 512 * b:512 * b + 512] for q in range(NT)], 2 * b)

        def dve_qkv(E):
            with E.loop(2, {s_hi: 2, s_lo: 2, s_mm: 4}):
                dve_lo(E, 2)
                dve_lo(E, 2)
            dve_lo(E, 2)
            dve_lo(E, 2)

        hs = view(sm, 128, [P, 16])
        osq = view(ar, 0, [P, 2048])

        def dve_subln(E):
            of = orow.rearrange("p q (h n) -> p (q h) n", n=P)
            E.eng.wait_ge(s_od, E.sofar(s_od))
            nc.vector.tensor_tensor(osq[:, :], yT[:, :, :].rearrange("p c t -> p (c t)"), yT[:, :, :].rearrange("p c t -> p (c t)"), ALU.mult).then_inc(s_d, E.adds(s_d))
            E.eng.wait_ge(E.last, E.sofar(E.last))
            nc.vector.tensor_reduce(hs[:, :], osq.rearrange("p (h n) -> p h n", n=P), AX.X, ALU.add).then_inc(s_d, E.adds(s_d))
            E.eng.wait_ge(E.last, E.sofar(E.last))
            nc.vector.tensor_scalar(hs[:, :], hs[:, :], 1.0 / P, EPS, ALU.mult, ALU.add).then_inc(s_mix, E.adds(s_mix))
            E.eng.wait_ge(s_mixa, E.next(s_mixa))
            nc.vector.reciprocal(hs[:, :], hs[:, :]).then_inc(s_d, E.adds(s_d))
            E.eng.wait_ge(E.last, E.sofar(E.last))
            nc.vector.tensor_tensor(of, of, hs[:, :].unsqueeze(2).to_broadcast([P, 16, P]), ALU.mult).then_inc(s_mix, E.adds(s_mix))

        def act_subln(E):
            E.eng.wait_ge(s_mix, E.next(s_mix))
            nc.scalar.activation(hs[:, :], hs[:, :], ACT.Sqrt).then_inc(s_mixa, E.adds(s_mixa))
            E.skip(s_mix)

        def sp_rest(E, layer):
            sp_mlp(E, d["mlp_w1"][layer], d["mlp_w2"][layer])
            E.eng.wait_ge(s_x, 4 * layer + 1)
            E.eng.dma_start(prow[:, :, :], d["p"][layer, 0].rearrange("(q p) n -> p q n", p=P)).then_inc(s_p, 16)
            for b in range(2):
                sp_cols(E, d["ple_gate_w"][layer][:, 512 * b:512 * b + 512], 512, 8)
            for b in range(2):
                sp_cols(E, d["ple_w"][layer][:, 512 * b:512 * b + 512], 512, 2)

        def pe_rest(E):
            pe_stats(E, DC)
            pe_stats(E, DC)
            E.eng.wait_ge(s_op, E.next(s_op, 8))
            E.skip(s_evd)
            pe_free(E)
            ahead(E, 8, lambda b: pe_h(E), lambda b: pe_y(E, b, 4, 2), {s_lo: 4, s_mm: 12, s_ev: 4, s_evd: 8, s_op: 4})
            pe_stats(E, DC, 0)
            E.eng.wait_ge(s_p, E.next(s_p, 16))
            for c in range(2):
                for q in range(NT):
                    last = nc.tensor.transpose(ps[:, 6, c * S + q * P:c * S + (q + 1) * P], prow[:, q, c * P:(c + 1) * P], ident[:, :])
            last.then_inc(s_tp, E.adds(s_tp))
            E.eng.wait_ge(s_op, E.next(s_op, 1))
            E.eng.wait_ge(s_op, E.next(s_op, 8))
            pe_free(E)
            pe_T(E, 512, 8, ah, al, 0)
            pe_T(E, 512, 8, ah, al, 2)
            E.skip(s_ev, 4)
            pe_T(E, 512, 2, pT, pTl, 4)
            if E.seen(s_ev):
                E.eng.wait_ge(s_ev, E.sofar(s_ev))
            pe_T(E, 512, 2, pT, pTl, 0)
            E.skip(s_evd, 4)

        def act_rest(E):
            act_stats(E, yT, DC, False)
            act_stats(E, xT, DC)
            act_operand(E, xT, DC, ah)
            ahead(E, 8, lambda b: act_h(E, b), lambda b: act_y(E), {s_mm: 12, s_ev: 4, s_uh: 4, s_op: 4, s_raw[0]: 64, s_raw[1]: 64, s_hi: 4})
            act_stats(E, yT, DC)
            E.eng.wait_ge(s_tp, E.next(s_tp))
            nc.scalar.activation(pT[:, :, :], bank(6), ACT.Copy).then_inc(s_uh, E.adds(s_uh))
            E.skip(s_op)
            act_operand(E, xT, DC, ah, False)
            for b in range(2):
                for n in range(2):
                    E.eng.wait_ge(s_mm, E.next(s_mm))
                    nc.scalar.activation(sg[:, 4 * b + 2 * n:4 * b + 2 * n + 2, :], bank(2 * b + n), ACT.Exp, scale=-1.0).then_inc(s_ev, E.adds(s_ev))
                act_hi(E)
            for b in range(2):
                E.eng.wait_ge(s_mm, E.next(s_mm, 2))
                act_hi(E)

        def dve_rest(E, layer):
            dve_stats(E, DC)
            dve_residual(E, g1(layer, 1))
            dve_stats(E, DC)
            dve_operand(E, xT, g1(layer, 2), DC, ah, al)
            nc.vector.memset(yT[:, :, :], 0.0).then_inc(s_evd, E.adds(s_evd))
            ahead(E, 8, lambda b: dve_h(E, b), lambda b: dve_y(E), {s_uh: 4, s_d: 4, s_op: 4, s_mm: 12, s_evd: 8, s_hi: 4, s_lo: 4})
            E.eng.wait_ge(s_evd, E.sofar(s_evd))
            nc.vector.tensor_copy(sm[:, 253:254], sm[:, 124:125]).then_inc(s_x, E.adds(s_x))
            dve_stats(E, DC, 0)
            dve_residual(E, g1(layer, 3))
            E.eng.wait_ge(s_uh, E.next(s_uh))
            nc.vector.tensor_tensor(pTl[:, :, :], bank(6), pT[:, :, :].bitcast(F32), ALU.subtract).then_inc(s_op, E.adds(s_op))
            dve_operand(E, xT, None, DC, ah, al, normed=False)
            dve_lo(E, 2)
            dve_lo(E, 2)
            nc.vector.tensor_scalar(sg[:, :, :], sg[:, :, :], 1.0, None, ALU.add).then_inc(s_d, E.adds(s_d))
            E.eng.wait_ge(E.last, E.sofar(E.last))
            nc.vector.reciprocal(sg[:, :, :], sg[:, :, :]).then_inc(s_d, E.adds(s_d))
            E.eng.wait_ge(E.last, E.sofar(E.last))
            for b in range(2):
                for n in range(2):
                    E.eng.wait_ge(s_mm, E.next(s_mm))
                    c = 4 * b + 2 * n
                    nc.vector.tensor_tensor(sg[:, c:c + 2, :], sg[:, c:c + 2, :], bank(4 + n if b == 0 else n), ALU.mult).then_inc(s_evd, E.adds(s_evd))
                dve_lo(E)
            E.eng.wait_ge(s_evd, E.sofar(s_evd))
            nc.vector.tensor_tensor(xT[:, :, :], xT[:, :, :], sg[:, :, :], ALU.add).then_inc(s_x, E.adds(s_x))
            E.eng.wait_ge(s_x, E.sofar(s_x))

        onesw = ones[:, 0:1].to_broadcast([P, S])
        fx = view(ar, 10240, [P, S])
        fm = view(ar, 10496, [P, S])
        fn = view(ar, 10752, [P, S])
        fc = view(ar, 11008, [P, S])

        def sp_fox(E):
            w = d["fox_w_in"][0][:, 0:3072].rearrange("k (a n) -> a k n", n=512)
            with E.loop(2, {s_lo: 2}) as i:
                for b in range(2):
                    sp_cols(E, w[2 * i + b], 512, 8)
            for b in range(2):
                sp_cols(E, w[4 + b], 512, 8)
            sp_cols(E, d["fox_w_in"][0][:, 3072:3088], 16, 8)
            sp_out(E, d["fox_w_out"][0])

        def pe_narrow(E, cols, kc, xa, xb, b, at=0):
            slot = E.slot()
            E.eng.wait_ge(s_lo, E.next(s_lo))
            for k in range(kc):
                c = slice(k * cols, k * cols + P)
                last = mm3(ps[:, b, at:at + S], wh[:, slot, c], wl[:, slot, c], xa[:, k], xb[:, k], k == 0, k == kc - 1)
            last.then_inc(s_mm, E.adds(s_mm))

        def pe_fox(E):
            pe_qkv(E)
            if E.seen(s_ev):
                E.eng.wait_ge(s_ev, E.sofar(s_ev))
            pe_narrow(E, 16, 8, ah, al, 0)
            E.skip(s_ev)
            E.skip(s_mix)
            E.skip(s_mixa)
            pe_attention(E, 8, fox=True)
            pe_turn(E, ready=s_od)

        def act_fox(E):
            act_qkv(E)
            E.eng.wait_ge(s_mm, E.next(s_mm))
            nc.scalar.activation(fx[0:H64, :], ps[0:H64, 0, 0:S], ACT.Identity, bias=bfc[0:H64, :]).then_inc(s_ev, E.adds(s_ev))
            act_hi(E)
            E.eng.wait_ge(s_mix, E.next(s_mix))
            nc.scalar.activation(fn[0:H64, :], fn[0:H64, :], ACT.Exp).then_inc(s_a, E.adds(s_a))
            E.eng.wait_ge(E.last, E.sofar(E.last))
            nc.scalar.activation(fn[0:H64, :], fn[0:H64, :], ACT.Ln, bias=1.0).then_inc(s_mixa, E.adds(s_mixa))
            act_attention(E, 8)
            act_turn(E)

        def dve_fox(E):
            dve_qkv(E)
            dve_lo(E, 1)
            h = slice(0, H64)
            nc.vector.tensor_scalar(fm[h, :], fx[h, :], 0.0, None, ALU.min).then_inc(s_d, E.adds(s_d))
            nc.vector.scalar_tensor_tensor(out=fn[h, :], in0=fx[h, :], scalar=-1.0, in1=fx[h, :], op0=ALU.mult, op1=ALU.min).then_inc(s_mix, E.adds(s_mix))
            E.eng.wait_ge(s_mixa, E.next(s_mixa))
            nc.vector.tensor_tensor(fm[h, :], fm[h, :], fn[h, :], ALU.subtract).then_inc(s_d, E.adds(s_d))
            E.eng.wait_ge(E.last, E.sofar(E.last))
            nc.vector.memset(fc[:, :], 0.0).then_inc(s_d, E.adds(s_d))
            E.eng.wait_ge(E.last, E.sofar(E.last))
            nc.vector.tensor_tensor_scan(fc[h, :], onesw[h, :], fm[h, :], 0.0, ALU.mult, ALU.add).then_inc(s_d, E.adds(s_d))
            E.eng.wait_ge(E.last, E.sofar(E.last))
            nc.vector.tensor_scalar(fc[h, :], fc[h, :], -8.0, None, ALU.mult).then_inc(s_d, E.adds(s_d))
            E.eng.wait_ge(E.last, E.sofar(E.last))
            E.eng.wait_ge(s_scr, E.next(s_scr, 32))
            nc.vector.tensor_tensor(fcm[:, :, :], fc[:, :].unsqueeze(1).to_broadcast([P, H64, S]),
                                           ident[:, 0:H64].unsqueeze(2).to_broadcast([P, H64, S]), ALU.mult).then_inc(s_d, E.adds(s_d))
            dve_attention(E, 8, "fox", 0.125, table=False)
            dve_turn(E)

        def pool_bias_again(E):
            E.eng.wait_ge(s_x, 4 * 2 + 1)
            E.eng.dma_start(bias.rearrange("p h k -> p (h k)"), bias_kept).then_inc(s_rows, 16)

        qn = lambda c: qk[:, c, 0, :]
        vsel = view(ar, 4096, [P, NT, DC, 64])
        vwin = view(ar, 5120, [P, NT, DC, 64])
        kwin = view(ar, 13056, [P, 4, S])
        kk = [view(ar, 10240, [P, 4, 16, 16]), view(ar, 11264, [P, 4, 16, 16])]
        yf = yT[:, :, :].rearrange("p c t -> p (c t)")
        gat = yf[:, 0:960].rearrange("p (a n) -> p a n", a=16)
        gu, gz, ge = (yf[:, 960 + 240 * k:1200 + 240 * k].rearrange("p (v m n) -> p v m n", v=2, m=2) for k in range(3))
        fwd = ar_fwd = view(ar, 12544, [P, 480])
        gah, gal = view(ar_r, 0, [P, 16, 60]), view(ar_r, 1024, [P, 16, 60])
        kcT = view(sm, 160, [P, 60])
        vbd = view(ar, 10240, [P, 4, 4, 64])
        pc = view(ar, 11264, [P, 32, 32])
        pcT = view(ar, 12288, [P, 4, P])
        cmx, csm = view(ar, 12800, [P, 32]), view(ar, 12832, [P, 32])

        def sp_nsa(E):
            w = d["nsa_w_in"][0]
            E.eng.wait_ge(s_x, 1)
            E.eng.dma_start(fwd[0:NB + 1, :], d["c_fwd"][:, 0:480]).then_inc(s_fwd, 16)
            for b in range(3):
                sp_cols(E, w[:, 512 * b:512 * b + 512], 512, 8)
            for a in (1536, 1792):
                slot = E.slot()
                v = wv(raw, slot, 512, 8)
                src = w.rearrange("(k p) n -> p k n", p=P)
                load(E, slot, [(v[:, :, 256 * n:256 * n + 256], src[:, :, a + 512 * n:a + 512 * n + 256]) for n in range(2)])
            sp_cols(E, w[:, 2560:2608], 48, 8)
            for n in range(2):
                sp_cols(E, d["nsa_cmp_w1"][0, n], 256, 16)
            sp_out(E, d["nsa_w_out"][0])

        def pe_nsa(E):
            E.eng.wait_ge(s_op, E.next(s_op, 8))
            pe_free(E)
            for b in range(2):
                pe_T(E, 512, 8, ah, al, 2 * b)
                E.skip(s_ev, 2)
            for b, f in enumerate((pe_T, pe_T, pe_rows, pe_rows)):
                if E.seen(s_ev, 2):
                    E.eng.wait_ge(s_ev, E.sofar(s_ev, 2))
                f(E, 48 if b == 3 else 512, 8, ah, al, 2 * (b % 2))
                E.skip(s_ev, 2)
            for n in range(2):
                E.eng.wait_ge(s_op, E.next(s_op))
                if E.seen(s_ev):
                    E.eng.wait_ge(s_ev, E.sofar(s_ev))
                pe_T(E, 256, 16, gah, gal, 2 * n, 60)
                E.skip(s_ev)
            E.skip(s_mix)
            E.eng.wait_ge(s_mix, E.next(s_mix))
            E.eng.wait_ge(s_fwd, E.next(s_fwd, 16))
            for k in range(2):
                for half in range(2):
                    nc.tensor.matmul(ps[64 * half:64 * half + 64, 4, 0:60], cw2k[:, k, :], ge[:, 0, k, :], start=k == 0, stop=k == 1, skip_group_check=True)
            for g in range(4):
                for k in range(2):
                    nc.tensor.matmul(ps[0:NCMP, 5, 64 * g:64 * g + 64], ge[:, 1, k, g::4], cw2v[:, k, :], start=k == 0, stop=k == 1)
            for q in range(NT):
                for n in range(NCMP):
                    a = 255 + P * q - 31 - 16 * n
                    last = nc.tensor.matmul(ps[:, 6 + q, 16 * n:16 * n + 16], fwd[0:NB + 1, a:a + P], rel[0:NB + 1, :], start=True, stop=True)
            last.then_inc(s_mixp, E.adds(s_mixp))
            E.eng.wait_ge(s_mixa, E.next(s_mixa, 2))
            for q in range(NT):
                for h in range(H64):
                    lo, a = slice(64 * (h % 2), 64 * (h % 2) + 64), (q * 8 + h // 2) * 16
                    last = nc.tensor.matmul(ps[:, h % 2, a:a + NCMP], qn(h // 2)[lo, q * P:(q + 1) * P], kcT[lo, h // 4::4], start=True, stop=True)
            last.then_inc(s_mixp, E.adds(s_mixp))
            E.skip(s_mix, 2)
            E.skip(s_mixa)
            for q in range(NT):
                if q:
                    E.eng.wait_ge(s_mix, E.next(s_mix))
                else:
                    if E.seen(s_mix):
                        E.eng.wait_ge(s_mix, E.sofar(s_mix))
                for g in range(4):
                    last = nc.tensor.transpose(ps[:, 5, g * P:(g + 1) * P], pc[:, q * 16 + 4 * g:q * 16 + 4 * g + 4, :].rearrange("p h n -> p (h n)"), ident[:, :])
                last.then_inc(s_mixp, E.adds(s_mixp))
                E.eng.wait_ge(s_mixa, E.next(s_mixa))
                for g in range(4):
                    last = nc.tensor.matmul(ps[:, 6 + g // 2, (g % 2) * S:(g % 2) * S + S], pcT[:, g, :], vbd[:, g, :, :].rearrange("p h n -> p (h n)"), start=True, stop=True)
                last.then_inc(s_mixp, E.adds(s_mixp))
            E.skip(s_mix)
            for v in (vsel, vwin):
                pe_attention(E, 8, v=lambda t, j, c: v[:, t, j, :])
            pe_turn(E, ready=s_od)

        def act_nsa(E):
            act_copy(E, [qk[:, 0:2, 0, :], qk[:, 2:4, 0, :]], 0)
            act_copy(E, [qk[:, 4:6, 0, :], qk[:, 6:8, 0, :]], 2)
            for v in range(2):
                E.eng.wait_ge(s_mm, E.next(s_mm))
                dst = kk[v].rearrange("p g a b -> p g (a b)")
                for g in range(4):
                    src = ps[64 * (g % 2):64 * (g % 2) + 64, v, S * (g // 2):S * (g // 2) + S]
                    nc.scalar.activation(dst[0:64, g, :], src, ACT.Copy)
                    last = nc.scalar.activation(dst[64:P, g, 0:S - 1], src[:, 1:S], ACT.Copy)
                last.then_inc(s_ev, E.adds(s_ev))
            act_hi(E)
            for v in range(2):
                E.eng.wait_ge(s_mm, E.next(s_mm))
                for g in range(4):
                    src = ps[64 * (g % 2):64 * (g % 2) + 64, 2 + v, S * (g // 2):S * (g // 2) + S]
                    for half in (slice(0, 64), slice(64, P)):
                        if v == 0:
                            for r in range(2):
                                last = nc.scalar.activation(qk[half, 2 * g + r, 1, :], src, ACT.Copy)
                        else:
                            last = nc.scalar.activation(kwin[half, g, :], src, ACT.Copy)
                last.then_inc(s_ev, E.adds(s_ev))
            act_hi(E)
            for q in range(NT):
                E.eng.wait_ge(s_mm, E.next(s_mm))
                for v, dst in enumerate((vsel, vwin)):
                    for r in range(2):
                        last = nc.scalar.activation(dst[:, q].rearrange("p (g r) n -> p g r n", r=2)[:, :, r, :],
                                                    ps[:, q, S * v:S * v + S].rearrange("p (g n) -> p g n", g=4), ACT.Copy)
                last.then_inc(s_ev, E.adds(s_ev))
            act_hi(E)
            for q in range(NT):
                E.eng.wait_ge(s_mm, E.next(s_mm))
                nc.scalar.activation(gates[:, q, :], ps[:, 2 + q, 0:48], ACT.Exp, scale=-1.0).then_inc(s_ev, E.adds(s_ev))
            act_hi(E)
            for n in range(2):
                E.eng.wait_ge(s_u, E.next(s_u))
                nc.scalar.activation(gah[:, :, :], gat, ACT.Copy).then_inc(s_uh, E.adds(s_uh))
                E.skip(s_op)
                E.eng.wait_ge(s_mm, E.next(s_mm))
                nc.scalar.activation(gu[:, n], bank(2 * n)[:, :, 0:60], ACT.Copy).then_inc(s_ev, E.adds(s_ev))
                act_hi(E)
            E.eng.wait_ge(s_mix, E.next(s_mix))
            nc.scalar.activation(ge, gz, ACT.Exp, scale=-2.0 * math.sqrt(2.0 / math.pi)).then_inc(s_mixa, E.adds(s_mixa))
            E.skip(s_mix)
            E.eng.wait_ge(s_mixp, E.next(s_mixp))
            nc.scalar.activation(kcT, ps[:, 4, 0:60], ACT.Copy)
            for q in range(NT):
                last = nc.scalar.activation(pc[:, 16 * q:16 * q + 16, 0:NCMP].rearrange("p h n -> p n h"),
                                            ps[:, 6 + q, 0:240].rearrange("p (n h) -> p n h", n=NCMP), ACT.Copy)
            last.then_inc(s_mixa, E.adds(s_mixa))
            E.skip(s_mixp)
            E.eng.wait_ge(s_mix, E.next(s_mix))
            nc.scalar.activation(pc[:, :, 0:NCMP], pc[:, :, 0:NCMP], ACT.Exp).then_inc(s_mixa, E.adds(s_mixa))
            E.skip(s_mix)
            for q in range(NT):
                E.eng.wait_ge(s_mixp, E.next(s_mixp))
                nc.scalar.activation(pcT[:, :, :], ps[:, 5, :].rearrange("p (g n) -> p g n", g=4), ACT.Copy).then_inc(s_mixa, E.adds(s_mixa))
                E.skip(s_mixp)
                E.skip(s_mix)
            for branch in range(2):
                act_attention(E, 8)
            act_turn(E)

        def dve_nsa(E):
            for mm in (2, 2, 2, 2, 2, 2):
                dve_lo(E, mm)
            nc.vector.tensor_scalar(gates[:, :, :], gates[:, :, :], 1.0, None, ALU.add).then_inc(s_d, E.adds(s_d))
            E.eng.wait_ge(E.last, E.sofar(E.last))
            nc.vector.reciprocal(gates[:, :, :], gates[:, :, :]).then_inc(s_d, E.adds(s_d))
            for v in range(2):
                for a in range(16):
                    src = kk[v][:, :, a // 8:a // 8 + NCMP, 2 * (a % 8)].rearrange("p g n -> p n g")
                    col = G2["nsa_cmp_pe"] + 16 * v + a
                    last = nc.vector.tensor_scalar(gat[:, a, :].rearrange("p (n g) -> p n g", g=4), src, g2[:, col:col + 1], None, ALU.add)
                last.then_inc(s_u, E.adds(s_u))
                E.eng.wait_ge(s_uh, E.next(s_uh))
                E.eng.wait_ge(s_u, E.sofar(s_u))
                nc.vector.tensor_tensor(gal[:, :, :], gat, gah[:, :, :].bitcast(F32), ALU.subtract).then_inc(s_op, E.adds(s_op))
                dve_lo(E, 1)
                E.eng.wait_ge(s_op, E.sofar(s_op))
            nc.vector.tensor_tensor(gz, gu, gu, ALU.mult).then_inc(s_d, E.adds(s_d))
            E.eng.wait_ge(E.last, E.sofar(E.last))
            nc.vector.tensor_scalar(gz, gz, 0.044715, 1.0, ALU.mult, ALU.add).then_inc(s_d, E.adds(s_d))
            E.eng.wait_ge(E.last, E.sofar(E.last))
            nc.vector.memset(vbd[:, :, :, :], 0.0)
            nc.vector.memset(pc[:, :, :], 0.0)
            nc.vector.tensor_tensor(gz, gz, gu, ALU.mult).then_inc(s_mix, E.adds(s_mix))
            E.eng.wait_ge(s_mixa, E.next(s_mixa))
            nc.vector.tensor_scalar(ge, ge, 1.0, None, ALU.add).then_inc(s_d, E.adds(s_d))
            E.eng.wait_ge(E.last, E.sofar(E.last))
            nc.vector.reciprocal(ge, ge).then_inc(s_d, E.adds(s_d))
            E.eng.wait_ge(E.last, E.sofar(E.last))
            nc.vector.tensor_tensor(ge, ge, gu, ALU.mult).then_inc(s_mix, E.adds(s_mix))
            E.eng.wait_ge(s_mixp, E.next(s_mixp))
            for h in range(4):
                last = nc.vector.tensor_copy(vbd[32 * h:32 * h + NCMP, :, h, :], ps[0:NCMP, 5, 0:S].rearrange("p (g n) -> p g n", g=4))
            last.then_inc(s_d, E.adds(s_d))
            E.eng.wait_ge(s_mixa, E.next(s_mixa))
            E.eng.wait_ge(s_mixp, E.next(s_mixp))
            p15 = pc[:, :, 0:NCMP]
            for c in range(2):
                half = pc.rearrange("p (a c) n -> p a c n", c=2)[:, :, c, 0:NCMP]
                last = nc.vector.scalar_tensor_tensor(out=half, in0=ps[:, c, 0:S].rearrange("p (h n) -> p h n", n=16)[:, :, 0:NCMP], scalar=0.125, in1=half,
                                                      op0=ALU.mult, op1=ALU.add)
            last.then_inc(s_d, E.adds(s_d))
            E.eng.wait_ge(E.last, E.sofar(E.last))
            nc.vector.tensor_reduce(cmx[:, :], p15, AX.X, ALU.max).then_inc(s_d, E.adds(s_d))
            E.eng.wait_ge(E.last, E.sofar(E.last))
            nc.vector.tensor_tensor(p15, p15, cmx[:, :].unsqueeze(2).to_broadcast([P, 32, NCMP]), ALU.subtract).then_inc(s_mix, E.adds(s_mix))
            E.eng.wait_ge(s_mixa, E.next(s_mixa))
            nc.vector.tensor_reduce(csm[:, :], p15, AX.X, ALU.add).then_inc(s_d, E.adds(s_d))
            E.eng.wait_ge(E.last, E.sofar(E.last))
            nc.vector.reciprocal(csm[:, :], csm[:, :]).then_inc(s_d, E.adds(s_d))
            E.eng.wait_ge(E.last, E.sofar(E.last))
            nc.vector.tensor_tensor(csm.rearrange("p (q h) -> p q h", q=NT), csm.rearrange("p (q h) -> p q h", q=NT),
                                           gates.rearrange("p q (h b) -> p q h b", b=3)[:, :, :, 0], ALU.mult).then_inc(s_d, E.adds(s_d))
            for q in range(NT):
                last = nc.vector.tensor_tensor(pc[:, 16 * q:16 * q + 16, 0:NCMP], pc[:, 16 * q:16 * q + 16, 0:NCMP],
                                               cmaskv[:, q, 0:NCMP].unsqueeze(1).to_broadcast([P, 16, NCMP]), ALU.mult)
            last.then_inc(s_d, E.adds(s_d))
            E.eng.wait_ge(E.last, E.sofar(E.last))
            nc.vector.tensor_tensor(p15, p15, csm[:, :].unsqueeze(2).to_broadcast([P, 32, NCMP]), ALU.mult).then_inc(s_mix, E.adds(s_mix))
            for q in range(NT):
                E.skip(s_mixa)
                E.skip(s_mixp)
                E.eng.wait_ge(s_mixp, E.next(s_mixp))
                nc.vector.tensor_copy(orow[:, q, :].rearrange("p (b n) -> p b n", b=2), ps[:, 6:8, :]).then_inc(s_mix, E.adds(s_mix))
            dve_attention(E, 8, "nsa", 0.125, branch=1)
            E.eng.wait_ge(E.last, E.sofar(E.last))
            for r in range(2):
                last = nc.vector.tensor_copy(qk.rearrange("p (g r) a t -> p g r a t", r=2)[:, :, r, 1, :], kwin[:, :, :])
            last.then_inc(s_d, E.adds(s_d))
            E.eng.wait_ge(E.last, E.sofar(E.last))
            dve_attention(E, 8, "nsa", 0.125, branch=2)
            dve_turn(E)

        def pe_glu(E):
            E.eng.wait_ge(s_op, E.next(s_op, 8))
            E.skip(s_evd)
            pe_free(E)
            n = F_GLU // 256
            first = [True]

            def h(b):
                if not first[0]:
                    E.eng.wait_ge(s_op, E.next(s_op))
                first[0] = False
                pe_T(E, 512, 8, ah, al, 0)

            def y(b):
                if E.seen(s_evd):
                    E.eng.wait_ge(s_evd, E.sofar(s_evd))
                pe_T(E, 1024, 2, hh[:, b], hl[:, b], 4)
                E.skip(s_evd, 4)
            h(0)
            turns = (n - 3) // 2
            with E.loop(turns, {s_lo: 4, s_mm: 12, s_evd: 8, s_op: 2}):
                for u in range(2):
                    h(1 - u)
                    y(u)
            for f in (n - 3, n - 2):
                h((f + 1) % 2)
                y(f % 2)
            E.eng.wait_ge(s_op, E.next(s_op))
            y((n - 1) % 2)

        def around(E, h, y, per):
            n = F_GLU // 256
            h(0)
            with E.loop((n - 3) // 2, per):
                for u in range(2):
                    h(1 - u)
                    y(u)
            for f in (n - 3, n - 2):
                h((f + 1) % 2)
                y(f % 2)
            y((n - 1) % 2)

        def act_glu(E):
            def h(b):
                if E.seen(s_op):
                    E.eng.wait_ge(s_op, E.sofar(s_op))
                E.eng.wait_ge(s_mm, E.next(s_mm))
                nc.scalar.activation(rr[:, 0], bank(0), ACT.Exp, scale=-1.0).then_inc(s_uh, E.adds(s_uh))
                E.eng.wait_ge(s_mm, E.next(s_mm))
                E.eng.wait_ge(s_u, E.next(s_u))
                nc.scalar.activation(hh[:, b, 0:2, :], rr[:, 1], ACT.Copy).then_inc(s_uh, E.adds(s_uh))
                E.skip(s_op)
                act_hi(E)
            around(E, h, lambda b: act_y(E), {s_mm: 12, s_uh: 4, s_u: 2, s_op: 2, s_raw[0]: 64, s_raw[1]: 64, s_hi: 4})

        def dve_glu(E):
            def h(b):
                E.eng.wait_ge(s_uh, E.next(s_uh))
                nc.vector.tensor_scalar(rr[:, 0], rr[:, 0], 1.0, None, ALU.add).then_inc(s_d, E.adds(s_d))
                E.eng.wait_ge(E.last, E.sofar(E.last))
                nc.vector.reciprocal(rr[:, 0], rr[:, 0]).then_inc(s_d, E.adds(s_d))
                E.eng.wait_ge(s_mm, E.next(s_mm, 2))
                E.eng.wait_ge(s_d, E.sofar(s_d))
                nc.vector.tensor_tensor(rr[:, 0], rr[:, 0], bank(0), ALU.mult).then_inc(s_d, E.adds(s_d))
                E.eng.wait_ge(E.last, E.sofar(E.last))
                nc.vector.tensor_tensor(rr[:, 1], rr[:, 0], bank(1), ALU.mult).then_inc(s_u, E.adds(s_u))
                E.eng.wait_ge(s_uh, E.next(s_uh))
                E.eng.wait_ge(s_u, E.sofar(s_u))
                nc.vector.tensor_tensor(hl[:, b, 0:2, :], rr[:, 1], hh[:, b, 0:2, :].bitcast(F32), ALU.subtract).then_inc(s_op, E.adds(s_op))
                dve_lo(E)
            around(E, h, lambda b: dve_y(E), {s_uh: 4, s_d: 6, s_u: 2, s_op: 2, s_mm: 12, s_evd: 8, s_hi: 4, s_lo: 4})

        def pe_ffn(E):
            pe_stats(E, DC)
            pe_glu(E)

        def act_ffn(E):
            act_stats(E, xT, DC)
            act_operand(E, xT, DC, ah)
            act_glu(E)

        def dve_ffn(E, name, layer):
            dve_stats(E, DC)
            dve_operand(E, xT, gg(name, layer, 8), DC, ah, al)
            nc.vector.memset(yT[:, :, :], 0.0).then_inc(s_evd, E.adds(s_evd))
            dve_glu(E)
            E.eng.wait_ge(s_evd, E.sofar(s_evd))
            nc.vector.scalar_tensor_tensor(out=xT[:, :, :], in0=yT[:, :, :], scalar=0.5, in1=xT[:, :, :], op0=ALU.mult, op1=ALU.add).then_inc(s_x, E.adds(s_x))
            E.eng.wait_ge(s_x, E.sofar(s_x))

        xs = view(ar, 0, [P, NT, 4, 512])
        bct = view(ar, 4096, [P, 2, 4, S])
        cin = view(ar, 6144, [P, 2, 260])
        cout = view(ar, 6664, [P, 2, S])
        cex = view(ar, 7176, [P, 2, S])
        bcs = view(ar, 6144, [P, 2, S])
        brs = view(ar, 6656, [P, P])
        cbm = view(ar, 6784, [P, 2, P])
        stt = view(ar, 7040, [P, 512])
        am = view(ar, 7688, [P, 2, 8, P])
        ee = view(ar, 9736, [P, 2, 8, P])
        xdt = view(ar, 11784, [P, 2, 8, 64])
        xdw = view(ar, 12808, [P, 8, 64])
        brow2 = view(ar, 13320, [P, 4, P])
        rws = view(ar, 13832, [P, 6, 32])
        upper = view(ar, 14024, [P, P])
        crow = view(ar, 14152, [P, P])
        cw = view(sm, 16, [P, 120])
        dtb, alog = view(sm, 136, [P, 1]), view(sm, 137, [P, 1])
        dsk = view(sm, 138, [P, 32])
        qng, kng = view(sm, 172, [P, 192]), view(sm, 364, [P, 192])
        s16 = view(sm, 556, [P, 16])
        posi = sb("posi", [P, NT], I32)
        dx, dm, dn, acT, wsT, eaT = (yf[:, 256 * k:256 * k + 256] for k in range(6))
        zt = view(ar, 6144, [P, 4, 512])
        zsq = view(ar, 6144, [P, NT, 2048])
        bh, bl = view(ar_r, 0, [P, DC, S]), view(ar_r, 2048, [P, DC, S])
        mg = view(ar, 8192, [P, DC, S])
        ge8 = view(ar, 10240, [P, DC, S])

        def sp_second(E, layer):
            w = d["w_in_2"][layer]
            sp_glu(E, d["ffn1_w13_2"][layer], d["ffn1_w2_2"][layer])
            for b in range(2):
                sp_cols(E, w[:, O_XBC + 512 * b:O_XBC + 512 * b + 512], 512, 8)
            E.eng.wait_ge(s_x, 4 * DEPTH + 4 * layer + 1)
            sp_small(E, layer)
            xw = w[:, O_XBC:O_XBC + 3072].rearrange("k (a n) -> a k n", n=512)
            for b in range(2, 6):
                sp_cols(E, xw[b], 512, 8)
            sp_cols(E, w[:, O_DT:O_DT + 32], 32, 8)
            zw = w[:, O_Z:O_Z + 2048].rearrange("k (a n) -> a k n", n=512)
            with E.loop(2, {s_lo: 2}) as i:
                for b in range(2):
                    sp_cols(E, zw[2 * i + b], 512, 8)
            for h in range(2):
                sp_out(E, d["w_ssd_out_2"][layer][1024 * h:1024 * h + 1024, :])
            sp_out(E, w[:, O_G:O_G + D])
            sp_cols(E, w[:, O_CQ:O_CQ + 512], 512, 8)
            sp_cols(E, w[:, O_CKV:O_CKV + 320], 320, 8)
            for b in range(2):
                sp_cols(E, d["w_ukv_2"][layer][:, 1024 * b:1024 * b + 1024], 1024, 2)
            for b in range(3):
                sp_cols(E, d["w_uq_2"][layer][:, 512 * b:512 * b + 512], 512, 4)
            sp_out(E, d["w_mla_out_2"][layer])
            sp_out(E, w[:, O_G + D:O_G + 2 * D])
            sp_out(E, d["w_o_2"][layer])
            sp_glu(E, d["ffn2_w13_2"][layer], d["ffn2_w2_2"][layer])

        n_small = 16 * 10

        def sp_small(E, layer):
            e = E.eng
            for dst, src in ((crow[0:96, :], d["conv_w_2"][layer].rearrange("k (c n) -> (k c) n", n=P)),
                             (crow[96:120, :], d["conv_b_2"][layer].rearrange("(c n) -> c n", n=P)),
                             (dtb[0:32, :], d["dt_bias_2"][layer].rearrange("(h a) -> h a", a=1)),
                             (alog[0:32, :], d["a_log_2"][layer].rearrange("(h a) -> h a", a=1)),
                             (dsk[:, :], d["d_skip_2"][layer].partition_broadcast(P)),
                             (qng[:, :], d["q_norm_2"][layer].partition_broadcast(P)),
                             (kng[:, :], d["k_norm_2"][layer].partition_broadcast(P)),
                             (upper[:, :], d["c_upper"]),
                             (posi[:, 0:1], d["positions_2"][0, 0:P].rearrange("(p a) -> p a", a=1)),
                             (posi[:, 1:2], d["positions_2"][0, P:S].rearrange("(p a) -> p a", a=1))):
                e.dma_start(dst, src).then_inc(s_small, 16)

        def pe_ssd(E):
            E.eng.wait_ge(s_small, E.next(s_small, n_small))
            E.eng.wait_ge(s_op, E.next(s_op, 8))
            pe_free(E)
            nc.tensor.transpose(ps[:, 6, 0:120], crow[0:120, :], ident[0:120, 0:120]).then_inc(s_tp, E.adds(s_tp))
            for b in range(6):
                if E.seen(s_cin):
                    E.eng.wait_ge(s_cin, E.sofar(s_cin))
                pe_T(E, 512, 8, ah, al, 2 * (b % 2))
                for n in range(2):
                    if b < 4:
                        E.eng.wait_ge(s_mix, E.next(s_mix))
                        for q in range(NT):
                            for c in range(2):
                                last = nc.tensor.transpose(ps[:, 4 + n, q * S + c * P:q * S + (c + 1) * P], cout[:, c, q * P:(q + 1) * P], ident[:, :])
                        last.then_inc(s_tp, E.adds(s_tp))
                        E.skip(s_cin, 2)
                    else:
                        E.skip(s_cin)
            if E.seen(s_cin):
                E.eng.wait_ge(s_cin, E.sofar(s_cin))
            pe_narrow(E, 32, 8, ah, al, 0)
            E.skip(s_ev)
            E.eng.wait_ge(s_mix, E.next(s_mix))
            for g in range(4):
                last = nc.tensor.transpose(ps[:, 6, g * P:(g + 1) * P], bct[:, 0, g, 0:P], ident[:, :])
            i32 = ident[0:32, 0:32]
            for n, src in enumerate((dn[0:32, 0:P], dn[0:32, P:S], acT[0:32, 0:P], acT[0:32, P:S], wsT[0:32, 0:P], eaT[0:32, 0:P])):
                last = nc.tensor.transpose(ps[:, 5, 32 * n:32 * n + 32], src, i32)
            last.then_inc(s_tp, E.adds(s_tp))
            with E.loop(4, {s_stg: 1, s_sc: 1, s_mix: 2, s_dec: 2, s_e: 2, s_scd: 2, s_o: 2, s_mixp: 1, s_pc: 1}):
                E.skip(s_e, 2)
                E.eng.wait_ge(s_stg, E.next(s_stg))
                for q in range(NT):
                    t = slice(q * P, (q + 1) * P)
                    last = nc.tensor.matmul(ps[:, 0, t], bcs[:, 0, t], bcs[:, 1, t], start=True, stop=True)
                last.then_inc(s_sc, E.adds(s_sc))
                for q in range(NT):
                    E.eng.wait_ge(s_mix, E.next(s_mix))
                    for n in range(2):
                        last = nc.tensor.matmul(ps[:, 2 + 2 * q + n, :], ones[0:32, :], am[0:32, q, 4 * n:4 * n + 4, :].rearrange("p h t -> p (h t)"), start=True, stop=True)
                    last.then_inc(s_dec, E.adds(s_dec))
                for q in range(NT):
                    E.eng.wait_ge(s_scd, E.next(s_scd))
                    for h in range(8):
                        last = nc.tensor.matmul(ps[:, 6 + q, 64 * h:64 * h + 64], ee[:, q, h, :], xdt[:, q, h, :], start=True, stop=True)
                    if q == 0:
                        last.then_inc(s_o, E.adds(s_o))
                        nc.tensor.matmul(ps[:, 1, :], brs[:, :], xdw.rearrange("p h n -> p (h n)"), start=True, stop=True).then_inc(s_mixp, E.adds(s_mixp))
                    else:
                        E.eng.wait_ge(s_pc, E.next(s_pc))
                        nc.tensor.matmul(ps[:, 2, :], bcs[:, 1, P:S], stt[:, :], start=True, stop=True).then_inc(s_o, E.adds(s_o))
            E.skip(s_evd)
            pe_free(E)
            with E.loop(2, {s_lo: 2, s_mm: 4, s_evd: 4}):
                for b in range(2):
                    if E.seen(s_evd, 2):
                        E.eng.wait_ge(s_evd, E.sofar(s_evd, 2))
                    pe_rows(E, 512, 8, ah, al, 2 * b)
                    E.skip(s_evd, 2)
            E.skip(s_mix, 2)
            for h in range(2):
                if h == 0:
                    E.eng.wait_ge(s_mix, E.next(s_mix))
                if E.seen(s_evd):
                    E.eng.wait_ge(s_evd, E.sofar(s_evd))
                if E.seen(s_ev):
                    E.eng.wait_ge(s_ev, E.sofar(s_ev))
                pe_turn(E, xs[:, :, 2 * h:2 * h + 2, :].rearrange("p q a n -> p q (a n)"), ready=s_mix)
                E.eng.wait_ge(s_op, E.next(s_op, 4))
                pe_T(E, 512, 8, bh, bl, 0)
                pe_T(E, 512, 8, bh, bl, 2)
                if h:
                    E.skip(s_evd, 4)
                else:
                    E.skip(s_ev, 4)
            if E.seen(s_evd):
                E.eng.wait_ge(s_evd, E.sofar(s_evd))
            pe_T(E, 512, 8, ah, al, 0)
            pe_T(E, 512, 8, ah, al, 2)
            E.skip(s_ev, 4)

        def act_ssd(E):
            E.eng.wait_ge(s_tp, E.next(s_tp))
            nc.scalar.activation(cw[:, :], ps[:, 6, 0:120], ACT.Copy).then_inc(s_mixa, E.adds(s_mixa))
            for b in range(6):
                for n in range(2):
                    E.eng.wait_ge(s_mm, E.next(s_mm))
                    if E.seen(s_u):
                        E.eng.wait_ge(s_u, E.sofar(s_u))
                    nc.scalar.activation(cin[:, :, 3:259], bank(2 * (b % 2) + n), ACT.Copy).then_inc(s_cin, E.adds(s_cin))
                    E.eng.wait_ge(s_u, E.next(s_u))
                    nc.scalar.activation(cex[:, :, :], cout[:, :, :], ACT.Exp, scale=-1.0).then_inc(s_uh, E.adds(s_uh))
                    if b < 4:
                        E.skip(s_mix)
                        E.eng.wait_ge(s_tp, E.next(s_tp))
                        c = 2 * b + n
                        nc.scalar.activation(xs.rearrange("p q g n -> p q (g n)")[:, :, S * c:S * c + S], ps[:, 4 + n, :].rearrange("p (q n) -> p q n", q=NT), ACT.Copy).then_inc(s_cin, E.adds(s_cin))
                act_hi(E)
            E.eng.wait_ge(s_mm, E.next(s_mm))
            nc.scalar.activation(dx[0:32, :], ps[0:32, 0, 0:S], ACT.Identity, bias=dtb[0:32, :]).then_inc(s_ev, E.adds(s_ev))
            act_hi(E)
            nc.scalar.activation(alog[0:32, :], alog[0:32, :], ACT.Exp).then_inc(s_a, E.adds(s_a))
            E.eng.wait_ge(s_u, E.next(s_u))
            nc.scalar.activation(dn[0:32, :], dn[0:32, :], ACT.Exp).then_inc(s_a, E.adds(s_a))
            E.eng.wait_ge(E.last, E.sofar(E.last))
            nc.scalar.activation(dn[0:32, :], dn[0:32, :], ACT.Ln, bias=1.0).then_inc(s_uh, E.adds(s_uh))
            E.eng.wait_ge(s_u, E.next(s_u))
            nc.scalar.activation(wsT[0:32, 0:P], acT[0:32, 0:P], ACT.Exp, scale=-1.0, bias=acT[0:32, P - 1:P])
            nc.scalar.activation(eaT[0:32, 0:P], acT[0:32, P:S], ACT.Exp).then_inc(s_uh, E.adds(s_uh))
            E.skip(s_mix)
            E.eng.wait_ge(s_tp, E.next(s_tp))
            nc.scalar.activation(brow2[:, :, :], ps[:, 6, :].rearrange("p (g n) -> p g n", g=4), ACT.Copy)
            nc.scalar.activation(rws[:, :, :], ps[:, 5, 0:192].rearrange("p (a h) -> p a h", a=6), ACT.Copy).then_inc(s_uh, E.adds(s_uh))
            with E.loop(4, {s_mx: 2, s_e: 2, s_mixp: 1, s_pc: 1, s_mix: 2, s_o: 2}):
                E.skip(s_o, 2)
                for q in range(NT):
                    E.eng.wait_ge(s_mx, E.next(s_mx))
                    nc.scalar.activation(ee[:, q], ee[:, q], ACT.Exp).then_inc(s_e, E.adds(s_e))
                E.eng.wait_ge(s_mixp, E.next(s_mixp))
                nc.scalar.activation(stt[:, :], ps[:, 1, :], ACT.Copy).then_inc(s_pc, E.adds(s_pc))
                E.skip(s_mix, 2)
            with E.loop(2, {s_mm: 4, s_u: 4, s_uh: 4, s_raw[0]: 32, s_raw[1]: 32, s_hi: 2}):
                for b in range(2):
                    if E.seen(s_u):
                        E.eng.wait_ge(s_u, E.sofar(s_u))
                    for q in range(NT):
                        E.eng.wait_ge(s_mm, E.next(s_mm))
                        nc.scalar.activation(zt[:, 2 * b + q, :], ps[:, 2 * b + q, :], ACT.Exp, scale=-1.0).then_inc(s_uh, E.adds(s_uh))
                    E.skip(s_u, 2)
                    act_hi(E)
            E.eng.wait_ge(s_mix, E.next(s_mix))
            for q in range(NT):
                last = nc.scalar.activation(zsq[:, q], xs[:, q].rearrange("p g n -> p (g n)"), ACT.Square, accum_out=s16[:, q:q + 1])
            last.then_inc(s_mixa, E.adds(s_mixa))
            E.eng.wait_ge(s_mix, E.next(s_mix))
            nc.scalar.activation(s16[:, 0:2], s16[:, 0:2], ACT.Sqrt).then_inc(s_mixa, E.adds(s_mixa))
            E.skip(s_mix)
            for h in range(2):
                act_turn(E, lambda c: gg("ssd_norm_2", layer2[0], 16)(8 * h + c), bh)
                if h == 0:
                    act_out(E)
                else:
                    for b in range(2):
                        E.eng.wait_ge(s_mm, E.next(s_mm, 2))
                        act_hi(E)
            for b in range(2):
                for n in range(2):
                    E.eng.wait_ge(s_mm, E.next(s_mm))
                    nc.scalar.activation(ge8[:, 4 * b + 2 * n:4 * b + 2 * n + 2, :], bank(2 * b + n), ACT.Exp, scale=-1.0).then_inc(s_ev, E.adds(s_ev))
                act_hi(E)
        layer2 = [0]

        def dve_ssd(E):
            E.eng.wait_ge(s_small, E.next(s_small, n_small))
            nc.vector.memset(cin[:, :, 0:3], 0.0).then_inc(s_d, E.adds(s_d))
            E.eng.wait_ge(E.last, E.sofar(E.last))
            E.eng.wait_ge(s_mixa, E.next(s_mixa))
            for b in range(6):
                for n in range(2):
                    E.eng.wait_ge(s_cin, E.next(s_cin))
                    for c in range(2):
                        k = 4 * b + 2 * n + c
                        nc.vector.tensor_scalar(cout[:, c, :], cin[:, c, 0:S], cw[:, k:k + 1], cw[:, 96 + k:97 + k], ALU.mult, ALU.add).then_inc(s_d, E.adds(s_d))
                    for tap in range(1, 4):
                        E.eng.wait_ge(E.last, E.sofar(E.last))
                        for c in range(2):
                            k = 4 * b + 2 * n + c
                            last = nc.vector.scalar_tensor_tensor(out=cout[:, c, :], in0=cin[:, c, tap:tap + S], scalar=cw[:, 24 * tap + k:24 * tap + k + 1],
                                                                  in1=cout[:, c, :], op0=ALU.mult, op1=ALU.add)
                            last.then_inc(s_u if tap == 3 and c else s_d, E.adds(s_u if tap == 3 and c else s_d))
                    E.eng.wait_ge(s_uh, E.next(s_uh))
                    nc.vector.tensor_scalar(cex[:, :, :], cex[:, :, :], 1.0, None, ALU.add).then_inc(s_d, E.adds(s_d))
                    E.eng.wait_ge(E.last, E.sofar(E.last))
                    nc.vector.reciprocal(cex[:, :, :], cex[:, :, :]).then_inc(s_d, E.adds(s_d))
                    E.eng.wait_ge(E.last, E.sofar(E.last))
                    if b < 4:
                        nc.vector.tensor_tensor(cout[:, :, :], cout[:, :, :], cex[:, :, :], ALU.mult).then_inc(s_mix, E.adds(s_mix))
                        E.eng.wait_ge(s_cin, E.next(s_cin))
                    else:
                        nc.vector.tensor_tensor(bct[:, b - 4, 2 * n:2 * n + 2, :], cout[:, :, :], cex[:, :, :], ALU.mult).then_inc(s_d, E.adds(s_d))
                        E.eng.wait_ge(E.last, E.sofar(E.last))
                dve_lo(E, 2)
            dve_lo(E, 1)
            r = slice(0, 32)
            nc.vector.tensor_scalar(dm[r, :], dx[r, :], 0.0, None, ALU.max).then_inc(s_d, E.adds(s_d))
            nc.vector.scalar_tensor_tensor(out=dn[r, :], in0=dx[r, :], scalar=-1.0, in1=dx[r, :], op0=ALU.mult, op1=ALU.min).then_inc(s_u, E.adds(s_u))
            E.eng.wait_ge(s_uh, E.next(s_uh))
            nc.vector.tensor_tensor(dn[r, :], dn[r, :], dm[r, :], ALU.add).then_inc(s_d, E.adds(s_d))
            E.eng.wait_ge(E.last, E.sofar(E.last))
            nc.vector.tensor_scalar(dx[r, :], dn[r, :], alog[r, :], -1.0, ALU.mult, ALU.mult).then_inc(s_d, E.adds(s_d))
            E.eng.wait_ge(E.last, E.sofar(E.last))
            for q in range(NT):
                last = nc.vector.tensor_tensor_scan(acT[r, q * P:(q + 1) * P], ones[r, 0:1].to_broadcast([32, P]), dx[r, q * P:(q + 1) * P], 0.0, ALU.mult, ALU.add)
            last.then_inc(s_u, E.adds(s_u))
            E.eng.wait_ge(s_uh, E.next(s_uh))
            nc.vector.memset(s16[:, 15:16], 0.0).then_inc(s_mix, E.adds(s_mix))
            E.eng.wait_ge(s_uh, E.next(s_uh))
            with E.loop(4, {s_stg: 1, s_mix: 2, s_d: 10, s_sc: 1, s_dec: 2, s_mx: 2, s_e: 2, s_scd: 2, s_o: 2}) as g:
                nc.vector.tensor_copy(bcs[:, :, :], bct[:, :, g, :])
                nc.vector.tensor_copy(brs[:, :], brow2[:, g, :]).then_inc(s_stg, E.adds(s_stg))
                for q in range(NT):
                    nc.vector.tensor_tensor(am[r, q], acT[r, q * P:(q + 1) * P].unsqueeze(1).to_broadcast([32, 8, P]),
                                                   ident[r, 0:32].rearrange("p (g h) -> p g h", h=8)[:, g, :].unsqueeze(2).to_broadcast([32, 8, P]), ALU.mult).then_inc(s_mix, E.adds(s_mix))
                x8 = lambda q: xs[:, q, g, :].rearrange("p (h n) -> p h n", n=64)
                col = lambda n: rws[:, n, :].rearrange("p (g h) -> p g h", h=8)[:, g, :]
                for q in range(NT):
                    nc.vector.tensor_tensor(xdt[:, q], x8(q), col(q).unsqueeze(2).to_broadcast([P, 8, 64]), ALU.mult).then_inc(s_d, E.adds(s_d))
                E.eng.wait_ge(E.last, E.sofar(E.last))
                nc.vector.tensor_tensor(xdw[:, :, :], xdt[:, 0], col(4).unsqueeze(2).to_broadcast([P, 8, 64]), ALU.mult).then_inc(s_d, E.adds(s_d))
                E.eng.wait_ge(s_sc, E.next(s_sc))
                for q in range(NT):
                    nc.vector.tensor_tensor(cbm[:, q, :], ps[:, 0, q * P:(q + 1) * P], upper[:, :], ALU.mult).then_inc(s_d, E.adds(s_d))
                for q in range(NT):
                    E.eng.wait_ge(s_dec, E.next(s_dec))
                    for h in range(8):
                        last = nc.vector.tensor_scalar(ee[:, q, h, :], ps[:, 2 + 2 * q + h // 4, (h % 4) * P:(h % 4) * P + P],
                                                       rws[:, 2 + q, :].rearrange("p (g h) -> p g h", h=8)[:, g, h:h + 1], 0.0, ALU.subtract, ALU.min)
                    last.then_inc(s_mx, E.adds(s_mx))
                for q in range(NT):
                    E.eng.wait_ge(s_e, E.next(s_e))
                    E.eng.wait_ge(s_d, E.sofar(s_d))
                    nc.vector.tensor_tensor(ee[:, q], ee[:, q], cbm[:, q, :].unsqueeze(1).to_broadcast([P, 8, P]), ALU.mult).then_inc(s_scd, E.adds(s_scd))
                dskb = dsk.rearrange("p (g h) -> p g h", h=8)[:, g, :].unsqueeze(2).to_broadcast([P, 8, 64])
                for q in range(NT):
                    nc.vector.tensor_tensor(x8(q), x8(q), dskb, ALU.mult).then_inc(s_d, E.adds(s_d))
                E.eng.wait_ge(s_o, E.next(s_o))
                E.eng.wait_ge(s_d, E.sofar(s_d))
                p8 = lambda b: ps[:, b, :].rearrange("p (h n) -> p h n", n=64)
                nc.vector.tensor_tensor(x8(0), x8(0), p8(6), ALU.add)
                E.eng.wait_ge(s_o, E.next(s_o))
                nc.vector.tensor_tensor(xdt[:, 0], p8(2), col(5).unsqueeze(2).to_broadcast([P, 8, 64]), ALU.mult).then_inc(s_d, E.adds(s_d))
                nc.vector.tensor_tensor(x8(1), x8(1), p8(7), ALU.add).then_inc(s_d, E.adds(s_d))
                E.eng.wait_ge(s_d, E.sofar(s_d))
                nc.vector.tensor_tensor(x8(1), x8(1), xdt[:, 0], ALU.add).then_inc(s_d, E.adds(s_d))
                E.eng.wait_ge(E.last, E.sofar(E.last))
            nc.vector.memset(s16[:, 13:14], 0.0).then_inc(s_evd, E.adds(s_evd))
            with E.loop(2, {s_uh: 4, s_d: 8, s_evd: 4, s_u: 4, s_hi: 2, s_lo: 2, s_mm: 4}) as i:
                for b in range(2):
                    for q in range(NT):
                        z = zt[:, 2 * b + q, :]
                        E.eng.wait_ge(s_uh, E.next(s_uh))
                        nc.vector.tensor_scalar(z, z, 1.0, None, ALU.add).then_inc(s_d, E.adds(s_d))
                        E.eng.wait_ge(E.last, E.sofar(E.last))
                        nc.vector.reciprocal(z, z).then_inc(s_d, E.adds(s_d))
                        E.eng.wait_ge(E.last, E.sofar(E.last))
                        nc.vector.tensor_tensor(z, z, ps[:, 2 * b + q, :], ALU.mult).then_inc(s_evd, E.adds(s_evd))
                        E.eng.wait_ge(E.last, E.sofar(E.last))
                        nc.vector.tensor_tensor(xs[:, q, 2 * i + b, :], xs[:, q, 2 * i + b, :], z, ALU.mult).then_inc(s_u, E.adds(s_u))
                    dve_lo(E, 2)
            nc.vector.memset(s16[:, 14:15], 0.0).then_inc(s_mix, E.adds(s_mix))
            E.eng.wait_ge(s_mixa, E.next(s_mixa))
            nc.vector.tensor_scalar(s16[:, 0:2], s16[:, 0:2], 1.0 / 2048, EPS, ALU.mult, ALU.add).then_inc(s_mix, E.adds(s_mix))
            E.eng.wait_ge(s_mixa, E.next(s_mixa))
            nc.vector.reciprocal(s16[:, 0:2], s16[:, 0:2]).then_inc(s_d, E.adds(s_d))
            E.eng.wait_ge(E.last, E.sofar(E.last))
            for q in range(NT):
                last = nc.vector.tensor_scalar(xs[:, q], xs[:, q], s16[:, q:q + 1], None, ALU.mult)
            last.then_inc(s_mix, E.adds(s_mix))
            for h in range(2):
                dve_turn(E, lambda c: gg("ssd_norm_2", layer2[0], 16)(8 * h + c), bh, bl)
                if h == 0:
                    dve_out_splits(E)
                else:
                    for b in range(2):
                        for n in range(2):
                            E.eng.wait_ge(s_mm, E.next(s_mm))
                            c = 4 * b + 2 * n
                            nc.vector.tensor_tensor(yT[:, c:c + 2, :], yT[:, c:c + 2, :], bank(2 * b + n), ALU.add).then_inc(s_evd, E.adds(s_evd))
                        dve_lo(E)
            dve_lo(E, 2)
            dve_lo(E, 2)
            dve_gate(E, mg, None)

        def dve_gate(E, dst, plus):
            nc.vector.tensor_scalar(ge8[:, :, :], ge8[:, :, :], 1.0, None, ALU.add).then_inc(s_d, E.adds(s_d))
            E.eng.wait_ge(E.last, E.sofar(E.last))
            nc.vector.reciprocal(ge8[:, :, :], ge8[:, :, :]).then_inc(s_d, E.adds(s_d))
            E.eng.wait_ge(E.last, E.sofar(E.last))
            if plus is None:
                nc.vector.tensor_tensor(dst[:, :, :], ge8[:, :, :], yT[:, :, :], ALU.mult).then_inc(s_d, E.adds(s_d))
            else:
                nc.vector.tensor_tensor(ge8[:, :, :], ge8[:, :, :], yT[:, :, :], ALU.mult).then_inc(s_d, E.adds(s_d))
                E.eng.wait_ge(E.last, E.sofar(E.last))
                nc.vector.tensor_tensor(dst[:, :, :], dst[:, :, :], ge8[:, :, :], ALU.add).then_inc(s_x, E.adds(s_x))
            E.eng.wait_ge(E.last, E.sofar(E.last))

        vm = view(ar, 0, [P, NT, 4, 2, P])
        qkn = view(ar, 2048, [P, 8, 2, S])
        qkr = view(ar, 6144, [P, 4, 2, S])
        rows = view(ar, 10240, [P, NT, 8, 192])
        cqT = view(ar, 4096, [P, 4, S])
        ckT = view(ar, 5120, [P, 2, S])
        krr = view(ar, 13312, [P, NT, 64])
        rb = view(ar, 13312, [P, NT, 8, 64])
        sgn = view(ar, 12544, [P, 2, 2, S])
        sgr = view(ar, 13568, [P, 2, S])
        yq = yf[:, 0:1536].rearrange("p (h n) -> p h n", n=192)
        rt1 = yf[:, 0:512].rearrange("p (q h n) -> p q h n", q=NT, h=8)
        rt2 = yf[:, 512:1024].rearrange("p (q h n) -> p q h n", q=NT, h=8)
        invf = yf[:, 1536:1568]
        ang = yf[:, 1568:1632].rearrange("p (q n) -> p q n", q=NT)
        kr2 = yf[:, 1632:1696].rearrange("p (q n) -> p q n", q=NT)
        trig = yf[:, 1696:1824].rearrange("p (a q n) -> p a q n", a=2, q=NT)
        posf = yf[:, 1824:1826]
        cqh, cql = view(ar_r, 0, [P, 4, S]), view(ar_r, 1024, [P, 4, S])
        ckh, ckl = view(ar_r, 2048, [P, 2, S]), view(ar_r, 2560, [P, 2, S])

        def pe_to_T(E):
            E.eng.wait_ge(s_mix, E.next(s_mix))
            for b in range(4):
                for h in (2 * b, 2 * b + 1):
                    for q in range(NT):
                        last = nc.tensor.transpose(ps[:, b, (h % 2) * S + q * P:(h % 2) * S + (q + 1) * P], rows[:, q, h, 0:P], ident[:, :])
                last.then_inc(s_tp, E.adds(s_tp))
            for b in range(2):
                for j in (2 * b, 2 * b + 1):
                    for q in range(NT):
                        last = nc.tensor.transpose(ps[:, 4 + b, (j % 2) * S + q * P:(j % 2) * S + (q + 1) * P],
                                                   rb[:, q, 2 * j:2 * j + 2, :].rearrange("p h n -> p (h n)"), ident[:, :])
                last.then_inc(s_tp, E.adds(s_tp))
            E.skip(s_ev, 6)

        def act_to_T(E, a):
            for b in range(4):
                E.eng.wait_ge(s_tp, E.next(s_tp))
                nc.scalar.activation(qkn[:, 2 * b:2 * b + 2, a, :], bank(b), ACT.Copy).then_inc(s_ev, E.adds(s_ev))
            for b in range(2):
                E.eng.wait_ge(s_tp, E.next(s_tp))
                nc.scalar.activation(qkr[:, 2 * b:2 * b + 2, a, :], bank(4 + b), ACT.Copy).then_inc(s_ev, E.adds(s_ev))

        def pe_scores_mla(E, _):
            E.eng.wait_ge(s_stg, E.next(s_stg))
            if E.seen(s_scd):
                E.eng.wait_ge(s_scd, E.sofar(s_scd))
            for c in range(2):
                lo = slice(64 * c, 64 * c + 64)
                for q, (a, b) in enumerate(COLS):
                    o, keys, qs = ps[:, c, a:b], slice(0, b - a), slice(q * P, (q + 1) * P)
                    nc.tensor.matmul(o, sgn[:, c, 0, qs], sgn[:, c, 1, keys], start=True, stop=False)
                    last = nc.tensor.matmul(o, sgr[lo, 0, qs], sgr[lo, 1, keys], start=False, stop=True)
                last.then_inc(s_sc, E.adds(s_sc))
            E.skip(s_scd, 2)

        def dve_stage_mla(E, j, _):
            nc.vector.tensor_copy(sgn.rearrange("p c a t -> p (c a t)"), qkn.rearrange("p (j c) a t -> p j (c a t)", c=2)[:, j, :])
            nc.vector.tensor_copy(sgr[:, :, :], qkr[:, j, :, :]).then_inc(s_stg, E.adds(s_stg))

        def pe_mla(E):
            if E.seen(s_ev):
                E.eng.wait_ge(s_ev, E.sofar(s_ev))
            pe_T(E, 512, 8, ah, al, 0)
            E.skip(s_ev, 2)
            slot = E.slot()
            E.eng.wait_ge(s_lo, E.next(s_lo))
            a, b = wv(wh, slot, 320, 8), wv(wl, slot, 320, 8)
            for m in range(2):
                for k in range(8):
                    c = slice(m * P, (m + 1) * P)
                    last = mm3(ps[:, 2, m * S:m * S + S], a[:, k, c], b[:, k, c], ah[:, k], al[:, k], k == 0, k == 7)
            last.then_inc(s_mm, E.adds(s_mm))
            for q in range(NT):
                t = slice(q * P, (q + 1) * P)
                for k in range(8):
                    last = mm3(ps[:, 3, 64 * q:64 * q + 64], ah[:, k, t], al[:, k, t], a[:, k, S:320], b[:, k, S:320], k == 0, k == 7)
            last.then_inc(s_mm, E.adds(s_mm))
            E.skip(s_ev, 2)
            pe_stats(E, 4)
            E.eng.wait_ge(s_op, E.next(s_op, 4))
            pe_stats(E, 2)
            E.eng.wait_ge(s_op, E.next(s_op, 2))
            for b in range(2):
                pe_free(E)
                slot = E.slot()
                E.eng.wait_ge(s_lo, E.next(s_lo))
                wa, wb = wv(wh, slot, 1024, 2), wv(wl, slot, 1024, 2)
                for q in range(NT):
                    t = slice(q * P, (q + 1) * P)
                    for n in range(2):
                        for k in range(2):
                            last = mm3(ps[:, 4 * b + 2 * q + n, :], ckh[:, k, t], ckl[:, k, t], wa[:, k, 512 * n:512 * n + 512], wb[:, k, 512 * n:512 * n + 512], k == 0, k == 1)
                        last.then_inc(s_mm, E.adds(s_mm))
                E.skip(s_ev, 4)
            pe_free(E)
            E.skip(s_mix, 2)
            pe_to_T(E)
            pe_free(E)
            for b in range(3):
                pe_rows(E, 512, 4, cqh, cql, 2 * b)
                E.skip(s_ev, 2)
            pe_free(E)
            E.skip(s_mix)
            pe_to_T(E)
            pe_free(E)
            pe_attention(E, 4, wide=P, scores=pe_scores_mla, v=lambda t, j, c: vm[:, t, j, c, :])
            pe_turn(E, ready=s_od)
            E.eng.wait_ge(s_op, E.next(s_op, 4))
            pe_T(E, 512, 8, bh, bl, 0)
            pe_T(E, 512, 8, bh, bl, 2)
            E.skip(s_ev, 4)
            if E.seen(s_ev, 2):
                E.eng.wait_ge(s_ev, E.sofar(s_ev, 2))
            pe_T(E, 512, 8, ah, al, 0)
            if E.seen(s_ev):
                E.eng.wait_ge(s_ev, E.sofar(s_ev))
            pe_T(E, 512, 8, ah, al, 2)
            E.skip(s_ev, 4)
            E.eng.wait_ge(s_op, E.next(s_op, 8))
            if E.seen(s_ev):
                E.eng.wait_ge(s_ev, E.sofar(s_ev))
            pe_T(E, 512, 8, ah, al, 0)
            pe_T(E, 512, 8, ah, al, 2)
            E.skip(s_ev, 4)

        def act_mla(E):
            act_copy(E, [cqT[:, 0:2, :], cqT[:, 2:4, :]], 0)
            E.eng.wait_ge(s_mm, E.next(s_mm))
            nc.scalar.activation(ckT[:, :, :], bank(2), ACT.Copy).then_inc(s_ev, E.adds(s_ev))
            E.eng.wait_ge(s_mm, E.next(s_mm))
            nc.scalar.activation(krr[:, :, :], ps[:, 3, 0:P].rearrange("p (q n) -> p q n", q=NT), ACT.Copy).then_inc(s_ev, E.adds(s_ev))
            act_hi(E)
            E.eng.wait_ge(s_ev, E.sofar(s_ev))
            act_stats(E, cqT, 4, False)
            act_operand(E, cqT, 4, cqh)
            act_stats(E, ckT, 2, False)
            act_operand(E, ckT, 2, ckh)
            for b in range(2):
                for q in range(NT):
                    for n in range(2):
                        E.eng.wait_ge(s_mm, E.next(s_mm))
                        src = ps[:, 4 * b + 2 * q + n, :].rearrange("p (h a n) -> p h a n", h=2, a=2)
                        j = 2 * b + n
                        nc.scalar.activation(rows[:, q, 2 * j:2 * j + 2, 0:P], src[:, :, 0, :], ACT.Copy)
                        nc.scalar.activation(vm[:, q, j], src[:, :, 1, :], ACT.Copy).then_inc(s_ev, E.adds(s_ev))
                act_hi(E)
            E.eng.wait_ge(s_mix, E.next(s_mix))
            nc.scalar.activation(trig[:, :, :, :], trig[:, :, :, :], ACT.Sin).then_inc(s_mixa, E.adds(s_mixa))
            for a in (1, 0):
                E.eng.wait_ge(s_mix, E.next(s_mix))
                nc.scalar.activation(s16[:, :], s16[:, :], ACT.Sqrt).then_inc(s_mixa, E.adds(s_mixa))
                E.skip(s_mix)
                act_to_T(E, a)
                if a == 1:
                    for b in range(3):
                        for q in range(NT):
                            E.eng.wait_ge(s_mm, E.next(s_mm))
                            nc.scalar.activation(rows.rearrange("p q h n -> p q (h n)")[:, q, 512 * b:512 * b + 512], ps[:, 2 * b + q, :], ACT.Copy).then_inc(s_ev, E.adds(s_ev))
                        act_hi(E)
            E.eng.wait_ge(s_ev, E.sofar(s_ev))
            nc.scalar.activation(sm[:, 600:601], sm[:, 0:1], ACT.Copy).then_inc(s_wo, E.adds(s_wo))
            act_attention(E, 4)
            act_turn(E, 1.0, bh)
            act_out(E)
            for b in range(2):
                for n in range(2):
                    E.eng.wait_ge(s_mm, E.next(s_mm))
                    nc.scalar.activation(ge8[:, 4 * b + 2 * n:4 * b + 2 * n + 2, :], bank(2 * b + n), ACT.Exp, scale=-1.0).then_inc(s_ev, E.adds(s_ev))
                act_hi(E)
            act_operand(E, mg, DC, ah, False)
            act_out(E)

        TWO_PI = 2 * math.pi

        def dve_angles(E):
            nc.vector.tensor_copy(posf, posi[:, :]).then_inc(s_d, E.adds(s_d))
            E.eng.wait_ge(E.last, E.sofar(E.last))
            for q in range(NT):
                last = nc.vector.tensor_scalar(ang[:, q, :], invf, posf[:, q:q + 1], None, ALU.mult)
            last.then_inc(s_d, E.adds(s_d))
            E.eng.wait_ge(E.last, E.sofar(E.last))
            magic = 12582912.0
            nc.vector.tensor_scalar(kr2, ang, 1.0 / TWO_PI, magic, ALU.mult, ALU.add).then_inc(s_d, E.adds(s_d))
            E.eng.wait_ge(E.last, E.sofar(E.last))
            nc.vector.tensor_scalar(kr2, kr2, magic, None, ALU.subtract).then_inc(s_d, E.adds(s_d))
            E.eng.wait_ge(E.last, E.sofar(E.last))
            for part in (6.28125, TWO_PI - 6.28125):
                nc.vector.scalar_tensor_tensor(out=ang, in0=kr2, scalar=-part, in1=ang, op0=ALU.mult, op1=ALU.add).then_inc(s_d, E.adds(s_d))
                E.eng.wait_ge(E.last, E.sofar(E.last))
            pi = 3.1415925
            nc.vector.tensor_scalar(trig[:, 0], ang, -pi, pi, ALU.max, ALU.min).then_inc(s_d, E.adds(s_d))
            nc.vector.tensor_scalar(ang, ang, math.pi / 2, None, ALU.add).then_inc(s_d, E.adds(s_d))
            E.eng.wait_ge(E.last, E.sofar(E.last))
            nc.vector.tensor_scalar(kr2, ang, math.pi, -TWO_PI, ALU.is_gt, ALU.mult).then_inc(s_d, E.adds(s_d))
            E.eng.wait_ge(E.last, E.sofar(E.last))
            nc.vector.tensor_tensor(ang, ang, kr2, ALU.add).then_inc(s_d, E.adds(s_d))
            E.eng.wait_ge(E.last, E.sofar(E.last))
            nc.vector.tensor_scalar(trig[:, 1], ang, -pi, pi, ALU.max, ALU.min).then_inc(s_mix, E.adds(s_mix))
            E.eng.wait_ge(s_mixa, E.next(s_mixa))

        def dve_heads(E, gain):
            for q in range(NT):
                nc.vector.tensor_tensor(yq, rows[:, q], rows[:, q], ALU.mult).then_inc(s_d, E.adds(s_d))
                E.eng.wait_ge(E.last, E.sofar(E.last))
                nc.vector.tensor_reduce(s16[:, 8 * q:8 * q + 8], yq, AX.X, ALU.add).then_inc(s_d, E.adds(s_d))
                E.eng.wait_ge(E.last, E.sofar(E.last))
            nc.vector.tensor_scalar(s16[:, :], s16[:, :], 1.0 / 192, EPS, ALU.mult, ALU.add).then_inc(s_mix, E.adds(s_mix))
            E.eng.wait_ge(s_mixa, E.next(s_mixa))
            nc.vector.reciprocal(s16[:, :], s16[:, :]).then_inc(s_d, E.adds(s_d))
            E.eng.wait_ge(E.last, E.sofar(E.last))
            for q in range(NT):
                nc.vector.tensor_tensor(rows[:, q], rows[:, q], s16[:, 8 * q:8 * q + 8].unsqueeze(2).to_broadcast([P, 8, 192]), ALU.mult).then_inc(s_d, E.adds(s_d))
            E.eng.wait_ge(E.last, E.sofar(E.last))
            for q in range(NT):
                nc.vector.tensor_tensor(rows[:, q], rows[:, q], gain[:, :].unsqueeze(1).to_broadcast([P, 8, 192]), ALU.mult).then_inc(s_d, E.adds(s_d))
            E.eng.wait_ge(E.last, E.sofar(E.last))
            b32 = lambda a: trig[:, a].unsqueeze(2).to_broadcast([P, NT, 8, 32])
            t1, t2 = rows[:, :, :, P:P + 32], rows[:, :, :, P + 32:192]
            for (x, y, op, at) in ((t1, t2, ALU.subtract, 0), (t2, t1, ALU.add, 32)):
                for q in range(NT):
                    bq = lambda a: trig[:, a, q, :].unsqueeze(1).to_broadcast([P, 8, 32])
                    nc.vector.tensor_tensor(rt1[:, q], x[:, q], bq(1), ALU.mult)
                    nc.vector.tensor_tensor(rt2[:, q], y[:, q], bq(0), ALU.mult).then_inc(s_d, E.adds(s_d))
                E.eng.wait_ge(E.last, E.sofar(E.last))
                last = nc.vector.tensor_tensor(rb[:, :, :, at:at + 32].rearrange("p q h n -> p (q h) n"), rt1.rearrange("p q h n -> p (q h) n"), rt2.rearrange("p q h n -> p (q h) n"), op)
                last.then_inc(s_mix if at else s_d, E.adds(s_mix if at else s_d))
                E.eng.wait_ge(E.last, E.sofar(E.last))

        def dve_mla(E):
            dve_lo(E, 2)
            dve_lo(E, 2)
            dve_stats(E, 4)
            dve_operand(E, cqT, gg("q_lora_norm_2", layer2[0], 4), 4, cqh, cql)
            dve_stats(E, 2)
            dve_operand(E, ckT, gg("kv_lora_norm_2", layer2[0], 2), 2, ckh, ckl)
            nc.vector.tensor_copy(invf, cinv[:, :]).then_inc(s_d, E.adds(s_d))
            dve_lo(E, 4)
            dve_lo(E, 4)
            dve_angles(E)
            for q in range(NT):
                last = nc.vector.tensor_copy(rows[:, q, :, P:192], krr[:, q, :].unsqueeze(1).to_broadcast([P, 8, 64]))
            last.then_inc(s_d, E.adds(s_d))
            E.eng.wait_ge(E.last, E.sofar(E.last))
            dve_heads(E, kng)
            for b in range(3):
                dve_lo(E, 2)
            dve_heads(E, qng)
            E.eng.wait_ge(s_wo, E.next(s_wo))
            dve_attention(E, 4, "mla", 192.0 ** -0.5, table=False, wide=P, stage=dve_stage_mla)
            dve_turn(E, 1.0, bh, bl)
            dve_out_splits(E)
            dve_lo(E, 2)
            dve_lo(E, 2)
            dve_gate(E, mg, True)
            dve_operand(E, mg, None, DC, ah, al, normed=False)
            dve_out_splits(E)
            E.eng.wait_ge(s_wo, E.next(s_wo))
            nc.vector.tensor_tensor(xT[:, :, :], xT[:, :, :], yT[:, :, :], ALU.add).then_inc(s_x, E.adds(s_x))
            E.eng.wait_ge(s_x, E.sofar(s_x))

        def pe_second(E, layer):
            pe_ffn(E)
            pe_stats(E, DC)
            pe_ssd(E)
            pe_mla(E)
            pe_ffn(E)
            E.skip(s_x, 4)

        def act_second(E, layer):
            layer2[0] = layer
            act_ffn(E)
            act_stats(E, xT, DC)
            act_operand(E, xT, DC, ah)
            act_ssd(E)
            act_mla(E)
            nc.scalar.activation(sm[:, 600:601], sm[:, 124:125], ACT.Copy).then_inc(s_wo, E.adds(s_wo))
            act_ffn(E)

        def dve_second(E, layer):
            layer2[0] = layer
            dve_ffn(E, "ln_ffn1_2", layer)
            dve_stats(E, DC)
            dve_operand(E, xT, gg("ln_mix_2", layer, 8), DC, ah, al)
            dve_ssd(E)
            dve_mla(E)
            dve_ffn(E, "ln_ffn2_2", layer)

        fin = view(ar, 0, [P, NT, D])

        def pe_end(E):
            E.eng.wait_ge(s_x, E.next(s_x))
            pe_free(E)
            for q in range(NT):
                for b in range(2):
                    for c in range(4):
                        last = nc.tensor.transpose(ps[:, 2 * q + b, c * P:(c + 1) * P], xT[:, 4 * b + c, q * P:(q + 1) * P], ident[:, :])
                    last.then_inc(s_tp, E.adds(s_tp))

        def act_end(E):
            for q in range(NT):
                for b in range(2):
                    E.eng.wait_ge(s_tp, E.next(s_tp))
                    nc.scalar.activation(fin[:, q, 512 * b:512 * b + 512], ps[:, 2 * q + b, :], ACT.Copy).then_inc(s_mixa, E.adds(s_mixa))
                E.eng.wait_ge(s_mixa, E.sofar(s_mixa))
                E.eng.dma_start(out[0].rearrange("(q p) n -> q p n", p=P)[q], fin[:, q, :]).then_inc(s_out, 16)
            E.eng.wait_ge(s_out, 16 * NT)

        block = ctx.enter_context(nc.Block())
        nl = DEPTH if stop is None else min(stop, DEPTH)
        nl2 = DEPTH2 if stop is None else max(0, stop - DEPTH)

        @block.sync
        def _(eng):
            E = Track(eng)
            sp_start(E)
            for layer in range(nl):
                if layer % 3 == 0:
                    sp_da(E, layer // 3)
                elif layer == 1:
                    sp_nsa(E)
                else:
                    sp_fox(E)
                sp_rest(E, layer)
            for layer in range(nl2):
                sp_second(E, layer)

        @block.gpsimd
        def _(eng):
            E = Track(eng)
            pool_start(E)
            if nl > 3:
                pool_bias_again(E)

        @block.scalar
        def _(eng):
            E = Track(eng)
            act_start(E)
            for layer in range(nl):
                act_stats(E, xT, DC, layer > 0)
                act_operand(E, xT, DC, ah)
                if layer % 3 == 0:
                    act_qkv(E)
                    if layer == 0:
                        act_flip(E)
                    act_attention(E, 8)
                    act_subln(E)
                    act_turn(E, lambda c: subl[:, layer // 3:layer // 3 + 1])
                elif layer == 1:
                    act_nsa(E)
                else:
                    act_fox(E)
                act_out(E)
                act_rest(E)
            for layer in range(nl2):
                act_second(E, layer)
            act_end(E)

        @block.tensor
        def _(eng):
            E = Track(eng)
            pe_start(E)
            for layer in range(nl):
                pe_stats(E, DC)
                if layer % 3 == 0:
                    pe_qkv(E)
                    if layer == 0:
                        pe_flip(E)
                    pe_attention(E, 8, shared=True)
                    E.skip(s_mix)
                    E.skip(s_mixa)
                    pe_turn(E)
                elif layer == 1:
                    pe_nsa(E)
                else:
                    pe_fox(E)
                pe_out(E, 4)
                pe_rest(E)
                E.skip(s_x, 4)
            for layer in range(nl2):
                pe_second(E, layer)
            E.n[s_x] -= 1
            pe_end(E)

        @block.vector
        def _(eng):
            E = Track(eng)
            dve_start(E)
            for layer in range(nl):
                dve_stats(E, DC)
                dve_operand(E, xT, g1(layer, 0), DC, ah, al)
                if layer % 3 == 0:
                    lamL[0] = layer // 3
                    dve_qkv(E)
                    if layer == 0:
                        E.skip(s_rows, 16)
                        E.eng.wait_ge(s_mixa, E.next(s_mixa))
                    else:
                        E.eng.wait_ge(s_rows, E.next(s_rows, 16))
                    dve_attention(E, 8, "da", 0.125)
                    dve_subln(E)
                    dve_turn(E, lambda c: subl[:, layer // 3:layer // 3 + 1])
                elif layer == 1:
                    dve_nsa(E)
                else:
                    dve_fox(E)
                dve_out_splits(E)
                dve_rest(E, layer)
            for layer in range(nl2):
                dve_second(E, layer)


_INS = ["x", "p", "rel_bias", "norm_g", "mlp_w1", "mlp_w2", "ple_w", "ple_gate_w", "da_w_in", "da_lambda", "da_subln",
        "da_w_out", "nsa_w_in", "nsa_cmp_pe", "nsa_cmp_w1", "nsa_cmp_w2", "nsa_w_out", "fox_w_in", "fox_b_f",
        "fox_w_out", "positions_2", "ln_ffn1_2", "ffn1_w13_2", "ffn1_w2_2", "ln_mix_2", "w_in_2", "conv_w_2",
        "conv_b_2", "dt_bias_2", "a_log_2", "d_skip_2", "ssd_norm_2", "w_ssd_out_2", "q_lora_norm_2", "w_uq_2",
        "kv_lora_norm_2", "w_ukv_2", "q_norm_2", "k_norm_2", "w_mla_out_2", "w_o_2", "ln_ffn2_2", "ffn2_w13_2",
        "ffn2_w2_2"]


def kernel(**inputs):
    import concourse.bacc as _bacc
    from concourse.bass_utils import run_bass_kernel_spmd as _run

    nc = _bacc.Bacc("TRN2", target_bir_lowering=False, num_devices=1)
    arrays, d = {}, {}
    given = {name: np.ascontiguousarray(inputs[name]) for name in _INS}
    for name, a in {**given, **shape_constants()}.items():
        arrays[f"in_{name}"] = a
        d[name] = nc.dram_tensor(f"in_{name}", a.shape, mybir.dt.from_np(a.dtype), kind="ExternalInput").ap()
    out = nc.dram_tensor("out_0", (1, S, D), F32, kind="ExternalOutput").ap()
    build(nc, d, out)
    r = _run(nc, [arrays], core_ids=[0])
    return r.results[0]["out_0"]
```

```python
import math
from contextlib import ExitStack, contextmanager

import numpy as np

import concourse.bass as bass
from concourse import mybir
from concourse.alu_op_type import AluOpType as ALU

F32 = mybir.dt.float32
F32R = mybir.dt.float32r
I32 = mybir.dt.int32
ACT = mybir.ActivationFunctionType
AX = mybir.AxisListType

P = 128
D = 1024
S = 256
NT = S // P
DC = D // P
DEPTH = 4
NEG = -1.0e30
EPS = 1e-6
BLK = 4096
H64 = 16
NB = 32
NCMP = (S - 32) // 16 + 1
F_MLP = 4096
F_GLU = 2816
DEPTH2 = 2
W_IN2 = 8032
O_Z, O_XBC, O_DT, O_CQ, O_CKV, O_KR, O_G = 0, 2048, 5120, 5152, 5664, 5920, 5984
LAM_INIT = [0.8 - 0.6 * math.exp(-0.3 * i) for i in range(DEPTH)]


class Track:

    def __init__(self, eng):
        self.eng, self.n, self.per, self.i, self.last = eng, {}, {}, None, None
        self.m = 0

    def adds(self, s, k=1):
        self.n[s] = self.n.get(s, 0) + k
        self.last = s
        return k

    def skip(self, s, k=1):
        self.n[s] = self.n.get(s, 0) + k

    def sofar(self, s, back=0):
        v = self.n.get(s, 0) - back
        if self.i is not None and self.per.get(s, 0):
            return self.i * self.per[s] + v
        return v

    def next(self, s, k=1):
        self.skip(s, k)
        return self.sofar(s)

    def seen(self, s, back=0):
        if self.n.get(s, 0) - back <= 0 and self.i is not None:
            raise ValueError(f"{s.name}: the first turn would wait for nothing")
        return self.n.get(s, 0) - back > 0

    def slot(self):
        self.m += 1
        return (self.m - 1) % 2

    @contextmanager
    def loop(self, turns, per):
        start, m = dict(self.n), self.m
        with self.eng.Fori(0, turns) as i:
            self.i, self.per = i, per
            yield i
        got = {s: v - start.get(s, 0) for s, v in self.n.items() if v != start.get(s, 0)}
        if got != {s: v for s, v in per.items() if v}:
            raise ValueError(f"a turn adds { {s.name: v for s, v in got.items()} }, stated { {s.name: v for s, v in per.items()} }")
        for s, v in per.items():
            self.n[s] = start.get(s, 0) + turns * v
        self.i, self.per = None, {}
        if (self.m - m) % 2:
            raise ValueError("a turn takes an odd number of blocks")
        self.m += (turns - 1) * (self.m - m)


def shape_constants():
    dist = np.arange(512) - 255
    n = np.maximum(dist, 0)
    nf = np.maximum(n, 1).astype(np.float32)
    large = 16 + (np.log(nf / np.float32(16)) / np.float32(math.log(8)) * np.float32(16)).astype(np.int32)
    bucket = np.where(n < 16, n, np.minimum(large, NB - 1))
    fwd = np.zeros((NB + 1, 512), np.float32)
    for j in range(511):
        if dist[j] < 0:
            fwd[NB, j] = NEG
        else:
            fwd[bucket[j], j] = 1.0
    rev = np.zeros((NB + 1, 512), np.float32)
    rev[:, :511] = fwd[:, :511][:, ::-1]
    q = np.arange(P)[:, None]
    k = np.arange(P)[None, :]
    tri = np.where(k <= q, 0.0, NEG).astype(np.float32)
    mask = np.concatenate([np.zeros((P, P), np.float32), tri], axis=1)
    t = np.arange(S).reshape(NT, P).T[:, :, None]
    cend = np.arange(NCMP)[None, None, :] * 16 + 31
    cmask = np.zeros((P, NT, 16), np.float32)
    cmask[:, :, :NCMP] = (t >= cend)
    inv = (1.0 / (np.float32(10000.0) ** (np.arange(0, 64, 2, dtype=np.float32) / np.float32(64)))).astype(np.float32)
    return {
        "c_ident": np.eye(P, dtype=np.float32),
        "c_fwd": fwd,
        "c_flip": np.ascontiguousarray(np.eye(P, dtype=np.float32)[::-1]),
        "c_rev": rev,
        "c_mask": mask,
        "c_cmask": cmask.reshape(P, NT * 16),
        "c_inv": np.tile(inv[None, :], (P, 1)),
        "c_upper": np.ascontiguousarray((k >= q).astype(np.float32)),
    }


def build(nc, d, out, stop=None):
    ctx = ExitStack()
    with ctx:
        sb = lambda n, s, dt=F32: ctx.enter_context(nc.sbuf_tensor(n, s, dt))
        sem = lambda n: ctx.enter_context(nc.semaphore(n))

        raw = sb("raw", [P, 2, BLK])
        wh = sb("wh", [P, 2, BLK], F32R)
        wl = sb("wl", [P, 2, BLK], F32R)
        xT = sb("xT", [P, DC, S])
        yT = sb("yT", [P, DC, S])
        ah = sb("ah", [P, DC, S], F32R)
        al = sb("al", [P, DC, S], F32R)
        ar = sb("ar", [P, 14336])
        ar_r = sb("ar_r", [P, 4096], F32R)
        ident = sb("ident", [P, P])
        ones = sb("ones", [P, P])
        cinv = sb("cinv", [P, 32])
        mask = sb("mask", [P, S])
        gT = sb("gT", [P, P])
        g2 = sb("g2", [P, P])
        st = sb("st", [P, 2, S])
        sm = sb("sm", [P, 608])
        ps = ctx.enter_context(nc.psum_tensor("ps", [P, 8, 512], F32))

        s_const = sem("s_const")
        s_rows = sem("s_rows")
        s_raw = [sem("s_raw0"), sem("s_raw1")]
        s_hi = sem("s_hi")
        s_lo = sem("s_lo")
        s_mm = sem("s_mm")
        s_ev = sem("s_ev")
        s_evd = sem("s_evd")
        s_a = sem("s_a")
        s_d = sem("s_d")
        s_u = sem("s_u")
        s_uh = sem("s_uh")
        s_op = sem("s_op")
        s_sq = sem("s_sq")
        s_ss = sem("s_ss")
        s_var = sem("s_var")
        s_rt = sem("s_rt")
        s_x = sem("s_x")
        s_tp = sem("s_tp")
        s_tpe = sem("s_tpe")
        s_stg = sem("s_stg")
        s_sc = sem("s_sc")
        s_scd = sem("s_scd")
        s_mx = sem("s_mx")
        s_e = sem("s_e")
        s_pt = sem("s_pt")
        s_pc = sem("s_pc")
        s_o = sem("s_o")
        s_od = sem("s_od")
        s_g = sem("s_g")
        s_p = sem("s_p")
        s_out = sem("s_out")
        s_fwd = sem("s_fwd")
        s_cin = sem("s_cin")
        s_xs = sem("s_xs")
        s_wo = sem("s_wo")
        s_gt = sem("s_gt")
        s_up = sem("s_up")
        s_small = sem("s_small")
        s_scr = sem("s_scr")
        s_dec = sem("s_dec")
        s_mix = sem("s_mix")
        s_mixp = sem("s_mixp")
        s_mixa = sem("s_mixa")

        scratch = nc.dram_tensor("bias_rows", [H64, 512], F32, kind="Internal").ap()
        bias_kept = nc.dram_tensor("bias_kept", [P, H64 * S], F32, kind="Internal").ap()

        def view(t, at, shape):
            n = math.prod(shape[1:])
            v = t[:, at:at + n]
            if len(shape) == 2:
                return v
            names = "abcd"[:len(shape) - 1]
            return v.rearrange(f"p ({' '.join(names)}) -> p {' '.join(names)}", **{c: s for c, s in zip(names[1:], shape[2:])})

        qk = view(ar, 0, [P, DC, 2, S])
        vv = view(ar, 4096, [P, NT, D])
        bias = view(ar, 6144, [P, H64, S])
        scb = view(ar, 10240, [P, 2, 384])
        eb = view(ar, 11008, [P, 2, 384])
        ptb = view(ar, 11776, [P, 2, 384])
        stg = view(ar, 12544, [P, 2, S])
        fcm = view(ar, 6144, [P, H64, S])
        orow = yT[:, :, :].rearrange("p c t -> p (c t)").rearrange("p (q n) -> p q n", q=NT)
        rr = view(ar, 13312, [P, 2, 2, S])
        hh = view(ar_r, 0, [P, 2, 4, S])
        hl = view(ar_r, 2048, [P, 2, 4, S])
        sq = view(ar, 0, [P, DC, S])
        tn = view(ar, 2048, [P, DC, S])
        sg = view(ar, 0, [P, DC, S])
        pT = view(ar_r, 0, [P, 2, S])
        pTl = view(ar_r, 512, [P, 2, S])
        prow = view(ar, 4096, [P, NT, S])
        bank = lambda b: ps[:, b, :].rearrange("p (g t) -> p g t", g=2)

        def wv(t, slot, cols, kc):
            return t[:, slot, 0:kc * cols].rearrange("p (k n) -> p k n", n=cols)

        total = [0]
        used = {}
        def load(E, slot, parts, size=BLK):
            E.eng.wait_ge(s_lo, E.next(s_lo))
            total[0] = E.m
            if E.i is None:
                used[E.m] = max(size, P * 8)
            for dst, src in parts:
                E.eng.dma_start(dst, src).then_inc(s_raw[slot], 16)

        def sp_cols(E, w, cols, kc):
            slot = E.slot()
            v, half = wv(raw, slot, cols, kc), kc // 2
            src = w.rearrange("(k p) n -> p k n", p=P)
            load(E, slot, [(v[:, 0:half, :], src[:, 0:half, :]), (v[:, half:, :], src[:, half:, :])], cols * kc)

        def sp_mlp(E, w1, w2):
            w1v = w1.rearrange("k (f n) -> f k n", n=512)
            w2v = w2.rearrange("(f r) n -> f r n", r=512)
            n = w1v.shape[0]
            sp_cols(E, w1v[0], 512, 8)
            with E.loop((n - 2) // 2, {s_lo: 4}) as i:
                for u in range(2):
                    sp_cols(E, w1v[2 * i + 1 + u], 512, 8)
                    sp_cols(E, w2v[2 * i + u], 1024, 4)
            sp_cols(E, w1v[n - 1], 512, 8)
            sp_cols(E, w2v[n - 2], 1024, 4)
            sp_cols(E, w2v[n - 1], 1024, 4)

        def sp_glu(E, w13, w2):
            full = F_GLU // 512
            gate = w13[:, 0:full * 512].rearrange("k (f n) -> f k n", n=512)
            up = w13[:, F_GLU:F_GLU + full * 512].rearrange("k (f n) -> f k n", n=512)
            down = w2[0:full * 512, :].rearrange("(f r) n -> f r n", r=512)

            def h(f):
                sp_cols(E, gate[f], 512, 8)
                sp_cols(E, up[f], 512, 8)
            h(0)
            with E.loop((full - 1) // 2, {s_lo: 6}) as i:
                for u in range(2):
                    h(2 * i + 1 + u)
                    sp_cols(E, down[2 * i + u], 1024, 4)
            slot = E.slot()
            v = wv(raw, slot, 512, 8)
            half = lambda at: w13[:, at + full * 512:at + F_GLU].rearrange("(k p) n -> p k n", p=P)
            load(E, slot, [(v[:, :, 0:256], half(0)), (v[:, :, 256:512], half(F_GLU))])
            sp_cols(E, down[full - 1], 1024, 4)
            sp_cols(E, w2[full * 512:, :], 1024, 2)

        def act_hi(E):
            if E.m >= total[0]:
                return
            slot = E.slot()
            E.eng.wait_ge(s_raw[slot], E.next(s_raw[slot], 32))
            n = BLK if E.i is not None else used.get(E.m, BLK)
            nc.scalar.activation(wh[:, slot, 0:n], raw[:, slot, 0:n], ACT.Copy).then_inc(s_hi, E.adds(s_hi))

        def dve_lo(E, mm=0):
            E.skip(s_mm, mm)
            if E.m >= total[0]:
                return
            slot = E.slot()
            E.eng.wait_ge(s_hi, E.next(s_hi))
            n = BLK if E.i is not None else used.get(E.m, BLK)
            nc.vector.tensor_tensor(wl[:, slot, 0:n], raw[:, slot, 0:n], wh[:, slot, 0:n].bitcast(F32), ALU.subtract).then_inc(s_lo, E.adds(s_lo))

        def mm3(o, wa, wb, xa, xb, start, stop):
            nc.tensor.matmul(o, wa, xa, start=start, stop=False)
            nc.tensor.matmul(o, wa, xb, start=False, stop=False)
            return nc.tensor.matmul(o, wb, xa, start=False, stop=stop)

        def pe_T(E, cols, kc, xa, xb, b0, width=S, more=None):
            slot = E.slot()
            E.eng.wait_ge(s_lo, E.next(s_lo))
            a, b = wv(wh, slot, cols, kc), wv(wl, slot, cols, kc)
            nm = cols // P
            for m in range(nm):
                o = ps[:, b0 + m // 2, (m % 2) * S:(m % 2) * S + width]
                for k in range(kc):
                    c = slice(m * P, (m + 1) * P)
                    last = mm3(o, a[:, k, c], b[:, k, c], xa[:, k], xb[:, k], k == 0 and not more, k == kc - 1 and (not more or (more == "last" and m % 2 == 1)))
                if m == nm - 1 or (m % 2 and not more):
                    last.then_inc(s_mm, E.adds(s_mm))

        def pe_rows(E, cols, kc, xa, xb, b0):
            slot = E.slot()
            E.eng.wait_ge(s_lo, E.next(s_lo))
            a, b = wv(wh, slot, cols, kc), wv(wl, slot, cols, kc)
            for q in range(NT):
                for k in range(kc):
                    t = slice(q * P, (q + 1) * P)
                    last = mm3(ps[:, b0 + q, 0:cols], xa[:, k, t], xb[:, k, t], a[:, k, :], b[:, k, :], k == 0, k == kc - 1)
                last.then_inc(s_mm, E.adds(s_mm))

        def act_copy(E, dsts, b0, hi=True):
            for n, dst in enumerate(dsts):
                E.eng.wait_ge(s_mm, E.next(s_mm))
                nc.scalar.activation(dst, bank(b0 + n) if len(dst.shape) == 3 else ps[:, b0 + n, :], ACT.Copy).then_inc(s_ev, E.adds(s_ev))
            if hi:
                act_hi(E)

        def act_stats(E, src, nch, wait=True, hi=False):
            if wait:
                E.eng.wait_ge(s_x, E.next(s_x))
            for h in range(0, nch, 4):
                n = min(4, nch - h)
                nc.scalar.activation(sq[:, h:h + n, :], src[:, h:h + n, :], ACT.Square).then_inc(s_sq, E.adds(s_sq))
            if hi:
                act_hi(E)
            E.eng.wait_ge(s_var, E.next(s_var))
            nc.scalar.activation(st[:, 1, :], st[:, 0, :], ACT.Sqrt).then_inc(s_rt, E.adds(s_rt))

        def pe_stats(E, nch, b=7, free=True):
            if free:
                pe_free(E)
            for h in range(0, nch, 4):
                n = min(4, nch - h)
                E.eng.wait_ge(s_sq, E.next(s_sq))
                for c in range(h, h + n):
                    last = nc.tensor.matmul(ps[:, b, 0:S], ones[:, :], sq[:, c, :], start=c == 0, stop=c == nch - 1)
            last.then_inc(s_ss, E.adds(s_ss))
            E.skip(s_var)

        def dve_stats(E, nch, b=7, lo=None):
            E.eng.wait_ge(s_ss, E.next(s_ss))
            nc.vector.tensor_scalar(st[:, 0, :], ps[:, b, 0:S], 1.0 / (nch * P), EPS, ALU.mult, ALU.add).then_inc(s_var, E.adds(s_var))
            if lo is not None:
                dve_lo(E, lo)
            E.eng.wait_ge(s_rt, E.next(s_rt))
            nc.vector.reciprocal(st[:, 1, :], st[:, 1, :]).then_inc(s_d, E.adds(s_d))
            E.eng.wait_ge(E.last, E.sofar(E.last))

        def dve_operand(E, src, gcol, nch, oh, ol, normed=True, tmp=None, later=False):
            tmp = tn if tmp is None else tmp
            if later:
                for c in range(nch):
                    nc.vector.tensor_scalar(tmp[:, c, :], src[:, c, :], gcol(c), None, ALU.mult).then_inc(s_u, E.adds(s_u))
                E.eng.wait_ge(s_u, E.sofar(s_u))
            elif normed:
                for c in range(nch):
                    nc.vector.scalar_tensor_tensor(out=tmp[:, c, :], in0=src[:, c, :], scalar=gcol(c), in1=st[:, 1, :],
                                                          op0=ALU.mult, op1=ALU.mult).then_inc(s_u, E.adds(s_u))
                E.eng.wait_ge(s_u, E.sofar(s_u))
            else:
                tmp = src
            for c in range(nch):
                E.eng.wait_ge(s_uh, E.next(s_uh))
                nc.vector.tensor_tensor(ol[:, c, :], tmp[:, c, :], oh[:, c, :].bitcast(F32), ALU.subtract).then_inc(s_op, E.adds(s_op))

        def act_operand(E, src, nch, oh, normed=True, tmp=None):
            tmp = (tn if tmp is None else tmp) if normed else src
            if not normed:
                E.eng.wait_ge(s_x, E.next(s_x))
            for c in range(nch):
                if normed:
                    E.eng.wait_ge(s_u, E.next(s_u))
                nc.scalar.activation(oh[:, c, :], tmp[:, c, :], ACT.Copy).then_inc(s_uh, E.adds(s_uh))
            E.skip(s_op, nch)

        def dve_residual(E, gcol, src=yT):
            for c in range(DC):
                nc.vector.scalar_tensor_tensor(out=tn[:, c, :], in0=src[:, c, :], scalar=gcol(c), in1=st[:, 1, :],
                                                      op0=ALU.mult, op1=ALU.mult).then_inc(s_d, E.adds(s_d))
            E.eng.wait_ge(s_d, E.sofar(s_d))
            nc.vector.tensor_tensor(xT[:, :, :], xT[:, :, :], tn[:, :, :], ALU.add).then_inc(s_x, E.adds(s_x))
            E.eng.wait_ge(s_x, E.sofar(s_x))

        yps = ps[:, 4:8, :].rearrange("p b (g t) -> p (b g) t", g=2)

        rstd = lambda n: st[:, 1, :].unsqueeze(1).to_broadcast([P, n, S])

        def pe_h(E, buf):
            pe_T(E, 512, 8, ah, al, 2 * buf)

        def pe_zero(E):
            for b in range(4, 8):
                nc.tensor.matmul(bank(b), mask[0:1, 0:P], mask[0:1, :].unsqueeze(1).to_broadcast([1, 2, S]), start=True, stop=False)

        def pe_y(E, buf, kc, n_op, last=False):
            E.eng.wait_ge(s_op, E.next(s_op, n_op))
            pe_T(E, 1024, kc, hh[:, buf], hl[:, buf], 4, more="last" if last else "on")

        def act_h(E, buf):
            for n in range(2):
                E.eng.wait_ge(s_u, E.next(s_u))
                nc.scalar.activation(hh[:, buf, 2 * n:2 * n + 2, :], rr[:, n], ACT.Square).then_inc(s_uh, E.adds(s_uh))
            E.skip(s_mm, 2)
            E.skip(s_op, 2)
            act_hi(E)

        def act_y(E, last=False):
            E.eng.wait_ge(s_mm, E.next(s_mm))
            if not last:
                act_hi(E)

        def dve_h(E, buf):
            for n in range(2):
                E.eng.wait_ge(s_mm, E.next(s_mm))
                if n == 0:
                    E.eng.wait_ge(s_op, E.sofar(s_op))
                nc.vector.scalar_tensor_tensor(out=rr[:, n], in0=bank(2 * buf + n), scalar=0.0, in1=rstd(2), op0=ALU.max, op1=ALU.mult).then_inc(s_u, E.adds(s_u))
            for n in range(2):
                E.eng.wait_ge(s_uh, E.next(s_uh))
                nc.vector.tensor_tensor(rr[:, n], rr[:, n], rr[:, n], ALU.mult).then_inc(s_d, E.adds(s_d))
                E.eng.wait_ge(s_d, E.sofar(s_d))
                nc.vector.tensor_tensor(hl[:, buf, 2 * n:2 * n + 2, :], rr[:, n], hh[:, buf, 2 * n:2 * n + 2, :].bitcast(F32), ALU.subtract).then_inc(s_op, E.adds(s_op))
            dve_lo(E)

        def dve_y(E, last=False):
            E.skip(s_mm)
            if not last:
                dve_lo(E)

        def ahead(E, n, h, y, per, norm=None):
            h(0)
            if norm is not None:
                norm()
            turns = (n - 2) // 2
            with E.loop(turns, per):
                h(1)
                y(0, False)
                h(0)
                y(1, False)
            for f in range(2 * turns, n - 1):
                h((f + 1) % 2)
                y(f % 2, False)
            y((n - 1) % 2, True)

        v4 = vv.rearrange("p q (j n) -> p q j n", n=P)
        o4 = orow.rearrange("p q (j n) -> p q j n", n=P)
        nm, sums, rs = view(sm, 0, [P, 2, 2]), view(sm, 4, [P, 2, 2]), view(sm, 8, [P, 2, 2])
        lamn = view(sm, 12, [P, 2])
        lamL = [0]
        gates = view(sm, 16, [P, NT, 48])
        g6 = gates.rearrange("p q (j c b) -> p q j c b", c=2, b=3)
        COLS = ((0, P), (P, 384))

        def pe_scores(E, fox=None):
            E.eng.wait_ge(s_stg, E.next(s_stg))
            if E.seen(s_scd):
                E.eng.wait_ge(s_scd, E.sofar(s_scd))
            for c in range(2):
                lo = slice(64 * c, 64 * c + 64)
                for q, (a, b) in enumerate(COLS):
                    o, keys = ps[:, c, a:b], slice(0, b - a)
                    if fox is not None:
                        nc.tensor.matmul(o, ones[:, :], fcm[:, 2 * fox + c, keys], start=True, stop=False)
                    last = nc.tensor.matmul(o, stg[lo, 0, q * P:(q + 1) * P], stg[lo, 1, keys], start=fox is None, stop=True)
                last.then_inc(s_sc, E.adds(s_sc))
            E.skip(s_scd, 2)

        def pe_values(E, j, shared, wide=64, v=None):
            E.eng.wait_ge(s_e, E.next(s_e))
            for c in range(2):
                for n in range(3):
                    last = nc.tensor.transpose(ps[:, 2 + c, n * P:(n + 1) * P], eb[:, c, n * P:(n + 1) * P], ident[:, :])
                last.then_inc(s_pt, E.adds(s_pt))
            if E.seen(s_od):
                E.eng.wait_ge(s_od, E.sofar(s_od))
            for c in range(2):
                E.eng.wait_ge(s_pc, E.next(s_pc))
                if v is not None:
                    val = lambda t: v(t, j, c)
                elif wide == P:
                    val = lambda t: vv[:, t, :].rearrange("p (h n) -> p h n", n=P)[:, 2 * j + c, :]
                else:
                    val = lambda t: v4[:, t, j, :] if shared else v4[:, t, j, 64 * c:64 * c + 64]
                w = P if shared else wide
                nc.tensor.matmul(ps[:, 4 + c, 0:w], ptb[:, c, 0:P], val(0), start=True, stop=True)
                nc.tensor.matmul(ps[:, 4 + c, P:P + w], ptb[:, c, P:2 * P], val(0), start=True, stop=False)
                last = nc.tensor.matmul(ps[:, 4 + c, P:P + w], ptb[:, c, 2 * P:], val(1), start=False, stop=True)
                last.then_inc(s_o, E.adds(s_o))
            E.skip(s_od, 2)

        def act_exp(E):
            E.eng.wait_ge(s_mx, E.next(s_mx))
            for c in range(2):
                for q, (a, b) in enumerate(COLS):
                    last = nc.scalar.activation(eb[:, c, a:b], scb[:, c, a:b], ACT.Exp, bias=nm[:, c, q:q + 1], accum_out=sums[:, c, q:q + 1])
            last.then_inc(s_e, E.adds(s_e))

        def act_pt(E):
            if E.seen(s_o):
                E.eng.wait_ge(s_o, E.sofar(s_o))
            for c in range(2):
                E.eng.wait_ge(s_pt, E.next(s_pt))
                nc.scalar.activation(ptb[:, c, :], ps[:, 2 + c, 0:384], ACT.Copy).then_inc(s_pc, E.adds(s_pc))
            E.skip(s_o, 2)

        def dve_stage(E, j, src=None):
            nc.vector.tensor_copy(stg[:, :, :], (qk if src is None else src)[:, j, :, :]).then_inc(s_stg, E.adds(s_stg))

        def dve_scale(E, j, table, scale):
            for c in range(2):
                E.eng.wait_ge(s_sc, E.next(s_sc))
                for a, b in COLS:
                    tab = bias[:, 2 * j + c, :] if table else mask[:, :]
                    tab = tab[:, S - (b - a):]
                    last = nc.vector.scalar_tensor_tensor(out=scb[:, c, a:b], in0=ps[:, c, a:b], scalar=scale, in1=tab, op0=ALU.mult, op1=ALU.add)
                last.then_inc(s_scd, E.adds(s_scd))
            E.eng.wait_ge(s_scd, E.sofar(s_scd))
            for q, (a, b) in enumerate(COLS):
                last = nc.vector.tensor_reduce(nm[:, :, q], scb[:, :, a:b], AX.X, ALU.max, negate=True)
            last.then_inc(s_mx, E.adds(s_mx))

        def dve_sums(E, j, kind, branch=0):
            E.eng.wait_ge(s_e, E.next(s_e))
            E.eng.wait_ge(E.last, E.sofar(E.last))
            nc.vector.reciprocal(rs[:, :, :], sums[:, :, :]).then_inc(s_d, E.adds(s_d))
            E.eng.wait_ge(s_d, E.sofar(s_d))
            if kind == "da":
                nc.vector.tensor_scalar(rs[:, 1, :], rs[:, 1, :], lamn[:, lamL[0]:lamL[0] + 1], None, ALU.mult).then_inc(s_d, E.adds(s_d))
                E.eng.wait_ge(s_d, E.sofar(s_d))
            if kind == "nsa":
                nc.vector.tensor_tensor(rs[:, :, :], rs[:, :, :], g6[:, :, j, :, branch].rearrange("p q c -> p c q"), ALU.mult).then_inc(s_d, E.adds(s_d))
                E.eng.wait_ge(s_d, E.sofar(s_d))

        def dve_out(E, j, kind, add=False, wide=64):
            for c in range(2):
                E.eng.wait_ge(s_o, E.next(s_o))
                for q in range(NT):
                    w = P if kind == "da" else wide
                    if kind == "da":
                        o = o4[:, q, j, :]
                    elif wide == P:
                        o = orow[:, q, :].rearrange("p (h n) -> p h n", n=P)[:, 2 * j + c, :]
                    else:
                        o = o4[:, q, j, 64 * c:64 * c + 64]
                    src = ps[:, 4 + c, q * P:q * P + w]
                    if add or (kind == "da" and c):
                        last = nc.vector.scalar_tensor_tensor(out=o, in0=src, scalar=rs[:, c, q:q + 1], in1=o, op0=ALU.mult, op1=ALU.add)
                    else:
                        last = nc.vector.tensor_scalar(o, src, rs[:, c, q:q + 1], None, ALU.mult)
                last.then_inc(s_od, E.adds(s_od))
                if kind == "da" and c == 0:
                    E.eng.wait_ge(s_od, E.sofar(s_od))

        def pe_attention(E, n, shared=False, fox=False, wide=64, scores=pe_scores, v=None):
            f = (lambda j: j) if fox else (lambda j: None)
            scores(E, f(0))
            scores(E, f(1))
            pe_values(E, 0, shared, wide, v)
            with E.loop(n - 2, {s_stg: 1, s_scd: 2, s_sc: 2, s_e: 1, s_pt: 2, s_pc: 2, s_o: 2, s_od: 2}) as i:
                scores(E, f(i + 2))
                pe_values(E, i + 1, shared, wide, v)
            pe_values(E, n - 1, shared, wide, v)

        def act_attention(E, n):
            act_exp(E)
            act_pt(E)
            with E.loop(n - 1, {s_mx: 1, s_e: 1, s_pt: 2, s_pc: 2, s_o: 2}):
                act_exp(E)
                act_pt(E)

        def dve_attention(E, n, kind, scale, branch=0, src=None, table=True, wide=64, stage=dve_stage):
            add = branch > 0
            stage(E, 0, src)
            dve_scale(E, 0, table, scale)
            stage(E, 1, src)
            dve_sums(E, 0, kind, branch)
            per = {s_sc: 2, s_scd: 2, s_mx: 1, s_stg: 1, s_o: 2, s_od: 2, s_e: 1, s_d: 1 + (kind in ("da", "nsa"))}
            with E.loop(n - 2, per) as i:
                dve_scale(E, i + 1, table, scale)
                stage(E, i + 2, src)
                dve_out(E, i, kind, add, wide)
                dve_sums(E, i + 1, kind, branch)
            dve_scale(E, n - 1, table, scale)
            dve_out(E, n - 2, kind, add, wide)
            dve_sums(E, n - 1, kind, branch)
            dve_out(E, n - 1, kind, add, wide)

        def pe_turn(E, src=None, ready=None):
            src = orow if src is None else src
            if ready is None:
                E.eng.wait_ge(s_mix, E.next(s_mix))
            else:
                if E.seen(ready):
                    E.eng.wait_ge(ready, E.sofar(ready))
            for b in range(4):
                for c in (2 * b, 2 * b + 1):
                    for q in range(NT):
                        o = ps[:, b, (c % 2) * S + q * P:(c % 2) * S + (q + 1) * P]
                        last = nc.tensor.transpose(o, src[:, q, c * P:(c + 1) * P], ident[:, :])
                last.then_inc(s_tp, E.adds(s_tp))

        def act_turn(E, scale=1.0, oh=None):
            oh = ah if oh is None else oh
            for b in range(4):
                E.eng.wait_ge(s_tp, E.next(s_tp))
                for c in (2 * b, 2 * b + 1):
                    sc = scale(c) if callable(scale) else scale
                    last = nc.scalar.activation(oh[:, c, :], bank(b)[:, c % 2, :], ACT.Copy, scale=sc)
                last.then_inc(s_uh, E.adds(s_uh))
            E.skip(s_op, 4)

        def dve_turn(E, scale=1.0, oh=None, ol=None):
            oh, ol = (ah, al) if oh is None else (oh, ol)
            for b in range(4):
                E.eng.wait_ge(s_uh, E.next(s_uh))
                for c in (2 * b, 2 * b + 1):
                    sc = scale(c) if callable(scale) else scale
                    last = nc.vector.scalar_tensor_tensor(out=ol[:, c, :], in0=bank(b)[:, c % 2, :], scalar=sc, in1=oh[:, c, :].bitcast(F32),
                                                          op0=ALU.mult, op1=ALU.subtract)
                last.then_inc(s_op, E.adds(s_op))

        def pe_out(E, n_op):
            E.eng.wait_ge(s_op, E.next(s_op, n_op))
            pe_free(E)
            pe_T(E, 512, 8, ah, al, 0)
            pe_T(E, 512, 8, ah, al, 2)
            E.skip(s_ev, 4)

        def act_out(E, hi=True):
            act_copy(E, [yT[:, 0:2, :], yT[:, 2:4, :]], 0)
            act_copy(E, [yT[:, 4:6, :], yT[:, 6:8, :]], 2, hi)
            E.eng.wait_ge(s_ev, E.sofar(s_ev))

        def dve_out_splits(E, n=2):
            for _ in range(n):
                dve_lo(E, 2)

        def pe_free(E):
            for s in (s_ev, s_evd, s_var, s_scd, s_pc, s_od):
                if E.seen(s):
                    E.eng.wait_ge(s, E.sofar(s))

        xrow = view(ar, 0, [P, NT, D])
        grow = view(ar, 2048, [P, P])
        g2row = view(ar, 2176, [P, P])
        lrow = view(ar, 2304, [P, 512])
        lprod = view(ar, 2816, [P, 2, 2, 64])
        rel = view(sm, 144, [P, H64])
        crev = view(ar, 3088, [P, 512])
        brow = view(ar, 13312, [P, 512])
        lsum = view(sm, 120, [P, 2, 2])
        subl = view(sm, 124, [P, 2])
        G2 = {}
        packs, at = [], 0
        for name, n in (("da_subln", 2), ("ln_ffn1_2", 16), ("ln_mix_2", 16), ("ln_ffn2_2", 16), ("ssd_norm_2", 32),
                        ("q_lora_norm_2", 8), ("kv_lora_norm_2", 4), ("nsa_cmp_pe", 32)):
            G2[name] = at
            packs.append((name, at, n))
            at += n
        n2 = at
        flat = lambda ap: ap.rearrange({1: "a -> a", 2: "a b -> (a b)", 3: "a b c -> (a b c)", 4: "a b c d -> (a b c d)"}[len(ap.shape)])
        DA_L = [0, 3]

        def sp_start(E):
            e = E.eng
            e.dma_start(xrow[:, :, :], d["x"][0].rearrange("(q p) n -> p q n", p=P)).then_inc(s_const, 16)
            e.dma_start(ident[:, :], d["c_ident"]).then_inc(s_const, 16)
            e.dma_start(grow[:, :], flat(d["norm_g"]).rearrange("(r n) -> r n", n=P)).then_inc(s_const, 16)
            for name, at, n in packs:
                e.dma_start(g2row[at:at + n, :], flat(d[name]).rearrange("(r n) -> r n", n=P)).then_inc(s_const, 16)
            e.dma_start(rel[0:NB, :], d["rel_bias"]).then_inc(s_const, 16)
            e.dma_start(cinv[:, :], d["c_inv"]).then_inc(s_const, 16)
            e.dma_start(crev[0:NB + 1, :], d["c_rev"]).then_inc(s_const, 16)
            e.dma_start(mask[:, :], d["c_mask"]).then_inc(s_const, 16)
            e.dma_start(lrow[:, :], flat(d["da_lambda"]).partition_broadcast(P)).then_inc(s_const, 16)
            e.dma_start(bfc[0:H64, :], flat(d["fox_b_f"]).rearrange("(h a) -> h a", a=1)).then_inc(s_const, 16)
            e.dma_start(cmaskv[:, :, :], d["c_cmask"].rearrange("p (q n) -> p q n", q=NT)).then_inc(s_const, 16)
            for n, w2 in enumerate((cw2k, cw2v)):
                e.dma_start(w2[:, :, :], d["nsa_cmp_w2"][0, n].rearrange("(k p) n -> p k n", p=P)).then_inc(s_const, 16)
            e.dma_start(flip[:, :], d["c_flip"]).then_inc(s_const, 16)
        n_const = 16 * (13 + len(packs))
        flip = view(ar, 10240, [P, P])
        bfc = view(sm, 126, [P, 1])
        cmaskv = view(sm, 220, [P, NT, 16])
        cw2k, cw2v = view(sm, 256, [P, 2, 64]), view(sm, 384, [P, 2, 64])

        def pool_start(E):
            e = E.eng
            e.wait_ge(s_mixa, 1)
            e.dma_start(scratch, brow[0:H64, :]).then_inc(s_scr, 16)
            e.wait_ge(s_scr, 16)
            e.dma_start(bias[:, :, :], bass.AP(scratch.tensor, 0, [[1, P], [512, H64], [1, S]])).then_inc(s_rows, 16)
            e.wait_ge(s_mixa, 3)
            e.dma_start(bias_kept, bias.rearrange("p h k -> p (h k)")).then_inc(s_scr, 16)
            e.wait_ge(s_scr, 32)

        def pe_flip(E):
            E.eng.wait_ge(s_rows, E.next(s_rows, 16))
            pe_free(E)
            for b in range(8):
                nc.tensor.matmul(ps[:, b, :], flip[:, :], bias[:, 2 * b:2 * b + 2, :].rearrange("p h k -> p (h k)"), start=True, stop=True).then_inc(s_tp, E.adds(s_tp))
            E.eng.wait_ge(s_mixa, E.next(s_mixa))

        def act_flip(E):
            for b in range(8):
                E.eng.wait_ge(s_tp, E.next(s_tp))
                last = nc.scalar.activation(bias[:, 2 * b:2 * b + 2, :], bank(b), ACT.Copy)
            last.then_inc(s_mixa, E.adds(s_mixa))

        def pe_start(E):
            E.eng.wait_ge(s_const, E.next(s_const, n_const))
            E.eng.wait_ge(s_g, E.next(s_g))
            for b in range(4):
                for c in (2 * b, 2 * b + 1):
                    for q in range(NT):
                        o = ps[:, b, (c % 2) * S + q * P:(c % 2) * S + (q + 1) * P]
                        last = nc.tensor.transpose(o, xrow[:, q, c * P:(c + 1) * P], ident[:, :])
                last.then_inc(s_tp, E.adds(s_tp))
            nc.tensor.transpose(ps[:, 4, 0:P], grow[:, :], ident[:, :])
            nc.tensor.transpose(ps[:, 4, P:P + n2], g2row[0:n2, :], ident[0:n2, 0:n2]).then_inc(s_tp, E.adds(s_tp))
            nc.tensor.matmul(ps[0:H64, 5, :], rel[0:NB + 1, :], crev[0:NB + 1, :], start=True, stop=True).then_inc(s_tp, E.adds(s_tp))
            E.skip(s_ev, 4)
            E.skip(s_evd)
            E.skip(s_lo, 2)
            E.skip(s_mix)
            E.skip(s_mixa, 2)

        def act_start(E):
            for b in range(4):
                E.eng.wait_ge(s_tp, E.next(s_tp))
                nc.scalar.activation(xT[:, 2 * b:2 * b + 2, :], bank(b), ACT.Copy).then_inc(s_ev, E.adds(s_ev))
            E.eng.wait_ge(s_tp, E.next(s_tp))
            nc.scalar.activation(gT[:, :], ps[:, 4, 0:P], ACT.Copy)
            nc.scalar.activation(g2[:, 0:n2], ps[:, 4, P:P + n2], ACT.Copy).then_inc(s_a, E.adds(s_a))
            E.eng.wait_ge(s_tp, E.next(s_tp))
            nc.scalar.activation(brow[0:H64, :], ps[0:H64, 5, :], ACT.Copy).then_inc(s_mixa, E.adds(s_mixa))
            E.eng.wait_ge(s_mix, E.next(s_mix))
            nc.scalar.activation(lsum[:, :, :], lsum[:, :, :], ACT.Exp).then_inc(s_mixa, E.adds(s_mixa))
            act_hi(E)
            act_hi(E)
            E.eng.wait_ge(s_ev, E.sofar(s_ev))

        def dve_start(E):
            nc.vector.memset(ones[:, :], 1.0)
            nc.vector.memset(rel[NB:NB + 1, :], 1.0).then_inc(s_g, E.adds(s_g))
            for slot in range(2):
                nc.vector.memset(raw[:, slot, :], 0.0).then_inc(s_lo, E.adds(s_lo))
            nc.vector.memset(st[:, :, :], 0.0).then_inc(s_evd, E.adds(s_evd))
            E.eng.wait_ge(s_const, E.next(s_const, n_const))
            lv = lrow.rearrange("p (l a b n) -> p l a b n", l=2, a=2, b=2)
            nc.vector.tensor_tensor(lprod[:, :, :, :], lv[:, :, :, 0, :], lv[:, :, :, 1, :], ALU.mult).then_inc(s_d, E.adds(s_d))
            E.eng.wait_ge(E.last, E.sofar(E.last))
            nc.vector.tensor_reduce(lsum[:, :, :], lprod[:, :, :, :], AX.X, ALU.add).then_inc(s_mix, E.adds(s_mix))
            E.eng.wait_ge(s_mixa, E.next(s_mixa, 2))
            for n, layer in enumerate(DA_L):
                nc.vector.tensor_scalar(lamn[:, n:n + 1], lsum[:, n, 1:2], lsum[:, n, 0:1], -LAM_INIT[layer], ALU.subtract, ALU.add).then_inc(s_d, E.adds(s_d))
                nc.vector.tensor_scalar(subl[:, n:n + 1], g2[:, n:n + 1], 1.0 - LAM_INIT[layer], None, ALU.mult).then_inc(s_d, E.adds(s_d))
            dve_lo(E)
            dve_lo(E)

        g1 = lambda layer, which: (lambda c: gT[:, (layer * 4 + which) * DC + c:(layer * 4 + which) * DC + c + 1])
        gg = lambda name, layer, n: (lambda c: g2[:, G2[name] + layer * n + c:G2[name] + layer * n + c + 1])

        def sp_da(E, k):
            w = d["da_w_in"][k].rearrange("k (a n) -> a k n", n=512)
            with E.loop(2, {s_lo: 2}) as i:
                for b in range(2):
                    sp_cols(E, w[2 * i + b], 512, 8)
            for b in range(2):
                sp_cols(E, w[4 + b], 512, 8)
            sp_out(E, d["da_w_out"][k])

        def sp_out(E, w):
            for b in range(2):
                sp_cols(E, w[:, 512 * b:512 * b + 512], 512, 8)

        def pe_qkv(E):
            E.eng.wait_ge(s_op, E.next(s_op, 8))
            pe_free(E)
            with E.loop(2, {s_lo: 2, s_mm: 4, s_ev: 4}):
                for b in range(2):
                    if E.seen(s_ev, 2):
                        E.eng.wait_ge(s_ev, E.sofar(s_ev, 2))
                    pe_T(E, 512, 8, ah, al, 2 * b)
                    E.skip(s_ev, 2)
            for b in range(2):
                if E.seen(s_ev, 2):
                    E.eng.wait_ge(s_ev, E.sofar(s_ev, 2))
                pe_rows(E, 512, 8, ah, al, 2 * b)
                E.skip(s_ev, 2)

        def act_qkv(E):
            with E.loop(2, {s_mm: 4, s_ev: 4, s_raw[0]: 32, s_raw[1]: 32, s_hi: 2}) as i:
                for b in range(2):
                    act_copy(E, [qk[:, 4 * b:4 * b + 2, i, :], qk[:, 4 * b + 2:4 * b + 4, i, :]], 2 * b)
            for b in range(2):
                act_copy(E, [vv[:, q, 512 * b:512 * b + 512] for q in range(NT)], 2 * b)

        def dve_qkv(E):
            with E.loop(2, {s_hi: 2, s_lo: 2, s_mm: 4}):
                dve_lo(E, 2)
                dve_lo(E, 2)
            dve_lo(E, 2)
            dve_lo(E, 2)

        hs = view(sm, 128, [P, 16])
        osq = view(ar, 0, [P, 2048])

        def dve_subln(E):
            of = orow.rearrange("p q (h n) -> p (q h) n", n=P)
            E.eng.wait_ge(s_od, E.sofar(s_od))
            nc.vector.tensor_tensor(osq[:, :], yT[:, :, :].rearrange("p c t -> p (c t)"), yT[:, :, :].rearrange("p c t -> p (c t)"), ALU.mult).then_inc(s_d, E.adds(s_d))
            E.eng.wait_ge(E.last, E.sofar(E.last))
            nc.vector.tensor_reduce(hs[:, :], osq.rearrange("p (h n) -> p h n", n=P), AX.X, ALU.add).then_inc(s_d, E.adds(s_d))
            E.eng.wait_ge(E.last, E.sofar(E.last))
            nc.vector.tensor_scalar(hs[:, :], hs[:, :], 1.0 / P, EPS, ALU.mult, ALU.add).then_inc(s_mix, E.adds(s_mix))
            E.eng.wait_ge(s_mixa, E.next(s_mixa))
            nc.vector.reciprocal(hs[:, :], hs[:, :]).then_inc(s_d, E.adds(s_d))
            E.eng.wait_ge(E.last, E.sofar(E.last))
            nc.vector.tensor_tensor(of, of, hs[:, :].unsqueeze(2).to_broadcast([P, 16, P]), ALU.mult).then_inc(s_mix, E.adds(s_mix))

        def act_subln(E):
            E.eng.wait_ge(s_mix, E.next(s_mix))
            nc.scalar.activation(hs[:, :], hs[:, :], ACT.Sqrt).then_inc(s_mixa, E.adds(s_mixa))
            E.skip(s_mix)

        def sp_rest(E, layer):
            sp_mlp(E, d["mlp_w1"][layer], d["mlp_w2"][layer])
            E.eng.wait_ge(s_x, 3 * layer + 1)
            E.eng.dma_start(prow[:, :, :], d["p"][layer, 0].rearrange("(q p) n -> p q n", p=P)).then_inc(s_p, 16)
            for b in range(2):
                sp_cols(E, d["ple_gate_w"][layer][:, 512 * b:512 * b + 512], 512, 8)
            for b in range(2):
                sp_cols(E, d["ple_w"][layer][:, 512 * b:512 * b + 512], 512, 2)

        def pe_norm(E):
            pe_stats(E, DC, free=False)
            E.eng.wait_ge(s_var, E.sofar(s_var))
            pe_zero(E)

        def pe_rest(E):
            pe_stats(E, DC)
            E.eng.wait_ge(s_op, E.next(s_op, 8))
            pe_free(E)
            ahead(E, 8, lambda b: pe_h(E, b), lambda b, last: pe_y(E, b, 4, 2, last), {s_lo: 4, s_mm: 6, s_op: 4}, lambda: pe_norm(E))
            pe_stats(E, DC, 0)
            E.eng.wait_ge(s_p, E.next(s_p, 16))
            for c in range(2):
                for q in range(NT):
                    last = nc.tensor.transpose(ps[:, 1, c * S + q * P:c * S + (q + 1) * P], prow[:, q, c * P:(c + 1) * P], ident[:, :])
            last.then_inc(s_tp, E.adds(s_tp))
            E.eng.wait_ge(s_op, E.next(s_op, 1))
            E.eng.wait_ge(s_op, E.next(s_op, 8))
            pe_free(E)
            pe_T(E, 512, 8, ah, al, 0)
            pe_T(E, 512, 8, ah, al, 2)
            E.skip(s_ev, 4)
            pe_T(E, 512, 2, pT, pTl, 4)
            if E.seen(s_ev):
                E.eng.wait_ge(s_ev, E.sofar(s_ev))
            pe_T(E, 512, 2, pT, pTl, 0)
            E.skip(s_evd, 4)

        def act_rest(E):
            act_stats(E, yT, DC, False, True)
            act_operand(E, xT, DC, ah)
            act_stats(E, xT, DC)
            ahead(E, 8, lambda b: act_h(E, b), lambda b, last: act_y(E, last), {s_mm: 6, s_u: 4, s_uh: 4, s_op: 4, s_raw[0]: 64, s_raw[1]: 64, s_hi: 4})
            act_stats(E, yps, DC, False, True)
            E.eng.wait_ge(s_tp, E.next(s_tp))
            nc.scalar.activation(pT[:, :, :], bank(1), ACT.Copy).then_inc(s_uh, E.adds(s_uh))
            E.skip(s_op)
            act_operand(E, xT, DC, ah, False)
            for b in range(2):
                for n in range(2):
                    E.eng.wait_ge(s_mm, E.next(s_mm))
                    nc.scalar.activation(sg[:, 4 * b + 2 * n:4 * b + 2 * n + 2, :], bank(2 * b + n), ACT.Tanh, scale=0.5).then_inc(s_ev, E.adds(s_ev))
                act_hi(E)
            for b in range(2):
                E.eng.wait_ge(s_mm, E.next(s_mm, 2))
                act_hi(E)

        def dve_rest(E, layer):
            dve_stats(E, DC, lo=2)
            dve_residual(E, g1(layer, 1))
            dve_operand(E, xT, g1(layer, 2), DC, ah, al, later=True)
            dve_stats(E, DC)
            ahead(E, 8, lambda b: dve_h(E, b), lambda b, last: dve_y(E, last), {s_uh: 4, s_d: 4, s_u: 4, s_op: 4, s_mm: 6, s_hi: 4, s_lo: 4})
            dve_stats(E, DC, 0, lo=0)
            dve_residual(E, g1(layer, 3), yps)
            E.eng.wait_ge(s_uh, E.next(s_uh))
            nc.vector.tensor_tensor(pTl[:, :, :], bank(1), pT[:, :, :].bitcast(F32), ALU.subtract).then_inc(s_op, E.adds(s_op))
            dve_operand(E, xT, None, DC, ah, al, normed=False)
            dve_lo(E, 2)
            dve_lo(E, 2)
            nc.vector.tensor_scalar(sg[:, :, :], sg[:, :, :], 0.5, 0.5, ALU.mult, ALU.add).then_inc(s_d, E.adds(s_d))
            E.eng.wait_ge(E.last, E.sofar(E.last))
            for b in range(2):
                for n in range(2):
                    E.eng.wait_ge(s_mm, E.next(s_mm))
                    c = 4 * b + 2 * n
                    nc.vector.tensor_tensor(sg[:, c:c + 2, :], sg[:, c:c + 2, :], bank(4 + n if b == 0 else n), ALU.mult).then_inc(s_evd, E.adds(s_evd))
                dve_lo(E)
            E.eng.wait_ge(s_evd, E.sofar(s_evd))
            nc.vector.tensor_tensor(xT[:, :, :], xT[:, :, :], sg[:, :, :], ALU.add).then_inc(s_x, E.adds(s_x))
            E.eng.wait_ge(s_x, E.sofar(s_x))

        onesw = ones[:, 0:1].to_broadcast([P, S])
        fx = view(ar, 10240, [P, S])
        fm = view(ar, 10496, [P, S])
        fn = view(ar, 10752, [P, S])
        fc = view(ar, 11008, [P, S])

        def sp_fox(E):
            w = d["fox_w_in"][0][:, 0:3072].rearrange("k (a n) -> a k n", n=512)
            with E.loop(2, {s_lo: 2}) as i:
                for b in range(2):
                    sp_cols(E, w[2 * i + b], 512, 8)
            for b in range(2):
                sp_cols(E, w[4 + b], 512, 8)
            sp_cols(E, d["fox_w_in"][0][:, 3072:3088], 16, 8)
            sp_out(E, d["fox_w_out"][0])

        def pe_narrow(E, cols, kc, xa, xb, b, at=0):
            slot = E.slot()
            E.eng.wait_ge(s_lo, E.next(s_lo))
            for k in range(kc):
                c = slice(k * cols, k * cols + P)
                last = mm3(ps[:, b, at:at + S], wh[:, slot, c], wl[:, slot, c], xa[:, k], xb[:, k], k == 0, k == kc - 1)
            last.then_inc(s_mm, E.adds(s_mm))

        def pe_fox(E):
            pe_qkv(E)
            if E.seen(s_ev):
                E.eng.wait_ge(s_ev, E.sofar(s_ev))
            pe_narrow(E, 16, 8, ah, al, 0)
            E.skip(s_ev)
            E.skip(s_mix)
            E.skip(s_mixa)
            pe_attention(E, 8, fox=True)
            pe_turn(E, ready=s_od)

        def act_fox(E):
            act_qkv(E)
            E.eng.wait_ge(s_mm, E.next(s_mm))
            nc.scalar.activation(fx[0:H64, :], ps[0:H64, 0, 0:S], ACT.Identity, bias=bfc[0:H64, :]).then_inc(s_ev, E.adds(s_ev))
            act_hi(E)
            E.eng.wait_ge(s_mix, E.next(s_mix))
            nc.scalar.activation(fn[0:H64, :], fn[0:H64, :], ACT.Exp).then_inc(s_a, E.adds(s_a))
            E.eng.wait_ge(E.last, E.sofar(E.last))
            nc.scalar.activation(fn[0:H64, :], fn[0:H64, :], ACT.Ln, bias=1.0).then_inc(s_mixa, E.adds(s_mixa))
            act_attention(E, 8)
            act_turn(E)

        def dve_fox(E):
            dve_qkv(E)
            dve_lo(E, 1)
            h = slice(0, H64)
            nc.vector.tensor_scalar(fm[h, :], fx[h, :], 0.0, None, ALU.min).then_inc(s_d, E.adds(s_d))
            nc.vector.scalar_tensor_tensor(out=fn[h, :], in0=fx[h, :], scalar=-1.0, in1=fx[h, :], op0=ALU.mult, op1=ALU.min).then_inc(s_mix, E.adds(s_mix))
            E.eng.wait_ge(s_mixa, E.next(s_mixa))
            nc.vector.tensor_tensor(fm[h, :], fm[h, :], fn[h, :], ALU.subtract).then_inc(s_d, E.adds(s_d))
            E.eng.wait_ge(E.last, E.sofar(E.last))
            nc.vector.memset(fc[:, :], 0.0).then_inc(s_d, E.adds(s_d))
            E.eng.wait_ge(E.last, E.sofar(E.last))
            nc.vector.tensor_tensor_scan(fc[h, :], onesw[h, :], fm[h, :], 0.0, ALU.mult, ALU.add).then_inc(s_d, E.adds(s_d))
            E.eng.wait_ge(E.last, E.sofar(E.last))
            nc.vector.tensor_scalar(fc[h, :], fc[h, :], -8.0, None, ALU.mult).then_inc(s_d, E.adds(s_d))
            E.eng.wait_ge(E.last, E.sofar(E.last))
            E.eng.wait_ge(s_scr, E.next(s_scr, 32))
            nc.vector.tensor_tensor(fcm[:, :, :], fc[:, :].unsqueeze(1).to_broadcast([P, H64, S]),
                                           ident[:, 0:H64].unsqueeze(2).to_broadcast([P, H64, S]), ALU.mult).then_inc(s_d, E.adds(s_d))
            dve_attention(E, 8, "fox", 0.125, table=False)
            dve_turn(E)

        def pool_bias_again(E):
            E.eng.wait_ge(s_x, 3 * 2 + 1)
            E.eng.dma_start(bias.rearrange("p h k -> p (h k)"), bias_kept).then_inc(s_rows, 16)

        qn = lambda c: qk[:, c, 0, :]
        vsel = view(ar, 4096, [P, NT, DC, 64])
        vwin = view(ar, 5120, [P, NT, DC, 64])
        kwin = view(ar, 13056, [P, 4, S])
        kk = [view(ar, 10240, [P, 4, 16, 16]), view(ar, 11264, [P, 4, 16, 16])]
        yf = yT[:, :, :].rearrange("p c t -> p (c t)")
        gat = yf[:, 0:960].rearrange("p (a n) -> p a n", a=16)
        gu, gz, ge = (yf[:, 960 + 240 * k:1200 + 240 * k].rearrange("p (v m n) -> p v m n", v=2, m=2) for k in range(3))
        fwd = ar_fwd = view(ar, 12544, [P, 480])
        gah, gal = view(ar_r, 0, [P, 16, 60]), view(ar_r, 1024, [P, 16, 60])
        kcT = view(sm, 160, [P, 60])
        vbd = view(ar, 10240, [P, 4, 4, 64])
        pc = view(ar, 11264, [P, 32, 32])
        pcT = view(ar, 12288, [P, 4, P])
        cmx, csm = view(ar, 12800, [P, 32]), view(ar, 12832, [P, 32])

        def sp_nsa(E):
            w = d["nsa_w_in"][0]
            E.eng.wait_ge(s_x, 1)
            E.eng.dma_start(fwd[0:NB + 1, :], d["c_fwd"][:, 0:480]).then_inc(s_fwd, 16)
            for b in range(3):
                sp_cols(E, w[:, 512 * b:512 * b + 512], 512, 8)
            for a in (1536, 1792):
                slot = E.slot()
                v = wv(raw, slot, 512, 8)
                src = w.rearrange("(k p) n -> p k n", p=P)
                load(E, slot, [(v[:, :, 256 * n:256 * n + 256], src[:, :, a + 512 * n:a + 512 * n + 256]) for n in range(2)])
            sp_cols(E, w[:, 2560:2608], 48, 8)
            for n in range(2):
                sp_cols(E, d["nsa_cmp_w1"][0, n], 256, 16)
            sp_out(E, d["nsa_w_out"][0])

        def pe_nsa(E):
            E.eng.wait_ge(s_op, E.next(s_op, 8))
            pe_free(E)
            for b in range(2):
                pe_T(E, 512, 8, ah, al, 2 * b)
                E.skip(s_ev, 2)
            for b, f in enumerate((pe_T, pe_T, pe_rows, pe_rows)):
                if E.seen(s_ev, 2):
                    E.eng.wait_ge(s_ev, E.sofar(s_ev, 2))
                f(E, 48 if b == 3 else 512, 8, ah, al, 2 * (b % 2))
                E.skip(s_ev, 2)
            for n in range(2):
                E.eng.wait_ge(s_op, E.next(s_op))
                if E.seen(s_ev):
                    E.eng.wait_ge(s_ev, E.sofar(s_ev))
                pe_T(E, 256, 16, gah, gal, 2 * n, 60)
                E.skip(s_ev)
            E.skip(s_mix)
            E.eng.wait_ge(s_mix, E.next(s_mix))
            E.eng.wait_ge(s_fwd, E.next(s_fwd, 16))
            for k in range(2):
                for half in range(2):
                    nc.tensor.matmul(ps[64 * half:64 * half + 64, 4, 0:60], cw2k[:, k, :], ge[:, 0, k, :], start=k == 0, stop=k == 1, skip_group_check=True)
            for g in range(4):
                for k in range(2):
                    nc.tensor.matmul(ps[0:NCMP, 5, 64 * g:64 * g + 64], ge[:, 1, k, g::4], cw2v[:, k, :], start=k == 0, stop=k == 1)
            for q in range(NT):
                for n in range(NCMP):
                    a = 255 + P * q - 31 - 16 * n
                    last = nc.tensor.matmul(ps[:, 6 + q, 16 * n:16 * n + 16], fwd[0:NB + 1, a:a + P], rel[0:NB + 1, :], start=True, stop=True)
            last.then_inc(s_mixp, E.adds(s_mixp))
            E.eng.wait_ge(s_mixa, E.next(s_mixa, 2))
            for q in range(NT):
                for h in range(H64):
                    lo, a = slice(64 * (h % 2), 64 * (h % 2) + 64), (q * 8 + h // 2) * 16
                    last = nc.tensor.matmul(ps[:, h % 2, a:a + NCMP], qn(h // 2)[lo, q * P:(q + 1) * P], kcT[lo, h // 4::4], start=True, stop=True)
            last.then_inc(s_mixp, E.adds(s_mixp))
            E.skip(s_mix, 2)
            E.skip(s_mixa)
            for q in range(NT):
                if q:
                    E.eng.wait_ge(s_mix, E.next(s_mix))
                else:
                    if E.seen(s_mix):
                        E.eng.wait_ge(s_mix, E.sofar(s_mix))
                for g in range(4):
                    last = nc.tensor.transpose(ps[:, 5, g * P:(g + 1) * P], pc[:, q * 16 + 4 * g:q * 16 + 4 * g + 4, :].rearrange("p h n -> p (h n)"), ident[:, :])
                last.then_inc(s_mixp, E.adds(s_mixp))
                E.eng.wait_ge(s_mixa, E.next(s_mixa))
                for g in range(4):
                    last = nc.tensor.matmul(ps[:, 6 + g // 2, (g % 2) * S:(g % 2) * S + S], pcT[:, g, :], vbd[:, g, :, :].rearrange("p h n -> p (h n)"), start=True, stop=True)
                last.then_inc(s_mixp, E.adds(s_mixp))
            E.skip(s_mix)
            for v in (vsel, vwin):
                pe_attention(E, 8, v=lambda t, j, c: v[:, t, j, :])
            pe_turn(E, ready=s_od)

        def act_nsa(E):
            act_copy(E, [qk[:, 0:2, 0, :], qk[:, 2:4, 0, :]], 0)
            act_copy(E, [qk[:, 4:6, 0, :], qk[:, 6:8, 0, :]], 2)
            for v in range(2):
                E.eng.wait_ge(s_mm, E.next(s_mm))
                dst = kk[v].rearrange("p g a b -> p g (a b)")
                for g in range(4):
                    src = ps[64 * (g % 2):64 * (g % 2) + 64, v, S * (g // 2):S * (g // 2) + S]
                    nc.scalar.activation(dst[0:64, g, :], src, ACT.Copy)
                    last = nc.scalar.activation(dst[64:P, g, 0:S - 1], src[:, 1:S], ACT.Copy)
                last.then_inc(s_ev, E.adds(s_ev))
            act_hi(E)
            for v in range(2):
                E.eng.wait_ge(s_mm, E.next(s_mm))
                for g in range(4):
                    src = ps[64 * (g % 2):64 * (g % 2) + 64, 2 + v, S * (g // 2):S * (g // 2) + S]
                    for half in (slice(0, 64), slice(64, P)):
                        if v == 0:
                            for r in range(2):
                                last = nc.scalar.activation(qk[half, 2 * g + r, 1, :], src, ACT.Copy)
                        else:
                            last = nc.scalar.activation(kwin[half, g, :], src, ACT.Copy)
                last.then_inc(s_ev, E.adds(s_ev))
            act_hi(E)
            for q in range(NT):
                E.eng.wait_ge(s_mm, E.next(s_mm))
                for v, dst in enumerate((vsel, vwin)):
                    for r in range(2):
                        last = nc.scalar.activation(dst[:, q].rearrange("p (g r) n -> p g r n", r=2)[:, :, r, :],
                                                    ps[:, q, S * v:S * v + S].rearrange("p (g n) -> p g n", g=4), ACT.Copy)
                last.then_inc(s_ev, E.adds(s_ev))
            act_hi(E)
            for q in range(NT):
                E.eng.wait_ge(s_mm, E.next(s_mm))
                nc.scalar.activation(gates[:, q, :], ps[:, 2 + q, 0:48], ACT.Exp, scale=-1.0).then_inc(s_ev, E.adds(s_ev))
            act_hi(E)
            for n in range(2):
                E.eng.wait_ge(s_u, E.next(s_u))
                nc.scalar.activation(gah[:, :, :], gat, ACT.Copy).then_inc(s_uh, E.adds(s_uh))
                E.skip(s_op)
                E.eng.wait_ge(s_mm, E.next(s_mm))
                nc.scalar.activation(gu[:, n], bank(2 * n)[:, :, 0:60], ACT.Copy).then_inc(s_ev, E.adds(s_ev))
                act_hi(E)
            E.eng.wait_ge(s_mix, E.next(s_mix))
            nc.scalar.activation(ge, gz, ACT.Exp, scale=-2.0 * math.sqrt(2.0 / math.pi)).then_inc(s_mixa, E.adds(s_mixa))
            E.skip(s_mix)
            E.eng.wait_ge(s_mixp, E.next(s_mixp))
            nc.scalar.activation(kcT, ps[:, 4, 0:60], ACT.Copy)
            for q in range(NT):
                last = nc.scalar.activation(pc[:, 16 * q:16 * q + 16, 0:NCMP].rearrange("p h n -> p n h"),
                                            ps[:, 6 + q, 0:240].rearrange("p (n h) -> p n h", n=NCMP), ACT.Copy)
            last.then_inc(s_mixa, E.adds(s_mixa))
            E.skip(s_mixp)
            E.eng.wait_ge(s_mix, E.next(s_mix))
            nc.scalar.activation(pc[:, :, 0:NCMP], pc[:, :, 0:NCMP], ACT.Exp).then_inc(s_mixa, E.adds(s_mixa))
            E.skip(s_mix)
            for q in range(NT):
                E.eng.wait_ge(s_mixp, E.next(s_mixp))
                nc.scalar.activation(pcT[:, :, :], ps[:, 5, :].rearrange("p (g n) -> p g n", g=4), ACT.Copy).then_inc(s_mixa, E.adds(s_mixa))
                E.skip(s_mixp)
                E.skip(s_mix)
            for branch in range(2):
                act_attention(E, 8)
            act_turn(E)

        def dve_nsa(E):
            for mm in (2, 2, 2, 2, 2, 2):
                dve_lo(E, mm)
            nc.vector.tensor_scalar(gates[:, :, :], gates[:, :, :], 1.0, None, ALU.add).then_inc(s_d, E.adds(s_d))
            E.eng.wait_ge(E.last, E.sofar(E.last))
            nc.vector.reciprocal(gates[:, :, :], gates[:, :, :]).then_inc(s_d, E.adds(s_d))
            for v in range(2):
                for a in range(16):
                    src = kk[v][:, :, a // 8:a // 8 + NCMP, 2 * (a % 8)].rearrange("p g n -> p n g")
                    col = G2["nsa_cmp_pe"] + 16 * v + a
                    last = nc.vector.tensor_scalar(gat[:, a, :].rearrange("p (n g) -> p n g", g=4), src, g2[:, col:col + 1], None, ALU.add)
                last.then_inc(s_u, E.adds(s_u))
                E.eng.wait_ge(s_uh, E.next(s_uh))
                E.eng.wait_ge(s_u, E.sofar(s_u))
                nc.vector.tensor_tensor(gal[:, :, :], gat, gah[:, :, :].bitcast(F32), ALU.subtract).then_inc(s_op, E.adds(s_op))
                dve_lo(E, 1)
                E.eng.wait_ge(s_op, E.sofar(s_op))
            nc.vector.tensor_tensor(gz, gu, gu, ALU.mult).then_inc(s_d, E.adds(s_d))
            E.eng.wait_ge(E.last, E.sofar(E.last))
            nc.vector.tensor_scalar(gz, gz, 0.044715, 1.0, ALU.mult, ALU.add).then_inc(s_d, E.adds(s_d))
            E.eng.wait_ge(E.last, E.sofar(E.last))
            nc.vector.memset(vbd[:, :, :, :], 0.0)
            nc.vector.memset(pc[:, :, :], 0.0)
            nc.vector.tensor_tensor(gz, gz, gu, ALU.mult).then_inc(s_mix, E.adds(s_mix))
            E.eng.wait_ge(s_mixa, E.next(s_mixa))
            nc.vector.tensor_scalar(ge, ge, 1.0, None, ALU.add).then_inc(s_d, E.adds(s_d))
            E.eng.wait_ge(E.last, E.sofar(E.last))
            nc.vector.reciprocal(ge, ge).then_inc(s_d, E.adds(s_d))
            E.eng.wait_ge(E.last, E.sofar(E.last))
            nc.vector.tensor_tensor(ge, ge, gu, ALU.mult).then_inc(s_mix, E.adds(s_mix))
            E.eng.wait_ge(s_mixp, E.next(s_mixp))
            for h in range(4):
                last = nc.vector.tensor_copy(vbd[32 * h:32 * h + NCMP, :, h, :], ps[0:NCMP, 5, 0:S].rearrange("p (g n) -> p g n", g=4))
            last.then_inc(s_d, E.adds(s_d))
            E.eng.wait_ge(s_mixa, E.next(s_mixa))
            E.eng.wait_ge(s_mixp, E.next(s_mixp))
            p15 = pc[:, :, 0:NCMP]
            for c in range(2):
                half = pc.rearrange("p (a c) n -> p a c n", c=2)[:, :, c, 0:NCMP]
                last = nc.vector.scalar_tensor_tensor(out=half, in0=ps[:, c, 0:S].rearrange("p (h n) -> p h n", n=16)[:, :, 0:NCMP], scalar=0.125, in1=half,
                                                      op0=ALU.mult, op1=ALU.add)
            last.then_inc(s_d, E.adds(s_d))
            E.eng.wait_ge(E.last, E.sofar(E.last))
            nc.vector.tensor_reduce(cmx[:, :], p15, AX.X, ALU.max).then_inc(s_d, E.adds(s_d))
            E.eng.wait_ge(E.last, E.sofar(E.last))
            nc.vector.tensor_tensor(p15, p15, cmx[:, :].unsqueeze(2).to_broadcast([P, 32, NCMP]), ALU.subtract).then_inc(s_mix, E.adds(s_mix))
            E.eng.wait_ge(s_mixa, E.next(s_mixa))
            nc.vector.tensor_reduce(csm[:, :], p15, AX.X, ALU.add).then_inc(s_d, E.adds(s_d))
            E.eng.wait_ge(E.last, E.sofar(E.last))
            nc.vector.reciprocal(csm[:, :], csm[:, :]).then_inc(s_d, E.adds(s_d))
            E.eng.wait_ge(E.last, E.sofar(E.last))
            nc.vector.tensor_tensor(csm.rearrange("p (q h) -> p q h", q=NT), csm.rearrange("p (q h) -> p q h", q=NT),
                                           gates.rearrange("p q (h b) -> p q h b", b=3)[:, :, :, 0], ALU.mult).then_inc(s_d, E.adds(s_d))
            for q in range(NT):
                last = nc.vector.tensor_tensor(pc[:, 16 * q:16 * q + 16, 0:NCMP], pc[:, 16 * q:16 * q + 16, 0:NCMP],
                                               cmaskv[:, q, 0:NCMP].unsqueeze(1).to_broadcast([P, 16, NCMP]), ALU.mult)
            last.then_inc(s_d, E.adds(s_d))
            E.eng.wait_ge(E.last, E.sofar(E.last))
            nc.vector.tensor_tensor(p15, p15, csm[:, :].unsqueeze(2).to_broadcast([P, 32, NCMP]), ALU.mult).then_inc(s_mix, E.adds(s_mix))
            for q in range(NT):
                E.skip(s_mixa)
                E.skip(s_mixp)
                E.eng.wait_ge(s_mixp, E.next(s_mixp))
                nc.vector.tensor_copy(orow[:, q, :].rearrange("p (b n) -> p b n", b=2), ps[:, 6:8, :]).then_inc(s_mix, E.adds(s_mix))
            dve_attention(E, 8, "nsa", 0.125, branch=1)
            E.eng.wait_ge(E.last, E.sofar(E.last))
            for r in range(2):
                last = nc.vector.tensor_copy(qk.rearrange("p (g r) a t -> p g r a t", r=2)[:, :, r, 1, :], kwin[:, :, :])
            last.then_inc(s_d, E.adds(s_d))
            E.eng.wait_ge(E.last, E.sofar(E.last))
            dve_attention(E, 8, "nsa", 0.125, branch=2)
            dve_turn(E)

        def glu_order(h, y, loop):
            h(0, False)
            with loop:
                h(1, False)
                y(0, False)
                h(0, False)
                y(1, False)
            h(1, True)
            y(0, False)
            y(1, True)
        glu_turns = (F_GLU // 512 - 1) // 2

        def pe_glu(E):
            E.eng.wait_ge(s_op, E.next(s_op, 8))
            pe_free(E)
            norm = [False]

            def h(b, half):
                if E.seen(s_gt):
                    E.eng.wait_ge(s_gt, E.sofar(s_gt))
                if half:
                    E.eng.wait_ge(s_up, E.sofar(s_up))
                pe_T(E, 512, 8, ah, al, 0)
                if not norm[0]:
                    pe_norm(E)
                    norm[0] = True
                if not half:
                    if E.seen(s_up):
                        E.eng.wait_ge(s_up, E.sofar(s_up))
                    pe_T(E, 512, 8, ah, al, 2)
                E.skip(s_gt)
                E.skip(s_up)

            def y(b, half):
                E.eng.wait_ge(s_op, E.next(s_op))
                pe_T(E, 1024, 2 if half else 4, hh[:, b], hl[:, b], 4, more="last" if half else "on")
            glu_order(h, y, E.loop(glu_turns, {s_lo: 6, s_mm: 10, s_gt: 2, s_up: 2, s_op: 2}))

        tg = view(ar, 12288, [P, 4, S])
        gr = view(ar, 13312, [P, 4, S])

        def act_glu(E):
            def h(b, half):
                n = 1 if half else 2
                E.eng.wait_ge(s_gt, E.next(s_gt))
                nc.scalar.activation(tg[:, 0:2 * n, :], gr[:, 0:2 * n, :], ACT.Tanh, scale=0.5).then_inc(s_uh, E.adds(s_uh))
                E.skip(s_mm, n)
                if not half:
                    act_hi(E)
                E.eng.wait_ge(s_mm, E.next(s_mm, n))
                act_hi(E)
                E.eng.wait_ge(s_u, E.next(s_u))
                nc.scalar.activation(hh[:, b, 0:2 * n, :], gr[:, 0:2 * n, :], ACT.Copy).then_inc(s_uh, E.adds(s_uh))
                E.skip(s_op)
            glu_order(h, lambda b, half: act_y(E, half), E.loop(glu_turns, {s_mm: 10, s_uh: 4, s_u: 2, s_gt: 2, s_op: 2, s_raw[0]: 96, s_raw[1]: 96, s_hi: 6}))

        def dve_glu(E):
            def h(b, half):
                n = 1 if half else 2
                g, t = gr[:, 0:2 * n, :], tg[:, 0:2 * n, :]
                pv = lambda at: ps[:, at:at + n, :].rearrange("p b (g t) -> p (b g) t", g=2)
                E.eng.wait_ge(s_mm, E.next(s_mm, n))
                E.eng.wait_ge(s_op, E.sofar(s_op))
                nc.vector.tensor_tensor(g, pv(0), rstd(2 * n), ALU.mult).then_inc(s_gt, E.adds(s_gt))
                if not half:
                    dve_lo(E)
                E.eng.wait_ge(s_uh, E.next(s_uh))
                nc.vector.scalar_tensor_tensor(out=g, in0=t, scalar=1.0, in1=g, op0=ALU.add, op1=ALU.mult).then_inc(s_d, E.adds(s_d))
                E.eng.wait_ge(s_d, E.sofar(s_d))
                E.eng.wait_ge(s_mm, E.next(s_mm, n))
                nc.vector.tensor_tensor(t, pv(n), rstd(2 * n), ALU.mult).then_inc(s_up, E.adds(s_up))
                E.eng.wait_ge(s_up, E.sofar(s_up))
                nc.vector.scalar_tensor_tensor(out=g, in0=g, scalar=0.5, in1=t, op0=ALU.mult, op1=ALU.mult).then_inc(s_u, E.adds(s_u))
                dve_lo(E)
                E.eng.wait_ge(s_uh, E.next(s_uh))
                nc.vector.tensor_tensor(hl[:, b, 0:2 * n, :], g, hh[:, b, 0:2 * n, :].bitcast(F32), ALU.subtract).then_inc(s_op, E.adds(s_op))
            glu_order(h, lambda b, half: dve_y(E, half), E.loop(glu_turns, {s_uh: 4, s_d: 2, s_u: 2, s_op: 2, s_gt: 2, s_up: 2, s_mm: 10, s_hi: 6, s_lo: 6}))

        def pe_ffn(E):
            pe_glu(E)

        def act_ffn(E, hi):
            act_operand(E, xT, DC, ah)
            if hi:
                act_hi(E)
            act_stats(E, xT, DC)
            act_glu(E)

        def dve_ffn(E, name, layer, lo):
            dve_operand(E, xT, gg(name, layer, 8), DC, ah, al, later=True)
            if lo is not None:
                dve_lo(E, lo)
            dve_stats(E, DC)
            dve_glu(E)
            E.eng.wait_ge(s_mm, E.sofar(s_mm))
            nc.vector.scalar_tensor_tensor(out=xT[:, :, :], in0=yps, scalar=0.5, in1=xT[:, :, :], op0=ALU.mult, op1=ALU.add).then_inc(s_x, E.adds(s_x))
            E.eng.wait_ge(s_x, E.sofar(s_x))

        xs = view(ar, 0, [P, NT, 4, 512])
        bct = view(ar, 4096, [P, 2, 4, S])
        cin = view(ar, 6144, [P, 2, 2, 260])
        cout = view(ar, 7184, [P, 4, 2, S])
        cex = view(ar, 9232, [P, 2, 2, S])
        cbm = view(ar, 6784, [P, 2, P])
        stt = view(ar, 7040, [P, 512])
        am = view(ar, 7688, [P, 2, 8, P])
        ee = view(ar, 9736, [P, 2, 8, P])
        xdt = view(ar, 11784, [P, 2, 8, 64])
        xdw = view(ar, 12808, [P, 8, 64])
        brow2 = view(ar, 13320, [P, 4, P])
        rws = view(ar, 13832, [P, 6, 32])
        upper = view(ar, 14024, [P, P])
        crow = view(ar, 14152, [P, P])
        cw = view(sm, 16, [P, 120])
        dtb, alog = view(sm, 136, [P, 1]), view(sm, 137, [P, 1])
        dsk = view(sm, 138, [P, 32])
        qng, kng = view(sm, 172, [P, 192]), view(sm, 364, [P, 192])
        s16 = view(sm, 556, [P, 16])
        posi = sb("posi", [P, NT], I32)
        dx, dm, dn, acT, wsT, eaT = (yf[:, 256 * k:256 * k + 256] for k in range(6))
        zt = view(ar, 6144, [P, 4, 512])
        zsq = view(ar, 6144, [P, NT, 2048])
        bh, bl = view(ar_r, 0, [P, DC, S]), view(ar_r, 2048, [P, DC, S])
        mg = view(ar, 8192, [P, DC, S])
        ge8 = view(ar, 10240, [P, DC, S])

        def sp_second(E, layer):
            w = d["w_in_2"][layer]
            sp_glu(E, d["ffn1_w13_2"][layer], d["ffn1_w2_2"][layer])
            for b in range(2):
                sp_cols(E, w[:, O_XBC + 512 * b:O_XBC + 512 * b + 512], 512, 8)
            E.eng.wait_ge(s_x, 3 * DEPTH + 4 * layer + 1)
            sp_small(E, layer)
            xw = w[:, O_XBC:O_XBC + 3072].rearrange("k (a n) -> a k n", n=512)
            for b in range(2, 6):
                sp_cols(E, xw[b], 512, 8)
            sp_cols(E, w[:, O_DT:O_DT + 32], 32, 8)
            zw = w[:, O_Z:O_Z + 2048].rearrange("k (a n) -> a k n", n=512)
            with E.loop(2, {s_lo: 2}) as i:
                for b in range(2):
                    sp_cols(E, zw[2 * i + b], 512, 8)
            for h in range(2):
                sp_out(E, d["w_ssd_out_2"][layer][1024 * h:1024 * h + 1024, :])
            sp_out(E, w[:, O_G:O_G + D])
            sp_cols(E, w[:, O_CQ:O_CQ + 512], 512, 8)
            sp_cols(E, w[:, O_CKV:O_CKV + 320], 320, 8)
            for b in range(2):
                sp_cols(E, d["w_ukv_2"][layer][:, 1024 * b:1024 * b + 1024], 1024, 2)
            for b in range(3):
                sp_cols(E, d["w_uq_2"][layer][:, 512 * b:512 * b + 512], 512, 4)
            sp_out(E, d["w_mla_out_2"][layer])
            sp_out(E, w[:, O_G + D:O_G + 2 * D])
            sp_out(E, d["w_o_2"][layer])
            sp_glu(E, d["ffn2_w13_2"][layer], d["ffn2_w2_2"][layer])

        n_small = 16 * 10

        def sp_small(E, layer):
            e = E.eng
            for dst, src in ((crow[0:96, :], d["conv_w_2"][layer].rearrange("k (c n) -> (k c) n", n=P)),
                             (crow[96:120, :], d["conv_b_2"][layer].rearrange("(c n) -> c n", n=P)),
                             (dtb[0:32, :], d["dt_bias_2"][layer].rearrange("(h a) -> h a", a=1)),
                             (alog[0:32, :], d["a_log_2"][layer].rearrange("(h a) -> h a", a=1)),
                             (dsk[:, :], d["d_skip_2"][layer].partition_broadcast(P)),
                             (qng[:, :], d["q_norm_2"][layer].partition_broadcast(P)),
                             (kng[:, :], d["k_norm_2"][layer].partition_broadcast(P)),
                             (upper[:, :], d["c_upper"]),
                             (posi[:, 0:1], d["positions_2"][0, 0:P].rearrange("(p a) -> p a", a=1)),
                             (posi[:, 1:2], d["positions_2"][0, P:S].rearrange("(p a) -> p a", a=1))):
                e.dma_start(dst, src).then_inc(s_small, 16)

        def pe_ssd(E):
            E.eng.wait_ge(s_small, E.next(s_small, n_small))
            E.eng.wait_ge(s_op, E.next(s_op, 8))
            pe_free(E)
            nc.tensor.transpose(ps[:, 6, 0:120], crow[0:120, :], ident[0:120, 0:120]).then_inc(s_tp, E.adds(s_tp))

            def x_rows(i):
                E.eng.wait_ge(s_mix, E.next(s_mix))
                if i >= 2:
                    E.eng.wait_ge(s_xs, E.sofar(s_xs, 1))
                for q in range(NT):
                    for c in range(2):
                        last = nc.tensor.transpose(ps[:, 4 + i % 2, q * S + c * P:q * S + (c + 1) * P], cout[:, i % 4, c, q * P:(q + 1) * P], ident[:, :])
                last.then_inc(s_tp, E.adds(s_tp))
                E.skip(s_xs)
            for b in range(6):
                if b >= 2:
                    E.eng.wait_ge(s_cin, E.sofar(s_cin, 2))
                pe_T(E, 512, 8, ah, al, 2 * (b % 2))
                E.skip(s_cin, 2)
                if 1 <= b <= 4:
                    x_rows(2 * b - 2)
                    x_rows(2 * b - 1)
            E.eng.wait_ge(s_cin, E.sofar(s_cin))
            E.eng.wait_ge(s_xs, E.sofar(s_xs))
            pe_narrow(E, 32, 8, ah, al, 0)
            E.skip(s_ev)
            E.eng.wait_ge(s_mix, E.next(s_mix))
            for g in range(4):
                last = nc.tensor.transpose(ps[:, 6, g * P:(g + 1) * P], bct[:, 0, g, 0:P], ident[:, :])
            i32 = ident[0:32, 0:32]
            for n, src in enumerate((dn[0:32, 0:P], dn[0:32, P:S], acT[0:32, 0:P], acT[0:32, P:S], wsT[0:32, 0:P], eaT[0:32, 0:P])):
                last = nc.tensor.transpose(ps[:, 5, 32 * n:32 * n + 32], src, i32)
            last.then_inc(s_tp, E.adds(s_tp))
            for g in range(4):
                for q in range(NT):
                    t = slice(q * P, (q + 1) * P)
                    last = nc.tensor.matmul(ps[:, 0, t], bct[:, 0, g, t], bct[:, 1, g, t], start=True, stop=True)
                last.then_inc(s_sc, E.adds(s_sc))
                for q in range(NT):
                    E.eng.wait_ge(s_mix, E.next(s_mix))
                    for n in range(2):
                        last = nc.tensor.matmul(ps[:, 2 + 2 * q + n, :], ones[0:32, :], am[0:32, q, 4 * n:4 * n + 4, :].rearrange("p h t -> p (h t)"), start=True, stop=True)
                    last.then_inc(s_dec, E.adds(s_dec))
                E.skip(s_e, 2)
                for q in range(NT):
                    E.eng.wait_ge(s_scd, E.next(s_scd))
                    for h in range(8):
                        last = nc.tensor.matmul(ps[:, 6 + q, 64 * h:64 * h + 64], ee[:, q, h, :], xdt[:, q, h, :], start=True, stop=True)
                    if q == 0:
                        last.then_inc(s_o, E.adds(s_o))
                        nc.tensor.matmul(ps[:, 1, :], brow2[:, g, :], xdw.rearrange("p h n -> p (h n)"), start=True, stop=True).then_inc(s_mixp, E.adds(s_mixp))
                    else:
                        E.eng.wait_ge(s_pc, E.next(s_pc))
                        nc.tensor.matmul(ps[:, 1, :], bct[:, 1, g, P:S], stt[:, :], start=True, stop=True).then_inc(s_o, E.adds(s_o))
            E.skip(s_evd)
            pe_free(E)
            with E.loop(2, {s_lo: 2, s_mm: 4, s_evd: 4}):
                for b in range(2):
                    if E.seen(s_evd, 2):
                        E.eng.wait_ge(s_evd, E.sofar(s_evd, 2))
                    pe_rows(E, 512, 8, ah, al, 2 * b)
                    E.skip(s_evd, 2)
            E.skip(s_mix, 2)
            for h in range(2):
                if h == 0:
                    E.eng.wait_ge(s_mix, E.next(s_mix))
                if E.seen(s_evd):
                    E.eng.wait_ge(s_evd, E.sofar(s_evd))
                if E.seen(s_ev):
                    E.eng.wait_ge(s_ev, E.sofar(s_ev))
                pe_turn(E, xs[:, :, 2 * h:2 * h + 2, :].rearrange("p q a n -> p q (a n)"), ready=s_mix)
                E.eng.wait_ge(s_op, E.next(s_op, 4))
                pe_T(E, 512, 8, bh, bl, 0)
                pe_T(E, 512, 8, bh, bl, 2)
                if h:
                    E.skip(s_evd, 4)
                else:
                    E.skip(s_ev, 4)
            if E.seen(s_evd):
                E.eng.wait_ge(s_evd, E.sofar(s_evd))
            pe_T(E, 512, 8, ah, al, 0)
            pe_T(E, 512, 8, ah, al, 2)
            E.skip(s_ev, 4)

        def act_ssd(E):
            E.eng.wait_ge(s_tp, E.next(s_tp))
            nc.scalar.activation(cw[:, :], ps[:, 6, 0:120], ACT.Copy, scale=0.5).then_inc(s_mixa, E.adds(s_mixa))
            E.eng.wait_ge(s_mixa, E.sofar(s_mixa))
            for i in range(13):
                if i < 12:
                    src = bank(2 * (i // 2 % 2) + i % 2)
                    E.eng.wait_ge(s_mm, E.next(s_mm))
                    nc.scalar.activation(cin[:, i % 2, :, 3:259], src, ACT.Copy)
                    for c in range(2):
                        k = 2 * i + c
                        last = nc.scalar.activation(cout[:, i % 4, c, :], src[:, c, :], ACT.Identity, scale=cw[:, 72 + k:73 + k], bias=cw[:, 96 + k:97 + k])
                    last.then_inc(s_cin, E.adds(s_cin))
                    if i % 2:
                        act_hi(E)
                if i >= 1:
                    E.eng.wait_ge(s_u, E.next(s_u))
                    nc.scalar.activation(cex[:, (i - 1) % 2], cout[:, (i - 1) % 4], ACT.Tanh).then_inc(s_uh, E.adds(s_uh))
                if 2 <= i < 10:
                    E.eng.wait_ge(s_tp, E.next(s_tp))
                    c = i - 2
                    nc.scalar.activation(xs.rearrange("p q g n -> p q (g n)")[:, :, S * c:S * c + S], ps[:, 4 + i % 2, :].rearrange("p (q n) -> p q n", q=NT), ACT.Copy).then_inc(s_xs, E.adds(s_xs))
            E.skip(s_mix, 8)
            E.eng.wait_ge(s_mm, E.next(s_mm))
            nc.scalar.activation(dx[0:32, :], ps[0:32, 0, 0:S], ACT.Identity, bias=dtb[0:32, :]).then_inc(s_ev, E.adds(s_ev))
            act_hi(E)
            nc.scalar.activation(alog[0:32, :], alog[0:32, :], ACT.Exp).then_inc(s_a, E.adds(s_a))
            E.eng.wait_ge(s_u, E.next(s_u))
            nc.scalar.activation(dn[0:32, :], dn[0:32, :], ACT.Exp).then_inc(s_a, E.adds(s_a))
            E.eng.wait_ge(E.last, E.sofar(E.last))
            nc.scalar.activation(dn[0:32, :], dn[0:32, :], ACT.Ln, bias=1.0).then_inc(s_uh, E.adds(s_uh))
            E.eng.wait_ge(s_u, E.next(s_u))
            nc.scalar.activation(wsT[0:32, 0:P], acT[0:32, 0:P], ACT.Exp, scale=-1.0, bias=acT[0:32, P - 1:P])
            nc.scalar.activation(eaT[0:32, 0:P], acT[0:32, P:S], ACT.Exp).then_inc(s_uh, E.adds(s_uh))
            E.skip(s_mix)
            E.eng.wait_ge(s_tp, E.next(s_tp))
            nc.scalar.activation(brow2[:, :, :], ps[:, 6, :].rearrange("p (g n) -> p g n", g=4), ACT.Copy)
            nc.scalar.activation(rws[:, :, :], ps[:, 5, 0:192].rearrange("p (a h) -> p a h", a=6), ACT.Copy).then_inc(s_uh, E.adds(s_uh))
            for g in range(4):
                E.skip(s_o, 2)
                for q in range(NT):
                    E.eng.wait_ge(s_mx, E.next(s_mx))
                    nc.scalar.activation(ee[:, q], ee[:, q], ACT.Exp).then_inc(s_e, E.adds(s_e))
                E.eng.wait_ge(s_mixp, E.next(s_mixp))
                nc.scalar.activation(stt[:, :], ps[:, 1, :], ACT.Copy).then_inc(s_pc, E.adds(s_pc))
                E.skip(s_mix, 2)
            with E.loop(2, {s_mm: 4, s_u: 4, s_uh: 4, s_raw[0]: 32, s_raw[1]: 32, s_hi: 2}):
                for b in range(2):
                    if E.seen(s_u):
                        E.eng.wait_ge(s_u, E.sofar(s_u))
                    for q in range(NT):
                        E.eng.wait_ge(s_mm, E.next(s_mm))
                        nc.scalar.activation(zt[:, 2 * b + q, :], ps[:, 2 * b + q, :], ACT.Tanh, scale=0.5).then_inc(s_uh, E.adds(s_uh))
                    E.skip(s_u, 2)
                    act_hi(E)
            E.eng.wait_ge(s_mix, E.next(s_mix))
            for q in range(NT):
                last = nc.scalar.activation(zsq[:, q], xs[:, q].rearrange("p g n -> p (g n)"), ACT.Square, accum_out=s16[:, q:q + 1])
            last.then_inc(s_mixa, E.adds(s_mixa))
            E.eng.wait_ge(s_mix, E.next(s_mix))
            nc.scalar.activation(s16[:, 0:2], s16[:, 0:2], ACT.Sqrt).then_inc(s_mixa, E.adds(s_mixa))
            E.skip(s_mix)
            for h in range(2):
                act_turn(E, lambda c: gg("ssd_norm_2", layer2[0], 16)(8 * h + c), bh)
                if h == 0:
                    act_out(E)
                else:
                    for b in range(2):
                        E.eng.wait_ge(s_mm, E.next(s_mm, 2))
                        act_hi(E)
            for b in range(2):
                for n in range(2):
                    E.eng.wait_ge(s_mm, E.next(s_mm))
                    nc.scalar.activation(ge8[:, 4 * b + 2 * n:4 * b + 2 * n + 2, :], bank(2 * b + n), ACT.Tanh, scale=0.5).then_inc(s_ev, E.adds(s_ev))
                act_hi(E)
        layer2 = [0]

        def dve_ssd(E):
            E.eng.wait_ge(s_small, E.next(s_small, n_small))
            nc.vector.memset(cin[:, :, :, 0:3], 0.0).then_inc(s_d, E.adds(s_d))
            E.eng.wait_ge(E.last, E.sofar(E.last))
            E.eng.wait_ge(s_mixa, E.next(s_mixa))
            for i in range(13):
                if i < 12:
                    E.eng.wait_ge(s_cin, E.next(s_cin))
                    if i % 2:
                        dve_lo(E, 2)
                    for tap in range(3):
                        if tap:
                            E.eng.wait_ge(s_d, E.sofar(s_d))
                        for c in range(2):
                            k = 24 * tap + 2 * i + c
                            last = nc.vector.scalar_tensor_tensor(out=cout[:, i % 4, c, :], in0=cin[:, i % 2, c, tap:tap + S], scalar=cw[:, k:k + 1],
                                                                  in1=cout[:, i % 4, c, :], op0=ALU.mult, op1=ALU.add)
                            if tap == 2 and c:
                                last.then_inc(s_u, E.adds(s_u))
                            else:
                                last.then_inc(s_d, E.adds(s_d))
                if i >= 1:
                    j = i - 1
                    E.eng.wait_ge(s_uh, E.next(s_uh))
                    dst = cout[:, j % 4] if j < 8 else bct[:, (j - 8) // 2, 2 * (j % 2):2 * (j % 2) + 2, :]
                    last = nc.vector.scalar_tensor_tensor(out=dst, in0=cex[:, j % 2], scalar=1.0, in1=cout[:, j % 4], op0=ALU.add, op1=ALU.mult)
                    if j < 8:
                        last.then_inc(s_mix, E.adds(s_mix))
                    else:
                        last.then_inc(s_d, E.adds(s_d))
            E.eng.wait_ge(s_d, E.sofar(s_d))
            dve_lo(E, 1)
            r = slice(0, 32)
            nc.vector.tensor_scalar(dm[r, :], dx[r, :], 0.0, None, ALU.max).then_inc(s_d, E.adds(s_d))
            nc.vector.scalar_tensor_tensor(out=dn[r, :], in0=dx[r, :], scalar=-1.0, in1=dx[r, :], op0=ALU.mult, op1=ALU.min).then_inc(s_u, E.adds(s_u))
            E.eng.wait_ge(s_uh, E.next(s_uh))
            nc.vector.tensor_tensor(dn[r, :], dn[r, :], dm[r, :], ALU.add).then_inc(s_d, E.adds(s_d))
            E.eng.wait_ge(E.last, E.sofar(E.last))
            nc.vector.tensor_scalar(dx[r, :], dn[r, :], alog[r, :], -1.0, ALU.mult, ALU.mult).then_inc(s_d, E.adds(s_d))
            E.eng.wait_ge(E.last, E.sofar(E.last))
            for q in range(NT):
                last = nc.vector.tensor_tensor_scan(acT[r, q * P:(q + 1) * P], ones[r, 0:1].to_broadcast([32, P]), dx[r, q * P:(q + 1) * P], 0.0, ALU.mult, ALU.add)
            last.then_inc(s_u, E.adds(s_u))
            E.eng.wait_ge(s_uh, E.next(s_uh))
            nc.vector.memset(s16[:, 15:16], 0.0).then_inc(s_mix, E.adds(s_mix))
            E.eng.wait_ge(s_uh, E.next(s_uh))

            def decays(g):
                for q in range(NT):
                    nc.vector.tensor_tensor(am[r, q], acT[r, q * P:(q + 1) * P].unsqueeze(1).to_broadcast([32, 8, P]),
                                            ident[r, 8 * g:8 * g + 8].unsqueeze(2).to_broadcast([32, 8, P]), ALU.mult).then_inc(s_mix, E.adds(s_mix))
            decays(0)
            for g in range(4):
                x8 = lambda q: xs[:, q, g, :].rearrange("p (h n) -> p h n", n=64)
                col = lambda n: rws[:, n, :].rearrange("p (g h) -> p g h", h=8)[:, g, :]
                for q in range(NT):
                    nc.vector.tensor_tensor(xdt[:, q], x8(q), col(q).unsqueeze(2).to_broadcast([P, 8, 64]), ALU.mult).then_inc(s_d, E.adds(s_d))
                E.eng.wait_ge(E.last, E.sofar(E.last))
                nc.vector.tensor_tensor(xdw[:, :, :], xdt[:, 0], col(4).unsqueeze(2).to_broadcast([P, 8, 64]), ALU.mult).then_inc(s_d, E.adds(s_d))
                E.eng.wait_ge(s_sc, E.next(s_sc))
                for q in range(NT):
                    nc.vector.tensor_tensor(cbm[:, q, :], ps[:, 0, q * P:(q + 1) * P], upper[:, :], ALU.mult).then_inc(s_d, E.adds(s_d))
                for q in range(NT):
                    E.eng.wait_ge(s_dec, E.next(s_dec))
                    for h in range(8):
                        last = nc.vector.tensor_scalar(ee[:, q, h, :], ps[:, 2 + 2 * q + h // 4, (h % 4) * P:(h % 4) * P + P],
                                                       rws[:, 2 + q, :].rearrange("p (g h) -> p g h", h=8)[:, g, h:h + 1], 0.0, ALU.subtract, ALU.min)
                    last.then_inc(s_mx, E.adds(s_mx))
                if g < 3:
                    decays(g + 1)
                for q in range(NT):
                    E.eng.wait_ge(s_e, E.next(s_e))
                    E.eng.wait_ge(s_d, E.sofar(s_d))
                    nc.vector.tensor_tensor(ee[:, q], ee[:, q], cbm[:, q, :].unsqueeze(1).to_broadcast([P, 8, P]), ALU.mult).then_inc(s_scd, E.adds(s_scd))
                dskb = dsk.rearrange("p (g h) -> p g h", h=8)[:, g, :].unsqueeze(2).to_broadcast([P, 8, 64])
                for q in range(NT):
                    nc.vector.tensor_tensor(x8(q), x8(q), dskb, ALU.mult).then_inc(s_d, E.adds(s_d))
                E.eng.wait_ge(s_o, E.next(s_o))
                E.eng.wait_ge(s_d, E.sofar(s_d))
                p8 = lambda b: ps[:, b, :].rearrange("p (h n) -> p h n", n=64)
                nc.vector.tensor_tensor(x8(0), x8(0), p8(6), ALU.add)
                E.eng.wait_ge(s_o, E.next(s_o))
                nc.vector.tensor_tensor(xdt[:, 0], p8(1), col(5).unsqueeze(2).to_broadcast([P, 8, 64]), ALU.mult).then_inc(s_d, E.adds(s_d))
                nc.vector.tensor_tensor(x8(1), x8(1), p8(7), ALU.add).then_inc(s_d, E.adds(s_d))
                E.eng.wait_ge(s_d, E.sofar(s_d))
                nc.vector.tensor_tensor(x8(1), x8(1), xdt[:, 0], ALU.add).then_inc(s_d, E.adds(s_d))
                E.eng.wait_ge(E.last, E.sofar(E.last))
            nc.vector.memset(s16[:, 13:14], 0.0).then_inc(s_evd, E.adds(s_evd))
            with E.loop(2, {s_uh: 4, s_evd: 4, s_u: 4, s_hi: 2, s_lo: 2, s_mm: 4}) as i:
                for b in range(2):
                    for q in range(NT):
                        z = zt[:, 2 * b + q, :]
                        E.eng.wait_ge(s_uh, E.next(s_uh))
                        nc.vector.scalar_tensor_tensor(out=z, in0=z, scalar=1.0, in1=ps[:, 2 * b + q, :], op0=ALU.add, op1=ALU.mult).then_inc(s_evd, E.adds(s_evd))
                        E.eng.wait_ge(s_evd, E.sofar(s_evd))
                        y = xs[:, q, 2 * i + b, :]
                        nc.vector.scalar_tensor_tensor(out=y, in0=z, scalar=0.5, in1=y, op0=ALU.mult, op1=ALU.mult).then_inc(s_u, E.adds(s_u))
                    dve_lo(E, 2)
            nc.vector.memset(s16[:, 14:15], 0.0).then_inc(s_mix, E.adds(s_mix))
            E.eng.wait_ge(s_mixa, E.next(s_mixa))
            nc.vector.tensor_scalar(s16[:, 0:2], s16[:, 0:2], 1.0 / 2048, EPS, ALU.mult, ALU.add).then_inc(s_mix, E.adds(s_mix))
            E.eng.wait_ge(s_mixa, E.next(s_mixa))
            nc.vector.reciprocal(s16[:, 0:2], s16[:, 0:2]).then_inc(s_d, E.adds(s_d))
            E.eng.wait_ge(E.last, E.sofar(E.last))
            for q in range(NT):
                last = nc.vector.tensor_scalar(xs[:, q], xs[:, q], s16[:, q:q + 1], None, ALU.mult)
            last.then_inc(s_mix, E.adds(s_mix))
            for h in range(2):
                dve_turn(E, lambda c: gg("ssd_norm_2", layer2[0], 16)(8 * h + c), bh, bl)
                if h == 0:
                    dve_out_splits(E)
                else:
                    for b in range(2):
                        for n in range(2):
                            E.eng.wait_ge(s_mm, E.next(s_mm))
                            c = 4 * b + 2 * n
                            nc.vector.tensor_tensor(yT[:, c:c + 2, :], yT[:, c:c + 2, :], bank(2 * b + n), ALU.add).then_inc(s_evd, E.adds(s_evd))
                        dve_lo(E)
            dve_lo(E, 2)
            dve_lo(E, 2)
            dve_gate(E, mg, None)

        def dve_gate(E, dst, plus):
            nc.vector.tensor_scalar(ge8[:, :, :], ge8[:, :, :], 0.5, 0.5, ALU.mult, ALU.add).then_inc(s_d, E.adds(s_d))
            E.eng.wait_ge(E.last, E.sofar(E.last))
            if plus is None:
                nc.vector.tensor_tensor(dst[:, :, :], ge8[:, :, :], yT[:, :, :], ALU.mult).then_inc(s_d, E.adds(s_d))
            else:
                nc.vector.tensor_tensor(ge8[:, :, :], ge8[:, :, :], yT[:, :, :], ALU.mult).then_inc(s_d, E.adds(s_d))
                E.eng.wait_ge(E.last, E.sofar(E.last))
                nc.vector.tensor_tensor(dst[:, :, :], dst[:, :, :], ge8[:, :, :], ALU.add).then_inc(s_x, E.adds(s_x))
            E.eng.wait_ge(E.last, E.sofar(E.last))

        vm = view(ar, 0, [P, NT, 4, 2, P])
        qkn = view(ar, 2048, [P, 8, 2, S])
        qkr = view(ar, 6144, [P, 4, 2, S])
        rows = view(ar, 10240, [P, NT, 8, 192])
        cqT = view(ar, 4096, [P, 4, S])
        ckT = view(ar, 5120, [P, 2, S])
        krr = view(ar, 13312, [P, NT, 64])
        rb = view(ar, 13312, [P, NT, 8, 64])
        sgn = view(ar, 12544, [P, 2, 2, S])
        sgr = view(ar, 13568, [P, 2, S])
        yq = yf[:, 0:1536].rearrange("p (h n) -> p h n", n=192)
        rt1 = yf[:, 0:512].rearrange("p (q h n) -> p q h n", q=NT, h=8)
        rt2 = yf[:, 512:1024].rearrange("p (q h n) -> p q h n", q=NT, h=8)
        invf = yf[:, 1536:1568]
        ang = yf[:, 1568:1632].rearrange("p (q n) -> p q n", q=NT)
        kr2 = yf[:, 1632:1696].rearrange("p (q n) -> p q n", q=NT)
        trig = yf[:, 1696:1824].rearrange("p (a q n) -> p a q n", a=2, q=NT)
        posf = yf[:, 1824:1826]
        cqh, cql = view(ar_r, 0, [P, 4, S]), view(ar_r, 1024, [P, 4, S])
        ckh, ckl = view(ar_r, 2048, [P, 2, S]), view(ar_r, 2560, [P, 2, S])

        def pe_to_T(E):
            E.eng.wait_ge(s_mix, E.next(s_mix))
            for b in range(4):
                for h in (2 * b, 2 * b + 1):
                    for q in range(NT):
                        last = nc.tensor.transpose(ps[:, b, (h % 2) * S + q * P:(h % 2) * S + (q + 1) * P], rows[:, q, h, 0:P], ident[:, :])
                last.then_inc(s_tp, E.adds(s_tp))
            for b in range(2):
                for j in (2 * b, 2 * b + 1):
                    for q in range(NT):
                        last = nc.tensor.transpose(ps[:, 4 + b, (j % 2) * S + q * P:(j % 2) * S + (q + 1) * P],
                                                   rb[:, q, 2 * j:2 * j + 2, :].rearrange("p h n -> p (h n)"), ident[:, :])
                last.then_inc(s_tp, E.adds(s_tp))
            E.skip(s_ev, 6)

        def act_to_T(E, a):
            for b in range(4):
                E.eng.wait_ge(s_tp, E.next(s_tp))
                nc.scalar.activation(qkn[:, 2 * b:2 * b + 2, a, :], bank(b), ACT.Copy).then_inc(s_ev, E.adds(s_ev))
            for b in range(2):
                E.eng.wait_ge(s_tp, E.next(s_tp))
                nc.scalar.activation(qkr[:, 2 * b:2 * b + 2, a, :], bank(4 + b), ACT.Copy).then_inc(s_ev, E.adds(s_ev))

        def pe_scores_mla(E, _):
            E.eng.wait_ge(s_stg, E.next(s_stg))
            if E.seen(s_scd):
                E.eng.wait_ge(s_scd, E.sofar(s_scd))
            for c in range(2):
                lo = slice(64 * c, 64 * c + 64)
                for q, (a, b) in enumerate(COLS):
                    o, keys, qs = ps[:, c, a:b], slice(0, b - a), slice(q * P, (q + 1) * P)
                    nc.tensor.matmul(o, sgn[:, c, 0, qs], sgn[:, c, 1, keys], start=True, stop=False)
                    last = nc.tensor.matmul(o, sgr[lo, 0, qs], sgr[lo, 1, keys], start=False, stop=True)
                last.then_inc(s_sc, E.adds(s_sc))
            E.skip(s_scd, 2)

        def dve_stage_mla(E, j, _):
            nc.vector.tensor_copy(sgn.rearrange("p c a t -> p (c a t)"), qkn.rearrange("p (j c) a t -> p j (c a t)", c=2)[:, j, :])
            nc.vector.tensor_copy(sgr[:, :, :], qkr[:, j, :, :]).then_inc(s_stg, E.adds(s_stg))

        def pe_mla(E):
            if E.seen(s_ev):
                E.eng.wait_ge(s_ev, E.sofar(s_ev))
            pe_T(E, 512, 8, ah, al, 0)
            E.skip(s_ev, 2)
            slot = E.slot()
            E.eng.wait_ge(s_lo, E.next(s_lo))
            a, b = wv(wh, slot, 320, 8), wv(wl, slot, 320, 8)
            for m in range(2):
                for k in range(8):
                    c = slice(m * P, (m + 1) * P)
                    last = mm3(ps[:, 2, m * S:m * S + S], a[:, k, c], b[:, k, c], ah[:, k], al[:, k], k == 0, k == 7)
            last.then_inc(s_mm, E.adds(s_mm))
            for q in range(NT):
                t = slice(q * P, (q + 1) * P)
                for k in range(8):
                    last = mm3(ps[:, 3, 64 * q:64 * q + 64], ah[:, k, t], al[:, k, t], a[:, k, S:320], b[:, k, S:320], k == 0, k == 7)
            last.then_inc(s_mm, E.adds(s_mm))
            E.skip(s_ev, 2)
            pe_stats(E, 4)
            E.eng.wait_ge(s_op, E.next(s_op, 4))
            pe_stats(E, 2)
            E.eng.wait_ge(s_op, E.next(s_op, 2))
            for b in range(2):
                pe_free(E)
                slot = E.slot()
                E.eng.wait_ge(s_lo, E.next(s_lo))
                wa, wb = wv(wh, slot, 1024, 2), wv(wl, slot, 1024, 2)
                for q in range(NT):
                    t = slice(q * P, (q + 1) * P)
                    for n in range(2):
                        for k in range(2):
                            last = mm3(ps[:, 4 * b + 2 * q + n, :], ckh[:, k, t], ckl[:, k, t], wa[:, k, 512 * n:512 * n + 512], wb[:, k, 512 * n:512 * n + 512], k == 0, k == 1)
                        last.then_inc(s_mm, E.adds(s_mm))
                E.skip(s_ev, 4)
            pe_free(E)
            E.skip(s_mix, 2)
            pe_to_T(E)
            pe_free(E)
            for b in range(3):
                pe_rows(E, 512, 4, cqh, cql, 2 * b)
                E.skip(s_ev, 2)
            pe_free(E)
            E.skip(s_mix)
            pe_to_T(E)
            pe_free(E)
            pe_attention(E, 4, wide=P, scores=pe_scores_mla, v=lambda t, j, c: vm[:, t, j, c, :])
            pe_turn(E, ready=s_od)
            E.eng.wait_ge(s_op, E.next(s_op, 4))
            pe_T(E, 512, 8, bh, bl, 0)
            pe_T(E, 512, 8, bh, bl, 2)
            E.skip(s_ev, 4)
            if E.seen(s_ev, 2):
                E.eng.wait_ge(s_ev, E.sofar(s_ev, 2))
            pe_T(E, 512, 8, ah, al, 0)
            if E.seen(s_ev):
                E.eng.wait_ge(s_ev, E.sofar(s_ev))
            pe_T(E, 512, 8, ah, al, 2)
            E.skip(s_ev, 4)
            E.eng.wait_ge(s_op, E.next(s_op, 8))
            if E.seen(s_ev):
                E.eng.wait_ge(s_ev, E.sofar(s_ev))
            pe_T(E, 512, 8, ah, al, 0)
            pe_T(E, 512, 8, ah, al, 2)
            E.skip(s_ev, 4)

        def act_mla(E):
            act_copy(E, [cqT[:, 0:2, :], cqT[:, 2:4, :]], 0)
            E.eng.wait_ge(s_mm, E.next(s_mm))
            nc.scalar.activation(ckT[:, :, :], bank(2), ACT.Copy).then_inc(s_ev, E.adds(s_ev))
            E.eng.wait_ge(s_mm, E.next(s_mm))
            nc.scalar.activation(krr[:, :, :], ps[:, 3, 0:P].rearrange("p (q n) -> p q n", q=NT), ACT.Copy).then_inc(s_ev, E.adds(s_ev))
            act_hi(E)
            E.eng.wait_ge(s_ev, E.sofar(s_ev))
            act_stats(E, cqT, 4, False)
            act_operand(E, cqT, 4, cqh)
            act_stats(E, ckT, 2, False)
            act_operand(E, ckT, 2, ckh)
            for b in range(2):
                for q in range(NT):
                    for n in range(2):
                        E.eng.wait_ge(s_mm, E.next(s_mm))
                        src = ps[:, 4 * b + 2 * q + n, :].rearrange("p (h a n) -> p h a n", h=2, a=2)
                        j = 2 * b + n
                        nc.scalar.activation(rows[:, q, 2 * j:2 * j + 2, 0:P], src[:, :, 0, :], ACT.Copy)
                        nc.scalar.activation(vm[:, q, j], src[:, :, 1, :], ACT.Copy).then_inc(s_ev, E.adds(s_ev))
                act_hi(E)
            E.eng.wait_ge(s_mix, E.next(s_mix))
            nc.scalar.activation(trig[:, :, :, :], trig[:, :, :, :], ACT.Sin).then_inc(s_mixa, E.adds(s_mixa))
            for a in (1, 0):
                E.eng.wait_ge(s_mix, E.next(s_mix))
                nc.scalar.activation(s16[:, :], s16[:, :], ACT.Sqrt).then_inc(s_mixa, E.adds(s_mixa))
                E.skip(s_mix)
                act_to_T(E, a)
                if a == 1:
                    for b in range(3):
                        for q in range(NT):
                            E.eng.wait_ge(s_mm, E.next(s_mm))
                            nc.scalar.activation(rows.rearrange("p q h n -> p q (h n)")[:, q, 512 * b:512 * b + 512], ps[:, 2 * b + q, :], ACT.Copy).then_inc(s_ev, E.adds(s_ev))
                        act_hi(E)
            E.eng.wait_ge(s_ev, E.sofar(s_ev))
            nc.scalar.activation(sm[:, 600:601], sm[:, 0:1], ACT.Copy).then_inc(s_wo, E.adds(s_wo))
            act_attention(E, 4)
            act_turn(E, 1.0, bh)
            act_out(E)
            for b in range(2):
                for n in range(2):
                    E.eng.wait_ge(s_mm, E.next(s_mm))
                    nc.scalar.activation(ge8[:, 4 * b + 2 * n:4 * b + 2 * n + 2, :], bank(2 * b + n), ACT.Tanh, scale=0.5).then_inc(s_ev, E.adds(s_ev))
                act_hi(E)
            act_operand(E, mg, DC, ah, False)
            act_out(E, False)

        TWO_PI = 2 * math.pi

        def dve_angles(E):
            nc.vector.tensor_copy(posf, posi[:, :]).then_inc(s_d, E.adds(s_d))
            E.eng.wait_ge(E.last, E.sofar(E.last))
            for q in range(NT):
                last = nc.vector.tensor_scalar(ang[:, q, :], invf, posf[:, q:q + 1], None, ALU.mult)
            last.then_inc(s_d, E.adds(s_d))
            E.eng.wait_ge(E.last, E.sofar(E.last))
            magic = 12582912.0
            nc.vector.tensor_scalar(kr2, ang, 1.0 / TWO_PI, magic, ALU.mult, ALU.add).then_inc(s_d, E.adds(s_d))
            E.eng.wait_ge(E.last, E.sofar(E.last))
            nc.vector.tensor_scalar(kr2, kr2, magic, None, ALU.subtract).then_inc(s_d, E.adds(s_d))
            E.eng.wait_ge(E.last, E.sofar(E.last))
            for part in (6.28125, TWO_PI - 6.28125):
                nc.vector.scalar_tensor_tensor(out=ang, in0=kr2, scalar=-part, in1=ang, op0=ALU.mult, op1=ALU.add).then_inc(s_d, E.adds(s_d))
                E.eng.wait_ge(E.last, E.sofar(E.last))
            pi = 3.1415925
            nc.vector.tensor_scalar(trig[:, 0], ang, -pi, pi, ALU.max, ALU.min).then_inc(s_d, E.adds(s_d))
            nc.vector.tensor_scalar(ang, ang, math.pi / 2, None, ALU.add).then_inc(s_d, E.adds(s_d))
            E.eng.wait_ge(E.last, E.sofar(E.last))
            nc.vector.tensor_scalar(kr2, ang, math.pi, -TWO_PI, ALU.is_gt, ALU.mult).then_inc(s_d, E.adds(s_d))
            E.eng.wait_ge(E.last, E.sofar(E.last))
            nc.vector.tensor_tensor(ang, ang, kr2, ALU.add).then_inc(s_d, E.adds(s_d))
            E.eng.wait_ge(E.last, E.sofar(E.last))
            nc.vector.tensor_scalar(trig[:, 1], ang, -pi, pi, ALU.max, ALU.min).then_inc(s_mix, E.adds(s_mix))
            E.eng.wait_ge(s_mixa, E.next(s_mixa))

        def dve_heads(E, gain):
            for q in range(NT):
                nc.vector.tensor_tensor(yq, rows[:, q], rows[:, q], ALU.mult).then_inc(s_d, E.adds(s_d))
                E.eng.wait_ge(E.last, E.sofar(E.last))
                nc.vector.tensor_reduce(s16[:, 8 * q:8 * q + 8], yq, AX.X, ALU.add).then_inc(s_d, E.adds(s_d))
                E.eng.wait_ge(E.last, E.sofar(E.last))
            nc.vector.tensor_scalar(s16[:, :], s16[:, :], 1.0 / 192, EPS, ALU.mult, ALU.add).then_inc(s_mix, E.adds(s_mix))
            E.eng.wait_ge(s_mixa, E.next(s_mixa))
            nc.vector.reciprocal(s16[:, :], s16[:, :]).then_inc(s_d, E.adds(s_d))
            E.eng.wait_ge(E.last, E.sofar(E.last))
            for q in range(NT):
                nc.vector.tensor_tensor(rows[:, q], rows[:, q], s16[:, 8 * q:8 * q + 8].unsqueeze(2).to_broadcast([P, 8, 192]), ALU.mult).then_inc(s_d, E.adds(s_d))
            E.eng.wait_ge(E.last, E.sofar(E.last))
            for q in range(NT):
                nc.vector.tensor_tensor(rows[:, q], rows[:, q], gain[:, :].unsqueeze(1).to_broadcast([P, 8, 192]), ALU.mult).then_inc(s_d, E.adds(s_d))
            E.eng.wait_ge(E.last, E.sofar(E.last))
            b32 = lambda a: trig[:, a].unsqueeze(2).to_broadcast([P, NT, 8, 32])
            t1, t2 = rows[:, :, :, P:P + 32], rows[:, :, :, P + 32:192]
            for (x, y, op, at) in ((t1, t2, ALU.subtract, 0), (t2, t1, ALU.add, 32)):
                for q in range(NT):
                    bq = lambda a: trig[:, a, q, :].unsqueeze(1).to_broadcast([P, 8, 32])
                    nc.vector.tensor_tensor(rt1[:, q], x[:, q], bq(1), ALU.mult)
                    nc.vector.tensor_tensor(rt2[:, q], y[:, q], bq(0), ALU.mult).then_inc(s_d, E.adds(s_d))
                E.eng.wait_ge(E.last, E.sofar(E.last))
                last = nc.vector.tensor_tensor(rb[:, :, :, at:at + 32].rearrange("p q h n -> p (q h) n"), rt1.rearrange("p q h n -> p (q h) n"), rt2.rearrange("p q h n -> p (q h) n"), op)
                last.then_inc(s_mix if at else s_d, E.adds(s_mix if at else s_d))
                E.eng.wait_ge(E.last, E.sofar(E.last))

        def dve_mla(E):
            dve_lo(E, 2)
            dve_lo(E, 2)
            dve_stats(E, 4)
            dve_operand(E, cqT, gg("q_lora_norm_2", layer2[0], 4), 4, cqh, cql)
            dve_stats(E, 2)
            dve_operand(E, ckT, gg("kv_lora_norm_2", layer2[0], 2), 2, ckh, ckl)
            nc.vector.tensor_copy(invf, cinv[:, :]).then_inc(s_d, E.adds(s_d))
            dve_lo(E, 4)
            dve_lo(E, 4)
            dve_angles(E)
            for q in range(NT):
                last = nc.vector.tensor_copy(rows[:, q, :, P:192], krr[:, q, :].unsqueeze(1).to_broadcast([P, 8, 64]))
            last.then_inc(s_d, E.adds(s_d))
            E.eng.wait_ge(E.last, E.sofar(E.last))
            dve_heads(E, kng)
            for b in range(3):
                dve_lo(E, 2)
            dve_heads(E, qng)
            E.eng.wait_ge(s_wo, E.next(s_wo))
            dve_attention(E, 4, "mla", 192.0 ** -0.5, table=False, wide=P, stage=dve_stage_mla)
            dve_turn(E, 1.0, bh, bl)
            dve_out_splits(E)
            dve_lo(E, 2)
            dve_lo(E, 2)
            dve_gate(E, mg, True)
            dve_operand(E, mg, None, DC, ah, al, normed=False)
            dve_out_splits(E, 1)
            E.eng.wait_ge(s_wo, E.next(s_wo))
            nc.vector.tensor_tensor(xT[:, :, :], xT[:, :, :], yT[:, :, :], ALU.add).then_inc(s_x, E.adds(s_x))
            E.eng.wait_ge(s_x, E.sofar(s_x))

        def pe_second(E, layer):
            pe_ffn(E)
            pe_stats(E, DC)
            pe_ssd(E)
            pe_mla(E)
            pe_ffn(E)
            E.skip(s_x, 4)

        def act_second(E, layer):
            layer2[0] = layer
            act_ffn(E, layer > 0)
            act_stats(E, xT, DC, hi=True)
            act_operand(E, xT, DC, ah)
            act_ssd(E)
            act_mla(E)
            nc.scalar.activation(sm[:, 600:601], sm[:, 124:125], ACT.Copy).then_inc(s_wo, E.adds(s_wo))
            act_ffn(E, True)

        def dve_second(E, layer):
            layer2[0] = layer
            dve_ffn(E, "ln_ffn1_2", layer, 0 if layer else None)
            dve_stats(E, DC, lo=0)
            dve_operand(E, xT, gg("ln_mix_2", layer, 8), DC, ah, al)
            dve_ssd(E)
            dve_mla(E)
            dve_ffn(E, "ln_ffn2_2", layer, 2)

        fin = view(ar, 0, [P, NT, D])

        def pe_end(E):
            E.eng.wait_ge(s_x, E.next(s_x))
            pe_free(E)
            for q in range(NT):
                for b in range(2):
                    for c in range(4):
                        last = nc.tensor.transpose(ps[:, 2 * q + b, c * P:(c + 1) * P], xT[:, 4 * b + c, q * P:(q + 1) * P], ident[:, :])
                    last.then_inc(s_tp, E.adds(s_tp))

        def act_end(E):
            for q in range(NT):
                for b in range(2):
                    E.eng.wait_ge(s_tp, E.next(s_tp))
                    nc.scalar.activation(fin[:, q, 512 * b:512 * b + 512], ps[:, 2 * q + b, :], ACT.Copy).then_inc(s_mixa, E.adds(s_mixa))
                E.eng.wait_ge(s_mixa, E.sofar(s_mixa))
                E.eng.dma_start(out[0].rearrange("(q p) n -> q p n", p=P)[q], fin[:, q, :]).then_inc(s_out, 16)
            E.eng.wait_ge(s_out, 16 * NT)

        block = ctx.enter_context(nc.Block())
        nl = DEPTH if stop is None else min(stop, DEPTH)
        nl2 = DEPTH2 if stop is None else max(0, stop - DEPTH)

        @block.sync
        def _(eng):
            E = Track(eng)
            sp_start(E)
            for layer in range(nl):
                if layer % 3 == 0:
                    sp_da(E, layer // 3)
                elif layer == 1:
                    sp_nsa(E)
                else:
                    sp_fox(E)
                sp_rest(E, layer)
            for layer in range(nl2):
                sp_second(E, layer)

        @block.gpsimd
        def _(eng):
            E = Track(eng)
            pool_start(E)
            if nl > 3:
                pool_bias_again(E)

        @block.scalar
        def _(eng):
            E = Track(eng)
            act_start(E)
            for layer in range(nl):
                act_stats(E, xT, DC, layer > 0)
                act_operand(E, xT, DC, ah)
                if layer % 3 == 0:
                    act_qkv(E)
                    if layer == 0:
                        act_flip(E)
                    act_attention(E, 8)
                    act_subln(E)
                    act_turn(E, lambda c: subl[:, layer // 3:layer // 3 + 1])
                elif layer == 1:
                    act_nsa(E)
                else:
                    act_fox(E)
                act_out(E, False)
                act_rest(E)
            for layer in range(nl2):
                act_second(E, layer)
            act_end(E)

        @block.tensor
        def _(eng):
            E = Track(eng)
            pe_start(E)
            for layer in range(nl):
                pe_stats(E, DC)
                if layer % 3 == 0:
                    pe_qkv(E)
                    if layer == 0:
                        pe_flip(E)
                    pe_attention(E, 8, shared=True)
                    E.skip(s_mix)
                    E.skip(s_mixa)
                    pe_turn(E)
                elif layer == 1:
                    pe_nsa(E)
                else:
                    pe_fox(E)
                pe_out(E, 4)
                pe_rest(E)
                E.skip(s_x, 3)
            for layer in range(nl2):
                pe_second(E, layer)
            E.n[s_x] -= 1
            pe_end(E)

        @block.vector
        def _(eng):
            E = Track(eng)
            dve_start(E)
            for layer in range(nl):
                dve_stats(E, DC)
                dve_operand(E, xT, g1(layer, 0), DC, ah, al)
                if layer % 3 == 0:
                    lamL[0] = layer // 3
                    dve_qkv(E)
                    if layer == 0:
                        E.skip(s_rows, 16)
                        E.eng.wait_ge(s_mixa, E.next(s_mixa))
                    else:
                        E.eng.wait_ge(s_rows, E.next(s_rows, 16))
                    dve_attention(E, 8, "da", 0.125)
                    dve_subln(E)
                    dve_turn(E, lambda c: subl[:, layer // 3:layer // 3 + 1])
                elif layer == 1:
                    dve_nsa(E)
                else:
                    dve_fox(E)
                dve_out_splits(E, 1)
                dve_rest(E, layer)
            for layer in range(nl2):
                dve_second(E, layer)


_INS = ["x", "p", "rel_bias", "norm_g", "mlp_w1", "mlp_w2", "ple_w", "ple_gate_w", "da_w_in", "da_lambda", "da_subln",
        "da_w_out", "nsa_w_in", "nsa_cmp_pe", "nsa_cmp_w1", "nsa_cmp_w2", "nsa_w_out", "fox_w_in", "fox_b_f",
        "fox_w_out", "positions_2", "ln_ffn1_2", "ffn1_w13_2", "ffn1_w2_2", "ln_mix_2", "w_in_2", "conv_w_2",
        "conv_b_2", "dt_bias_2", "a_log_2", "d_skip_2", "ssd_norm_2", "w_ssd_out_2", "q_lora_norm_2", "w_uq_2",
        "kv_lora_norm_2", "w_ukv_2", "q_norm_2", "k_norm_2", "w_mla_out_2", "w_o_2", "ln_ffn2_2", "ffn2_w13_2",
        "ffn2_w2_2"]


def kernel(**inputs):
    import concourse.bacc as _bacc
    from concourse.bass_utils import run_bass_kernel_spmd as _run

    nc = _bacc.Bacc("TRN2", target_bir_lowering=False, num_devices=1)
    arrays, d = {}, {}
    given = {name: np.ascontiguousarray(inputs[name]) for name in _INS}
    for name, a in {**given, **shape_constants()}.items():
        arrays[f"in_{name}"] = a
        d[name] = nc.dram_tensor(f"in_{name}", a.shape, mybir.dt.from_np(a.dtype), kind="ExternalInput").ap()
    out = nc.dram_tensor("out_0", (1, S, D), F32, kind="ExternalOutput").ap()
    build(nc, d, out)
    r = _run(nc, [arrays], core_ids=[0])
    return r.results[0]["out_0"]
```
